# Optimizing a Trainium2 kernel written in Bass

```python
import jax, jax.numpy as jnp
from jax import lax
import numpy as np

D_MODEL = 1024
BATCH = 1
SEQ = 512
DEPTH = 2

GRID_W = 64
CTX_LEN = 256
EPS = 1e-6

HEAD_DIM = 64
ATT_HEADS = 8
ATT_KV_HEADS = 2
ATT_GROUP = ATT_HEADS // ATT_KV_HEADS
WINDOW = 128
ATT_BLOCK = 128
ROPE_BASE = 10000.0
ATT_DIM = ATT_HEADS * HEAD_DIM
KV_DIM = ATT_KV_HEADS * HEAD_DIM

POOL_WINDOWS = (2, 4, 8, 16)
POOL_GROUPS = len(POOL_WINDOWS)
POOL_GROUP_DIM = 64
POOL_DIM = POOL_GROUPS * POOL_GROUP_DIM

GLA_HEADS = 4
GLA_DK = 32
GLA_DV = 64
GLA_GATE_RANK = 16
GLA_TAU = 16.0
GLA_CHUNK = 64
GLA_QK_DIM = GLA_HEADS * GLA_DK
GLA_V_DIM = GLA_HEADS * GLA_DV

N_BRANCH = 3

SPLITS = (ATT_DIM, KV_DIM, KV_DIM, POOL_DIM, GLA_QK_DIM, GLA_QK_DIM, GLA_V_DIM,
          GLA_V_DIM, 2 * GLA_GATE_RANK, N_BRANCH * D_MODEL)
SPLIT_IDX = tuple(int(s) for s in np.cumsum(SPLITS)[:-1])
IN_DIM = int(sum(SPLITS))

D_FF = 2816
CONV_W = 3

kernel_name = "hybrid_gated_branch_flow_block"

F32 = jnp.float32

def rmsnorm(x, g):
    xf = x.astype(F32)
    y = xf * lax.rsqrt(jnp.mean(xf * xf, axis=-1, keepdims=True) + EPS)
    return (y * g.astype(F32)).astype(x.dtype)

def axial_rope_tables(L):
    rows = L // GRID_W
    row = jnp.repeat(jnp.arange(rows, dtype=F32), GRID_W)
    col = jnp.tile(jnp.arange(GRID_W, dtype=F32), rows)
    n = HEAD_DIM // 4
    inv = ROPE_BASE ** (-jnp.arange(n, dtype=F32) / n)
    ang = jnp.concatenate([row[:, None] * inv, col[:, None] * inv], axis=-1)
    return jnp.cos(ang), jnp.sin(ang)

def apply_rope(x, cos, sin):
    xf = x.astype(F32)
    half = HEAD_DIM // 2
    x1, x2 = xf[..., :half], xf[..., half:]
    c = cos[None, :, None, :]
    s = sin[None, :, None, :]
    return jnp.concatenate([x1 * c - x2 * s, x1 * s + x2 * c], axis=-1).astype(x.dtype)

def window_attention(q, k, v, k_ctx, v_ctx, sink):
    B, L = q.shape[:2]
    C = k_ctx.shape[1]
    nb = L // ATT_BLOCK
    scale = HEAD_DIM ** -0.5
    qb = q.reshape(B, nb, ATT_BLOCK, ATT_KV_HEADS, ATT_GROUP, HEAD_DIM)
    pad = ((0, 0), (ATT_BLOCK, ATT_BLOCK), (0, 0), (0, 0))
    kp = jnp.pad(k, pad).reshape(B, nb + 2, ATT_BLOCK, ATT_KV_HEADS, HEAD_DIM)
    vp = jnp.pad(v, pad).reshape(B, nb + 2, ATT_BLOCK, ATT_KV_HEADS, HEAD_DIM)
    kw = jnp.concatenate([kp[:, :-2], kp[:, 1:-1], kp[:, 2:]], axis=2)
    vw = jnp.concatenate([vp[:, :-2], vp[:, 1:-1], vp[:, 2:]], axis=2)
    s_loc = jnp.einsum('bnqkgd,bnskd->bnkgqs', qb, kw, preferred_element_type=F32) * scale
    s_ctx = jnp.einsum('bnqkgd,bckd->bnkgqc', qb, k_ctx, preferred_element_type=F32) * scale
    qi = jnp.arange(ATT_BLOCK)[:, None]
    kj = jnp.arange(3 * ATT_BLOCK)[None, :]
    band = jnp.abs(kj - ATT_BLOCK - qi) <= WINDOW
    kpos = jnp.arange(nb)[:, None] * ATT_BLOCK - ATT_BLOCK + jnp.arange(3 * ATT_BLOCK)[None, :]
    valid = (kpos >= 0) & (kpos < L)
    mask = band[None, :, :] & valid[:, None, :]
    s_loc = jnp.where(mask[None, :, None, None], s_loc, -jnp.inf)
    sk = jnp.broadcast_to(sink.astype(F32).reshape(ATT_KV_HEADS, ATT_GROUP)[:, :, None, None],
                          s_loc.shape[:-1] + (1,))
    p = jax.nn.softmax(jnp.concatenate([s_loc, s_ctx, sk], axis=-1), axis=-1)
    nl = 3 * ATT_BLOCK
    p_loc = p[..., :nl].astype(v.dtype)
    p_ctx = p[..., nl:nl + C].astype(v.dtype)
    o = (jnp.einsum('bnkgqs,bnskd->bnqkgd', p_loc, vw)
         + jnp.einsum('bnkgqc,bckd->bnqkgd', p_ctx, v_ctx))
    return o.reshape(B, L, ATT_DIM)

def ctx_attention(q, k, v, sink):
    B, C = q.shape[:2]
    qg = q.reshape(B, C, ATT_KV_HEADS, ATT_GROUP, HEAD_DIM)
    s = jnp.einsum('bqkgd,bskd->bkgqs', qg, k, preferred_element_type=F32) * (HEAD_DIM ** -0.5)
    sk = jnp.broadcast_to(sink.astype(F32).reshape(ATT_KV_HEADS, ATT_GROUP)[:, :, None, None],
                          s.shape[:-1] + (1,))
    p = jax.nn.softmax(jnp.concatenate([s, sk], axis=-1), axis=-1)[..., :C].astype(v.dtype)
    return jnp.einsum('bkgqs,bskd->bqkgd', p, v).reshape(B, C, ATT_DIM)

def multiscale_pool(u):
    T = u.shape[1]
    uf = u.astype(F32)
    cs = jnp.pad(jnp.cumsum(uf, axis=1), ((0, 0), (1, 0), (0, 0)))
    t = jnp.arange(T)
    outs = []
    for g, w in enumerate(POOL_WINDOWS):
        lo = w // 2
        hi = w - lo - 1
        start = jnp.clip(t - lo, 0, T)
        end = jnp.clip(t + hi + 1, 0, T)
        sl = slice(g * POOL_GROUP_DIM, (g + 1) * POOL_GROUP_DIM)
        csg = cs[..., sl]
        cnt = (end - start).astype(F32)
        outs.append((csg[:, end] - csg[:, start]) / cnt[None, :, None] - uf[..., sl])
    return jnp.concatenate(outs, axis=-1)

def pool_branch(u, pool_w, pool_scale):
    B, T, _ = u.shape
    d = multiscale_pool(u).astype(u.dtype).reshape(B, T, POOL_GROUPS, POOL_GROUP_DIM)
    y = jnp.einsum('btgi,gio->btgo', d, pool_w).reshape(B, T, POOL_DIM)
    return y * pool_scale

def gla_inputs(gq, gk, gv, glr, gla_wa2, gla_ba):
    B, T = gq.shape[:2]
    q = gq.reshape(B, T, GLA_HEADS, GLA_DK) * (GLA_DK ** -0.5)
    k = gk.reshape(B, T, GLA_HEADS, GLA_DK)
    v = gv.reshape(B, T, GLA_HEADS, GLA_DV)
    lr = glr.astype(F32).reshape(B, T, 2, GLA_GATE_RANK)
    z = jnp.einsum('btnr,nrd->btnd', lr, gla_wa2.astype(F32)) + gla_ba.astype(F32)
    log_a = jax.nn.log_sigmoid(z) / GLA_TAU
    la_f = log_a[:, :, 0].reshape(B, T, GLA_HEADS, GLA_DK)
    la_b = log_a[:, :, 1].reshape(B, T, GLA_HEADS, GLA_DK)
    return q, k, v, la_f, la_b

def gla_scan(q, k, v, log_a, state0):
    B, T = q.shape[:2]
    n = T // GLA_CHUNK

    def to_chunks(t):
        return t.reshape(B, n, GLA_CHUNK, GLA_HEADS, -1).transpose(1, 0, 3, 2, 4).astype(F32)

    tri = jnp.tril(jnp.ones((GLA_CHUNK, GLA_CHUNK), dtype=bool))

    def step(S, inp):
        qi, ki, vi, ai = inp
        b = jnp.cumsum(ai, axis=2)
        b_last = b[:, :, -1:, :]
        o_inter = jnp.einsum('bhcd,bhde->bhce', qi * jnp.exp(b), S)
        diff = b[:, :, :, None, :] - b[:, :, None, :, :]
        decay = jnp.exp(jnp.where(tri[:, :, None], diff, -jnp.inf))
        att = jnp.einsum('bhid,bhjd,bhijd->bhij', qi, ki, decay)
        o = o_inter + jnp.einsum('bhij,bhje->bhie', att, vi)
        S_new = (S * jnp.exp(b_last[:, :, 0, :])[..., None]
                 + jnp.einsum('bhcd,bhce->bhde', ki * jnp.exp(b_last - b), vi))
        return S_new, o

    S_fin, o = lax.scan(step, state0, (to_chunks(q), to_chunks(k), to_chunks(v), to_chunks(log_a)))
    o = o.transpose(1, 0, 3, 2, 4).reshape(B, T, GLA_HEADS, GLA_DV)
    return o, S_fin

def flip(t):
    return t[:, ::-1]

def gla_output(o, r, gla_norm):
    B, T = o.shape[:2]
    on = o * lax.rsqrt(jnp.mean(o * o, axis=-1, keepdims=True) + EPS) * gla_norm.astype(F32)
    return on.reshape(B, T, GLA_V_DIM).astype(r.dtype) * jax.nn.silu(r)

def merge_branches(y_att, y_pool, y_gla, mg, w_br_att, w_br_pool, w_br_gla, w_o):
    B, T = y_att.shape[:2]
    g = jax.nn.sigmoid(mg).reshape(B, T, N_BRANCH, D_MODEL)
    m = (g[:, :, 0] * (y_att @ w_br_att) + g[:, :, 1] * (y_pool @ w_br_pool)
         + g[:, :, 2] * (y_gla @ w_br_gla))
    return m @ w_o

def token_mixer(h, hc, need_ctx, w_in, att_sink, pool_w, pool_scale, gla_wa2, gla_ba, gla_norm,
                w_br_att, w_br_pool, w_br_gla, w_o):
    B, L, _ = h.shape
    C = hc.shape[1]
    aq, ak, av, pu, gq, gk, gv, gr, glr, mg = jnp.split(h @ w_in, SPLIT_IDX, axis=-1)
    caq, cak, cav, cpu, cgq, cgk, cgv, cgr, cglr, cmg = jnp.split(hc @ w_in, SPLIT_IDX, axis=-1)

    k_ctx = cak.reshape(B, C, ATT_KV_HEADS, HEAD_DIM)
    v_ctx = cav.reshape(B, C, ATT_KV_HEADS, HEAD_DIM)
    cos, sin = axial_rope_tables(L)
    q = apply_rope(aq.reshape(B, L, ATT_HEADS, HEAD_DIM), cos, sin)
    k = apply_rope(ak.reshape(B, L, ATT_KV_HEADS, HEAD_DIM), cos, sin)
    v = av.reshape(B, L, ATT_KV_HEADS, HEAD_DIM)
    y_att = window_attention(q, k, v, k_ctx, v_ctx, att_sink)

    y_pool = pool_branch(pu, pool_w, pool_scale)

    lq, lk, lv, la_f, la_b = gla_inputs(gq, gk, gv, glr, gla_wa2, gla_ba)
    xq, xk, xv, xa_f, xa_b = gla_inputs(cgq, cgk, cgv, cglr, gla_wa2, gla_ba)
    S0 = jnp.zeros((B, GLA_HEADS, GLA_DK, GLA_DV), F32)
    co_f, S_f = gla_scan(xq, xk, xv, xa_f, S0)
    co_b, S_b = gla_scan(flip(xq), flip(xk), flip(xv), flip(xa_b), S0)
    o_f, _ = gla_scan(lq, lk, lv, la_f, S_f)
    o_b, _ = gla_scan(flip(lq), flip(lk), flip(lv), flip(la_b), S_b)
    y_gla = gla_output(o_f + flip(o_b), gr, gla_norm)

    y = merge_branches(y_att, y_pool, y_gla, mg, w_br_att, w_br_pool, w_br_gla, w_o)
    if not need_ctx:
        return y, None
    yc_att = ctx_attention(caq.reshape(B, C, ATT_HEADS, HEAD_DIM), k_ctx, v_ctx, att_sink)
    yc_pool = pool_branch(cpu, pool_w, pool_scale)
    yc_gla = gla_output(co_f + flip(co_b), cgr, gla_norm)
    yc = merge_branches(yc_att, yc_pool, yc_gla, cmg, w_br_att, w_br_pool, w_br_gla, w_o)
    return y, yc

def conv_ffn(h, w_up, conv_w, conv_b, w_down):
    u = h @ w_up
    up = jnp.pad(u, ((0, 0), (1, 1), (0, 0)))
    u = up[:, :-2] * conv_w[0] + up[:, 1:-1] * conv_w[1] + up[:, 2:] * conv_w[2] + conv_b
    a, g = jnp.split(u, 2, axis=-1)
    return (a * jax.nn.silu(g)) @ w_down

def setup_inputs(seed: int = 0) -> dict:
    key = jax.random.key(seed)
    ks = jax.random.split(key, 28)

    def nrm(k, shape, scale):
        return jax.random.normal(k, shape, F32) * scale

    return {
        "x": nrm(ks[0], (BATCH, SEQ, D_MODEL), 1.0),
        "c": nrm(ks[1], (BATCH, D_MODEL), 1.0),
        "ctx": nrm(ks[2], (BATCH, CTX_LEN, D_MODEL), 1.0),
        "c_ctx": nrm(ks[3], (D_MODEL,), 1.0),
        "w_ada": nrm(ks[4], (DEPTH, D_MODEL, 6 * D_MODEL), 0.5 * D_MODEL ** -0.5),
        "b_ada": nrm(ks[5], (DEPTH, 6 * D_MODEL), 0.01),
        "g_pre_mix": 1.0 + nrm(ks[6], (DEPTH, D_MODEL), 0.02),
        "g_post_mix": 1.0 + nrm(ks[7], (DEPTH, D_MODEL), 0.02),
        "g_pre_ffn": 1.0 + nrm(ks[8], (DEPTH, D_MODEL), 0.02),
        "g_post_ffn": 1.0 + nrm(ks[9], (DEPTH, D_MODEL), 0.02),
        "w_in": nrm(ks[10], (DEPTH, D_MODEL, IN_DIM), D_MODEL ** -0.5),
        "att_sink": nrm(ks[11], (DEPTH, ATT_HEADS), 0.5),
        "pool_w": nrm(ks[12], (DEPTH, POOL_GROUPS, POOL_GROUP_DIM, POOL_GROUP_DIM), POOL_GROUP_DIM ** -0.5),
        "pool_scale": 1.0 + nrm(ks[13], (DEPTH, POOL_DIM), 0.02),
        "gla_wa2": nrm(ks[14], (DEPTH, 2, GLA_GATE_RANK, GLA_QK_DIM), GLA_GATE_RANK ** -0.5),
        "gla_ba": 1.0 + nrm(ks[15], (DEPTH, 2, GLA_QK_DIM), 0.1),
        "gla_norm": 1.0 + nrm(ks[16], (DEPTH, GLA_HEADS, GLA_DV), 0.02),
        "w_br_att": nrm(ks[17], (DEPTH, ATT_DIM, D_MODEL), ATT_DIM ** -0.5),
        "w_br_pool": nrm(ks[18], (DEPTH, POOL_DIM, D_MODEL), POOL_DIM ** -0.5),
        "w_br_gla": nrm(ks[19], (DEPTH, GLA_V_DIM, D_MODEL), GLA_V_DIM ** -0.5),
        "w_o": nrm(ks[20], (DEPTH, D_MODEL, D_MODEL), D_MODEL ** -0.5),
        "w_up": nrm(ks[21], (DEPTH, D_MODEL, 2 * D_FF), D_MODEL ** -0.5),
        "conv_w": nrm(ks[22], (DEPTH, CONV_W, 2 * D_FF), CONV_W ** -0.5),
        "conv_b": nrm(ks[23], (DEPTH, 2 * D_FF), 0.01),
        "w_down": nrm(ks[24], (DEPTH, D_FF, D_MODEL), D_FF ** -0.5),
    }

def reference(x, c, ctx, c_ctx, w_ada, b_ada, g_pre_mix, g_post_mix, g_pre_ffn, g_post_ffn,
              w_in, att_sink, pool_w, pool_scale, gla_wa2, gla_ba, gla_norm,
              w_br_att, w_br_pool, w_br_gla, w_o, w_up, conv_w, conv_b, w_down):
    for l in range(DEPTH):
        last = l == DEPTH - 1
        m = jax.nn.silu(c) @ w_ada[l] + b_ada[l]
        mc = jax.nn.silu(c_ctx) @ w_ada[l] + b_ada[l]
        sh1, sc1, g1, sh2, sc2, g2 = jnp.split(m[:, None, :], 6, axis=-1)
        csh1, csc1, cg1, csh2, csc2, cg2 = jnp.split(mc, 6)

        h = rmsnorm(x, g_pre_mix[l]) * (1.0 + sc1) + sh1
        hc = rmsnorm(ctx, g_pre_mix[l]) * (1.0 + csc1) + csh1
        y, yc = token_mixer(h, hc, not last, w_in[l], att_sink[l], pool_w[l], pool_scale[l],
                            gla_wa2[l], gla_ba[l], gla_norm[l], w_br_att[l], w_br_pool[l],
                            w_br_gla[l], w_o[l])
        x = x + g1 * rmsnorm(y, g_post_mix[l])
        h = rmsnorm(x, g_pre_ffn[l]) * (1.0 + sc2) + sh2
        x = x + g2 * rmsnorm(conv_ffn(h, w_up[l], conv_w[l], conv_b[l], w_down[l]), g_post_ffn[l])

        if not last:
            ctx = ctx + cg1 * rmsnorm(yc, g_post_mix[l])
            hc = rmsnorm(ctx, g_pre_ffn[l]) * (1.0 + csc2) + csh2
            ctx = ctx + cg2 * rmsnorm(conv_ffn(hc, w_up[l], conv_w[l], conv_b[l], w_down[l]), g_post_ffn[l])
    return x


_drawn_inputs = setup_inputs


def setup_inputs(seed=0):
    import zlib

    import numpy as np

    out = dict(_drawn_inputs(seed))
    spreads = {}
    factors = {'g_pre_mix': 4.584,
     'g_post_mix': 6.736,
     'g_pre_ffn': 5.049,
     'g_post_ffn': 6.872,
     'att_sink': 8.0,
     'pool_scale': 8.0,
     'gla_ba': 4.0,
     'gla_norm': 8.0,
     'conv_b': 8.0}
    for name, (base, spread) in spreads.items():
        noise = np.random.default_rng([zlib.crc32(name.encode()), seed]).standard_normal(out[name].shape)
        drawn = base * np.exp(spread * noise) if base else spread * noise
        out[name] = __import__('jax').numpy.asarray(drawn.astype(out[name].dtype))
    for name, factor in factors.items():
        out[name] = (out[name] * factor).astype(out[name].dtype)
    return out
```

```python
from contextlib import ExitStack

import numpy as np

import concourse.bass as bass
from concourse import mybir

ALU = mybir.AluOpType
ACT = mybir.ActivationFunctionType
F32 = mybir.dt.float32
F32R = mybir.dt.float32r
I32 = mybir.dt.int32
AX_X = mybir.AxisListType.X

P = 128
DEPTH = 2
D = 1024
KT = D // P
NX, NC = 512, 256
T = NX + NC
EPS = 1e-6
GRID_W = 64
HD = 64
NQT = 4
GLA_H, DK, DV, CH = 4, 32, 64, 64
NCH = T // CH
TAU = 16.0
NFF = 2816 // P
BLK = 1024
RAW, SPL = 4, 2
NEG = -3.0e38
LEVELS = (32, 16, 8, 4, 2, 1)
NGRAM = len(LEVELS) + 1

TQ, TK, TV, TPOOL, TGQ, TGK, TGV, TGR, TLR = 0, 4, 5, 6, 8, 9, 10, 12, 14
NPROJ = 15
EARLY = (TLR, TGK, TGV, TGV + 1, TGQ, TGR, TGR + 1)
LATE = (TK, TV, 0, 1, 2, 3, TPOOL, TPOOL + 1)
WITH_CTX = (TLR, TGK, TGV, TGV + 1, TK, TV)

(C_BADA, C_GPRE, C_GPOST, C_GPRE2, C_GPOST2, C_PSC, C_BA, C_GN, C_CW, C_CB, C_SINK, NPAR) = np.cumsum(
    [0, 48, 8, 8, 8, 8, 2, 2, 2, 3 * 2 * NFF, 2 * NFF, 8]).tolist()
K_ONES, K_BONES, K_ROT, K_ID, NCON = 0, 128, 256, 384, 512
SH1, SC1, G1, SH2, SC2, G2 = range(0, 48, 8)


class Plan:

    def __init__(self):
        self.group_end = []
        self.branch_end = []
        self.layers = []
        g = q = 0
        for _ in range(DEPTH):
            at = {"early_q": q, "early_g": g}
            for _ in EARLY:
                g += 1
                self.group_end.append(g)
            at["late_q"], at["late_g"] = len(self.group_end), g
            for _ in LATE:
                g += 1
                self.group_end.append(g)
            at["gate_q"], at["gate_g"], at["gate_b"] = len(self.group_end), g, len(self.branch_end)
            for j in range(KT):
                mixing = 0 if j else 2
                self.group_end += [g + 1, g + 3 + mixing]
                g += 4 + mixing
                if j % 2:
                    self.branch_end.append(g)
            at["mix_q"], at["mix_g"], at["mix_b"] = len(self.group_end), g, len(self.branch_end)
            for c in range(KT // 2 + 1):
                if c < KT // 2:
                    self.group_end += [g + 1, g + 3]
                    g += 4
                    self.branch_end.append(g)
                if c > 0:
                    self.group_end += [g + 4, g + 8]
                    g += 8
            at["ffn_q"], at["ffn_g"] = len(self.group_end), g
            for c in range(NFF // 2 + 1):
                if c < NFF // 2:
                    self.group_end += [g + 1, g + 2, g + 3, g + 4]
                    g += 4
                if c > 0:
                    self.group_end += [g + 4, g + 8]
                    g += 8
            q = len(self.group_end)
            at["end_g"] = g
            self.layers.append(at)
        self.blocks = q
        self.branches = len(self.branch_end)


PLAN = Plan()
FFN_BODY_Q, FFN_BODY_G, FFN_LOOPS = 12, 24, (NFF // 2 - 1) // 2


class Chain:

    def __init__(self, eng, sem):
        self.eng, self.sem, self.n, self.shift = eng, sem, 0, 0

    def __call__(self, ins):
        ins.then_inc(self.sem, 1)
        self.n += 1
        self.eng.wait_ge(self.sem, self.n + self.shift)

    def enter(self, reg, per):
        self.start, self.per, self.shift = self.n, per, reg * per

    def leave(self, loops):
        assert self.n - self.start == self.per, (self.n - self.start, self.per)
        self.n, self.shift = self.start + self.per * loops, 0


def segments(ctx):
    return [(0, NX, 0), (NX, T, 1)] if ctx else [(0, NX, 0)]


def build(nc, x_t, c_t, par_d, con_d, ada_d, wst_d, brw_d, wa2_d, poolw_d, scanm_d, gmask_d, amask_d, rope_d, inv_d,
          out):
    spill = nc.dram_tensor("x_spill", (P, KT * T), F32).ap()
    with ExitStack() as es:
        def sem(name):
            return es.enter_context(nc.semaphore(name))

        def sb(name, shape, dt=F32, stack=es):
            return stack.enter_context(nc.sbuf_tensor(name, shape, dt))

        hhi = sb("hhi", [P, KT, T], F32R)
        hlo = sb("hlo", [P, KT, T], F32R)
        whi = sb("whi", [P, SPL, BLK], F32R)
        wlo = sb("wlo", [P, SPL, BLK], F32R)
        raw = sb("raw", [P, RAW, BLK])
        brw = sb("brw", [P, 2, 2, 4, P])
        par = sb("par", [P, DEPTH, NPAR])
        con = sb("con", [P, NCON])
        cvec = sb("cvec", [P, KT, 2])
        ada = sb("ada", [P, DEPTH, 48, 2])
        wa2 = sb("wa2", [32, DEPTH, 256])
        poolw = sb("poolw", [P, DEPTH, 256])
        gmask = sb("gmask", [P, NGRAM, CH], I32)
        small = sb("small", [P, 2, 24])
        eps = sb("eps", [P, 1])
        dec = sb("dec", [P, 2, NCH])
        bt = sb("bt", [P, KT, T])
        y = sb("y", [P, KT, T])
        over = ExitStack()
        gact = sb("gact", [P, 2, 2, 2, T], F32R, over)
        over.close()
        ext = sb("ext", [P, 3840])
        proj = sb("proj", [P, NPROJ, T])
        x = proj[:, TPOOL + 1:NPROJ, :]
        part = x

        ones, bones = con[:, K_ONES:K_ONES + P], con[:, K_BONES:K_BONES + P]
        rot, ident = con[:, K_ROT:K_ROT + P], con[:, K_ID:K_ID + P]

        sq = [bt[:, 0, :], bt[:, 1, :]]
        rstd = bt[:, 2, :]
        tmp = [bt[:, 3, :], bt[:, 4, :]]
        conv_a = [bt[:, 3, :], bt[:, 4, :]]
        conv_g = [bt[:, 5, :], bt[:, 6, :]]
        adaw = y[:, 0:6, :].rearrange("p a b -> p (a b)")[:, 0:4 * BLK].rearrange("p (s n) -> p s n", s=4)
        cumf, cumb = y[:, 0, :], y[:, 1, :]
        pair = [y[:, 2:4, :], y[:, 4:6, :]]
        qdec = y[:, 6:8, :]
        vtok = ext[:, 0:6 * 256].rearrange("p (b n) -> p b n", b=6)
        ktok = ext[:, 1536:3072].rearrange("p (d b n) -> p d b n", d=2, b=6)
        scanm = ext[:, 3072:3072 + T]
        attg = bt[:, 0:2, :].rearrange("p a b -> p (a b)").rearrange("p (h c i) -> p h c i", h=GLA_H, c=6)
        state = bt[:, 2:4, :].rearrange("p d (c e) -> p d c e", c=NCH)
        yf = y[:, :, :].rearrange("p a b -> p (a b)")
        sco = [yf[:, 0:2560].rearrange("p (r k) -> p r k", r=4), yf[:, 2560:5120].rearrange("p (r k) -> p r k", r=4)]
        vat = yf[:, 5120:5120 + 768].rearrange("p (b n) -> p b n", b=6)
        ptb = [ext[:, 0:512], ext[:, 512:1024]]
        gates = [ext[:, 1024:1024 + T], ext[:, 1792:1792 + T]]
        gtmp = ext[:, 2560:2560 + T]
        amask = ext[:, 3328:3328 + 3 * P]
        ropec, ropes = ext[:, 1024:1536], ext[:, 1536:2048]
        up, pa, pb = (sco[1].rearrange("p r k -> p (r k)")[:, i * 800:i * 800 + 800] for i in range(3))
        inv = bt[:, 0:2, :]
        mgate = [proj[:, 3, :], proj[:, 4, :]]
        mtmp = proj[:, 5, :]

        acc = es.enter_context(nc.psum_tensor("acc", [P, 2, 1024], F32))
        aux = es.enter_context(nc.psum_tensor("aux", [P, 4, 512], F32))
        auxw = aux[:, :, :].rearrange("p (t b) n -> p t (b n)", b=2)

        aux_flat = aux[:, :, :].rearrange("p b n -> p (b n)")

        consts_in = sem("consts_in")
        x_in = sem("x_in")
        x_spilled = sem("x_spilled")
        tables_in = sem("tables_in")
        scanm_in = sem("scanm_in")
        out_done = sem("out_done")
        w_landed = [sem(f"w_landed{i}") for i in range(RAW)]
        b_landed = [sem(f"b_landed{i}") for i in range(2)]
        ada_landed = [sem(f"ada_landed{i}") for i in range(4)]
        ada_used = sem("ada_used")
        cond_ready = sem("cond_ready")
        cvec_ready = sem("cvec_ready")
        w_hi = sem("w_hi")
        w_split = sem("w_split")
        mm_done = sem("mm_done")
        acc_free = [sem("acc_free0"), sem("acc_free1")]
        sq_ready = sem("sq_ready")
        sq_used = sem("sq_used")
        rstd_ready = sem("rstd_ready")
        t_ready = sem("t_ready")
        h_hi = sem("h_hi")
        h_ready = sem("h_ready")
        x_ready = sem("x_ready")
        y_zero = sem("y_zero")
        z_full, z_used, z_log = sem("z_full"), sem("z_used"), sem("z_log")
        cum_ready = sem("cum_ready")
        v_full, v_ready = sem("v_full"), sem("v_ready")
        kd_args, kd_exp, kd_ready = sem("kd_args"), sem("kd_exp"), sem("kd_ready")
        kt_full, kt_ready = sem("kt_full"), sem("kt_ready")
        u_full, states_ready = sem("u_full"), sem("states_ready")
        e_args, e_exp, ab_ready = sem("e_args"), sem("e_exp"), sem("ab_ready")
        gram_full, gram_used = sem("gram_full"), sem("gram_used")
        o_full, o_copied, o_sum, o_rstd, gla_out = (sem(n) for n in ("o_full", "o_copied", "o_sum", "o_rstd", "gla_out"))
        pool_d = sem("pool_d")
        rot_full, rot_used, rope_done = sem("rot_full"), sem("rot_used"), sem("rope_done")
        va_full, va_ready = sem("va_full"), sem("va_ready")
        s_full, s_local, s_ctx = sem("s_full"), sem("s_local"), sem("s_ctx")
        m_ready, p_exp, r_ready, p_ready = sem("m_ready"), sem("p_exp"), sem("r_ready"), sem("p_ready")
        pt_full, pt_ready = sem("pt_full"), sem("pt_ready")
        pv_full, pv_used = sem("pv_full"), sem("pv_used")
        r_silu = sem("r_silu")
        conv_mid = sem("conv_mid")
        g_val, g_hi, g_ready = sem("g_val"), sem("g_hi"), sem("g_ready")
        silu_ready = sem("silu_ready")
        eps_set = sem("eps_set")
        dve_link, act_link, pool_link = sem("dve_link"), sem("act_link"), sem("pool_link")

        def units(l):
            return [(qb, g) for qb in range(4 if l == DEPTH - 1 else 6) for g in range(2)]

        def local_blocks(qb):
            return list(range(max(qb - 1, 0), min(qb + 2, 4))) if qb < 4 else []

        unit_base, head_base, lhead_base, blk_base = [0], [0], [0], [0]
        for l in range(DEPTH):
            us = units(l)
            unit_base.append(unit_base[-1] + len(us))
            head_base.append(head_base[-1] + 4 * len(us))
            lhead_base.append(lhead_base[-1] + 4 * sum(qb < 4 for qb, _ in us))
            blk_base.append(blk_base[-1] + sum(len(local_blocks(qb)) + 2 for qb, _ in us))

        def gate_group(l, j, n):
            return PLAN.layers[l]["gate_g"] + 4 * j + n + (2 if j + n else 0)

        def key_blocks(l, u):
            return local_blocks(units(l)[u][0]) + [4, 5]

        def block_index(l, u, b):
            return blk_base[l] + sum(len(key_blocks(l, v)) for v in range(u)) + b

        def g_count(l, part_, tiles):
            return l * (KT + NFF) + (KT if part_ == "ffn" else 0) + tiles

        def wait_evac(eng, g):
            eng.wait_ge(acc_free[g % 2], g // 2 + 1)

        def x_valid(eng, l, post, kt):
            if post == 0:
                eng.wait_ge(x_in, 16)
            else:
                eng.wait_ge(x_ready, KT * (post - 1) + kt + 1)

        def norm_ctx(k):
            return k % 4 == 0 or k // 4 < DEPTH - 1

        def norm_source_ready(eng, k, kt):
            l, part_ = divmod(k, 4)
            if part_ in (0, 2):
                x_valid(eng, l, 2 * l + part_ // 2, kt)
            else:
                end = PLAN.layers[l]["ffn_g" if part_ == 1 else "end_g"]
                wait_evac(eng, end - KT + kt)

        block = es.enter_context(nc.Block())

        @block.sync
        def _(sp):
            for dst, src in ((cvec[:, :, :], c_t), (par[:, :, :], par_d), (con[:, :], con_d), (wa2[:, :, :], wa2_d),
                             (poolw[:, :, :], poolw_d), (gmask[:, :, :], gmask_d)):
                sp.dma_start(dst, src).then_inc(consts_in, 16)
            for s in range(4):
                sp.dma_start(adaw[:, s, :], ada_d[s]).then_inc(ada_landed[s], 16)
            sp.dma_start(x, x_t).then_inc(x_in, 16)
            with sp.Fori(1, DEPTH * 48 // 4) as i:
                for s in range(4):
                    sp.wait_ge(ada_used, 4 * i + s - 3)
                    sp.dma_start(adaw[:, s, :], ada_d[4 * i + s]).then_inc(ada_landed[s], 16)

            def weights(q, i=0, per=0):
                if q >= RAW:
                    sp.wait_ge(w_split, q - RAW + 1 + per * i)
                sp.dma_start(raw[:, q % RAW, :], wst_d[q + per * i]).then_inc(w_landed[q % RAW], 16)

            def branch(b):
                if b >= 2:
                    sp.wait_ge(mm_done, PLAN.branch_end[b - 2])
                sp.dma_start(brw[:, b % 2, :, :, :], brw_d[b]).then_inc(b_landed[b % 2], 16)

            for l, at in enumerate(PLAN.layers):
                for q in range(at["early_q"], at["early_q"] + RAW):
                    weights(q)
                if l > 0:
                    for kt in range(KT):
                        x_valid(sp, l, 2 * l, kt)
                    sp.dma_start(spill, x).then_inc(x_spilled, 16)
                    sp.wait_ge(mm_done, PLAN.layers[l - 1]["end_g"])
                sp.dma_start(scanm, scanm_d).then_inc(scanm_in, 16)
                for q in range(at["early_q"] + RAW, at["gate_q"]):
                    weights(q)
                branch(at["gate_b"])
                weights(at["gate_q"])
                weights(at["gate_q"] + 1)
                sp.wait_ge(o_full, l + 1)
                sp.dma_start(ext[:, 1024:2048], rope_d).then_inc(tables_in, 16)
                sp.dma_start(inv, inv_d).then_inc(tables_in, 16)
                sp.dma_start(amask, amask_d).then_inc(tables_in, 16)
                for n, q in enumerate(range(at["gate_q"] + 2, at["mix_q"])):
                    if n % 4 == 0 and 0 < n // 4 + 1 < 4:
                        branch(at["gate_b"] + n // 4 + 1)
                    weights(q)
                for q in range(at["mix_q"], at["ffn_q"]):
                    n = q - at["mix_q"]
                    if n in (0, 2, 4, 6):
                        branch(at["mix_b"] + n // 2)
                    weights(q)
                sp.wait_ge(g_ready, g_count(l, "mix", KT))
                if l == 0:
                    sp.dma_start(x, x_t).then_inc(x_in, 16)
                else:
                    sp.wait_ge(x_spilled, 16 * l)
                    sp.dma_start(x, spill).then_inc(x_in, 16)
                q0 = at["ffn_q"]
                for q in range(q0, q0 + 4):
                    weights(q)
                with sp.Fori(0, FFN_LOOPS) as i:
                    for p in range(FFN_BODY_Q):
                        weights(q0 + 4 + p, i, FFN_BODY_Q)
                for q in range(q0 + 4 + FFN_BODY_Q * FFN_LOOPS, PLAN.layers[l + 1]["early_q"] if l + 1 < DEPTH else PLAN.blocks):
                    weights(q)
            for kt in range(KT):
                x_valid(sp, DEPTH, 2 * DEPTH, kt)
                sp.dma_start(out[:, kt, :], x[:, kt, 0:NX]).then_inc(out_done, 16)
            sp.wait_ge(out_done, 16 * KT)

        @block.tensor
        def _(pe):
            def product(g, q, ctx, ks, i=0, per_g=0, first=True, last=True, h=None):
                s = q % SPL
                for k in ks:
                    if h is not None:
                        pe.wait_ge(h_ready, KT * h + k + 1)
                    for w_, a_ in ((whi, hhi), (whi, hlo), (wlo, hhi)):
                        start = first and k == ks[0] and w_ is whi and a_ is hhi
                        stop = last and k == ks[-1] and w_ is wlo
                        for t0, t1, _ in segments(ctx):
                            mm = pe.matmul(acc[:, g % 2, t0:t1], w_[:, s, k * P:k * P + P], a_[:, k, t0:t1],
                                           start=start, stop=stop)
                if last:
                    mm.then_inc(mm_done, 1)

            def open_group(g, i=0, per=0):
                if g >= 2:
                    pe.wait_ge(acc_free[g % 2], g // 2 + (per // 2) * i)

            def block_split(q, i=0, per=0):
                pe.wait_ge(w_split, q + 1 + per * i)

            def norm_sum(k):
                for kt in range(KT):
                    n = KT * k + kt
                    pe.wait_ge(sq_ready, n + 1)
                    for t0, t1, b in segments(norm_ctx(k)):
                        mm = pe.matmul(aux[:, b, 0:t1 - t0], ones, sq[n % 2][:, t0:t1], start=kt == 0, stop=kt == KT - 1)
                    mm.then_inc(sq_used, 1)

            pe.wait_ge(cvec_ready, 1)
            adap = aux[:, 0, 0:DEPTH * 96]
            with pe.Fori(0, DEPTH * 48 // 4) as i:
                for s in range(4):
                    for kt in range(KT):
                        if kt == 0:
                            pe.wait_ge(ada_landed[s], 16 * i + 16)
                        mm = pe.matmul(adap[:, bass.ds(8 * i + 2 * s, 2)], adaw[:, s, kt * P:kt * P + P], cvec[:, kt, :],
                                       start=kt == 0, stop=kt == KT - 1)
                    mm.then_inc(ada_used, 1)

            def early_block(l, n):
                at = PLAN.layers[l]
                g, q = at["early_g"] + n, at["early_q"] + n
                block_split(q)
                open_group(g)
                product(g, q, l < DEPTH - 1 or EARLY[n] in WITH_CTX, range(KT), h=2 * l if n == 0 else None)

            def late_block(l, n):
                at = PLAN.layers[l]
                g, q = at["late_g"] + n, at["late_q"] + n
                block_split(q)
                open_group(g)
                product(g, q, l < DEPTH - 1 or LATE[n] in WITH_CTX, range(KT))

            def early_group(l, tile):
                return PLAN.layers[l]["early_g"] + EARLY.index(tile)

            def gla_z(l):
                wait_evac(pe, early_group(l, TLR))
                for d in range(2):
                    for t0, t1, b in segments(True):
                        mm = pe.matmul(aux[:, 2 * d + b, 0:t1 - t0], wa2[:, l, d * P:d * P + P],
                                       proj[0:32, TLR, t0:t1], start=True, stop=True)
                mm.then_inc(z_full, 1)

            def gla_values(l):
                for t in range(2):
                    wait_evac(pe, early_group(l, TGV + t))
                pe.wait_ge(z_used, 2 * (l + 1))
                for b in range(6):
                    for t in range(2):
                        mm = pe.transpose(aux[:, b // 2, (b % 2) * 256 + t * P:(b % 2) * 256 + t * P + P],
                                          proj[:, TGV + t, b * P:b * P + P], ident)
                mm.then_inc(v_full, 1)

            def gla_keys(l):
                pe.wait_ge(kd_ready, l + 1)
                pe.wait_ge(v_ready, l + 1)
                for d in range(2):
                    for b in range(6):
                        n = 6 * d + b
                        mm = pe.transpose(aux[:, n // 4, (n % 4) * P:(n % 4) * P + P],
                                          pair[1][:, d, b * P:b * P + P], ident)
                mm.then_inc(kt_full, 1)

            def gla_updates(l):
                pe.wait_ge(kt_ready, l + 1)
                for d in range(2):
                    for c in range(NCH):
                        rows = slice((c % 2) * 64, (c % 2) * 64 + 64)
                        for h in range(GLA_H):
                            mm = pe.matmul(aux[h * DK:h * DK + DK, 2 * d + c % 2, (c // 2) * DV:(c // 2) * DV + DV],
                                           ktok[rows, d, c // 2, h * DK:h * DK + DK],
                                           vtok[rows, c // 2, h * DV:h * DV + DV], start=True, stop=True)
                mm.then_inc(u_full, 1)

            def gla_gram(l, n):
                pe.wait_ge(ab_ready, NGRAM * l + n + 1)
                if n == 0:
                    pe.wait_ge(states_ready, l + 1)
                else:
                    pe.wait_ge(gram_used, NGRAM * l + n)
                chunks = NCH if l < DEPTH - 1 else NX // CH
                for c in range(chunks):
                    for h in range(GLA_H):
                        rows, cols = slice(h * DK, h * DK + DK), slice(c * CH, c * CH + CH)
                        left = pair[n % 2][rows, 0, cols] if n < NGRAM - 1 else proj[rows, TGK, cols]
                        mm = pe.matmul(aux[(c % 2) * 64:(c % 2) * 64 + 64, h, (c // 2) * CH:(c // 2) * CH + CH],
                                       left, pair[n % 2][rows, 1, cols], start=True, stop=True)
                mm.then_inc(gram_full, 1)

            def gla_outputs(l):
                pe.wait_ge(gram_used, NGRAM * (l + 1))
                chunks = NCH if l < DEPTH - 1 else NX // CH
                for h in range(GLA_H):
                    for c in range(chunks):
                        o = aux[(h % 2) * DV:(h % 2) * DV + DV, 2 * (h // 2) + c % 2, (c // 2) * CH:(c // 2) * CH + CH]
                        rows, krows = slice((c % 2) * 64, (c % 2) * 64 + 64), slice(h * DK, h * DK + DK)
                        pe.matmul(o, vtok[rows, c // 2, h * DV:h * DV + DV], attg[rows, h, c // 2, :],
                                  start=True, stop=False)
                        for d in range(2):
                            mm = pe.matmul(o, state[krows, d, c, :], qdec[krows, d, c * CH:c * CH + CH],
                                           start=False, stop=d == 1)
                mm.then_inc(o_full, 1)

            def gla_norm_sum(l):
                pe.wait_ge(o_copied, l + 1)
                for t in range(2):
                    for t0, t1, b in segments(l < DEPTH - 1):
                        mm = pe.matmul(auxw[:, t, t0:t1], bones, pair[0][:, t, t0:t1], start=True, stop=True)
                mm.then_inc(o_sum, 1)

            def attention_prepare(l):
                pe.wait_ge(o_rstd, l + 1)
                for n, tile in enumerate((TK, 0, 1, 2, 3)):
                    if n == 4:
                        pe.wait_ge(rot_used, 5 * l + 1)
                    pe.matmul(aux[:, n % 4, :], rot, proj[:, tile, 0:NX], start=True, stop=True).then_inc(rot_full, 1)
                pe.wait_ge(rot_used, 5 * l + 3)
                for b in range(6):
                    mm = pe.transpose(aux[:, 1 + b // 4, (b % 4) * P:(b % 4) * P + P], proj[:, TV, b * P:b * P + P], ident)
                mm.then_inc(va_full, 1)

            def pool_mix(l):
                for t in range(2):
                    g = gate_group(l, 0, 0) + 1 + t
                    pe.wait_ge(pool_d, 2 * l + t + 1)
                    open_group(g)
                    for t0, t1, _ in segments(l < DEPTH - 1):
                        mm = pe.matmul(acc[:, g % 2, t0:t1], poolw[:, l, t * P:t * P + P], proj[:, TPOOL + t, t0:t1],
                                       start=True, stop=True)
                    mm.then_inc(mm_done, 1)

            def scores(l, u, r):
                qb, g = units(l)[u]
                n, rows = head_base[l] + 4 * u + r, slice(g * HD, g * HD + HD)
                blocks = local_blocks(qb)
                if n > head_base[l]:
                    pe.wait_ge(s_ctx, n)
                if blocks and u + r > 0:
                    pe.wait_ge(s_local, lhead_base[l] + 4 * u + r)
                lhs = proj[rows, r, qb * P:qb * P + P]
                if blocks:
                    pe.matmul(aux[:, 0, 0:P * len(blocks)], lhs, proj[rows, TK, P * blocks[0]:P * blocks[-1] + P],
                              start=True, stop=True)
                pe.matmul(aux[:, 1, 0:NC], lhs, proj[rows, TK, NX:T], start=True, stop=True).then_inc(s_full, 1)

            def turn_probs(l, u, b):
                n = block_index(l, u, b)
                if b == 0:
                    pe.wait_ge(p_ready, unit_base[l] + u + 1)
                if n > blk_base[l]:
                    pe.wait_ge(pt_ready, n)
                for r in range(4):
                    mm = pe.transpose(aux[:, 2, r * P:r * P + P], sco[u % 2][:, r, b * P:b * P + P], ident)
                mm.then_inc(pt_full, 1)

            def attend(l, u, b):
                n, g = block_index(l, u, b), units(l)[u][1]
                blocks = key_blocks(l, u)
                pe.wait_ge(pt_ready, n + 1)
                if b == 0 and unit_base[l] + u >= 2:
                    pe.wait_ge(pv_used, unit_base[l] + u - 1)
                mm = pe.matmul(aux[g * HD:g * HD + HD, 3, :], vat[:, blocks[b], g * HD:g * HD + HD], ptb[n % 2],
                               start=b == 0, stop=b == len(blocks) - 1)
                if b == len(blocks) - 1:
                    mm.then_inc(pv_full, 1)

            def gate_piece(l, j, i):
                at, ctx = PLAN.layers[l], l < DEPTH - 1
                q, b = at["gate_q"] + 2 * j, at["gate_b"] + j // 2
                if i == 0:
                    block_split(q)
                    open_group(gate_group(l, j, 0))
                    product(gate_group(l, j, 0), q, ctx, range(0, 4), last=False)
                elif i == 1:
                    product(gate_group(l, j, 0), q, ctx, range(4, 8), first=False)
                elif i == 2:
                    if j == 0:
                        pool_mix(l)
                        wait_evac(pe, gate_group(l, 0, 0) + 1)
                        wait_evac(pe, gate_group(l, 0, 0) + 2)
                    pe.wait_ge(b_landed[b % 2], 16 * (b // 2 + 1))
                    project_branch(gate_group(l, j, 1), b, j % 2, (0, 1), 4, ctx)
                    block_split(q + 1)
                    open_group(gate_group(l, j, 2))
                    product(gate_group(l, j, 2), q + 1, ctx, range(0, 4), last=False)
                elif i == 3:
                    product(gate_group(l, j, 2), q + 1, ctx, range(4, 8), first=False)
                else:
                    if j == 0:
                        pe.wait_ge(gla_out, l + 1)
                    project_branch(gate_group(l, j, 3), b, j % 2, (2, 3), 4, ctx)

            def project_branch(g, b, jj, ks, tile0, ctx):
                open_group(g)
                for n, k in enumerate(ks):
                    for t0, t1, _ in segments(ctx):
                        mm = pe.matmul(acc[:, g % 2, t0:t1], brw[:, b % 2, jj, k, :], bt[:, tile0 + k, t0:t1],
                                       start=n == 0, stop=n == len(ks) - 1)
                mm.then_inc(mm_done, 1)

            def down(l, g, q, par_, ctx, ready, i=0, per_g=0, per_q=0, per_t=0):
                pe.wait_ge(g_ready, ready + per_t * i)
                for half in range(2):
                    block_split(q + half, i, per_q)
                    s = (q + half) % SPL
                    for m in range(4):
                        gg = g + 4 * half + m
                        open_group(gg, i, per_g)
                        for kk in range(2):
                            for w_, a_ in ((whi, 0), (whi, 1), (wlo, 0)):
                                for t0, t1, _ in segments(ctx):
                                    mm = pe.matmul(acc[:, gg % 2, t0:t1], w_[:, s, kk * 512 + m * P:kk * 512 + m * P + P],
                                                   gact[:, par_, kk, a_, t0:t1], start=kk == 0 and w_ is whi and a_ == 0,
                                                   stop=kk == 1 and w_ is wlo)
                        mm.then_inc(mm_done, 1)

            def ups(l, g, q, ctx, i=0, per_g=0, per_q=0, h=None):
                for n in range(4):
                    block_split(q + n, i, per_q)
                    open_group(g + n, i, per_g)
                    product(g + n, q + n, ctx, range(KT), h=h if n == 0 else None)

            for l, at in enumerate(PLAN.layers):
                ctx = l < DEPTH - 1
                if l == 0:
                    pe.wait_ge(cond_ready, 1)
                norm_sum(4 * l)
                for n in range(len(EARLY)):
                    early_block(l, n)
                pe.wait_ge(rstd_ready, 4 * l + 1)
                steps = (gla_z, gla_values, gla_keys, gla_updates)
                for n in range(len(LATE)):
                    if n < 4:
                        steps[n](l)
                    else:
                        gla_gram(l, n - 4)
                    late_block(l, n)
                for n in range(len(LATE) - 4, NGRAM):
                    gla_gram(l, n)
                gla_outputs(l)
                gla_norm_sum(l)
                attention_prepare(l)
                us = units(l)
                pe.wait_ge(rope_done, 5 * (l + 1))
                pe.wait_ge(va_ready, l + 1)
                for u in range(len(us) + 1):
                    blocks = len(key_blocks(l, u - 1)) if u else 0
                    for i in range(6):
                        if u < len(us) and i < 4:
                            scores(l, u, i)
                        if u < KT and i < 5:
                            gate_piece(l, u, i)
                        if i < blocks:
                            turn_probs(l, u - 1, i)
                        if 0 < i <= blocks:
                            attend(l, u - 1, i - 1)
                g, q = at["mix_g"], at["mix_q"]
                for c in range(KT // 2 + 1):
                    if c < KT // 2:
                        b = at["mix_b"] + c
                        for jj in range(2):
                            block_split(q)
                            open_group(g)
                            product(g, q, ctx, range(KT))
                            if c == 0 and jj == 0:
                                pe.wait_ge(pv_used, unit_base[l + 1])
                            if jj == 0:
                                pe.wait_ge(b_landed[b % 2], 16 * (b // 2 + 1))
                            project_branch(g + 1, b, jj, range(4), 0, ctx)
                            g, q = g + 2, q + 1
                    if c > 0:
                        down(l, g, q, (c - 1) % 2, ctx, g_count(l, "mix", 2 * c))
                        g, q = g + 8, q + 2
                norm_sum(4 * l + 1)
                norm_sum(4 * l + 2)
                g, q = at["ffn_g"], at["ffn_q"]
                ups(l, g, q, ctx, h=2 * l + 1)
                g, q = g + 4, q + 4
                with pe.Fori(0, FFN_LOOPS) as i:
                    pg, pq = FFN_BODY_G, FFN_BODY_Q
                    ups(l, g, q, ctx, i, pg, pq)
                    down(l, g + 4, q + 4, 0, ctx, g_count(l, "ffn", 2), i, pg, pq, 4)
                    ups(l, g + 12, q + 6, ctx, i, pg, pq)
                    down(l, g + 16, q + 10, 1, ctx, g_count(l, "ffn", 4), i, pg, pq, 4)
                g, q = g + FFN_BODY_G * FFN_LOOPS, q + FFN_BODY_Q * FFN_LOOPS
                down(l, g, q, 0, ctx, g_count(l, "ffn", NFF))
                norm_sum(4 * l + 3)

        @block.scalar
        def _(act):
            link = Chain(act, act_link)

            def split(q, i=0, per_q=0, per_g=0):
                if q >= PLAN.blocks:
                    return
                act.wait_ge(w_landed[q % RAW], 16 * (q // RAW + 1) + 16 * (per_q // RAW) * i)
                if q >= SPL:
                    act.wait_ge(mm_done, PLAN.group_end[q - SPL] + per_g * i)
                act.activation(whi[:, q % SPL, :], raw[:, q % RAW, :], ACT.Copy).then_inc(w_hi, 1)

            def squares(k):
                w = T if norm_ctx(k) else NX
                for kt in range(KT):
                    n = KT * k + kt
                    norm_source_ready(act, k, kt)
                    if n >= 2:
                        act.wait_ge(sq_used, n - 1)
                    source = x if k % 2 == 0 else y
                    act.activation(sq[n % 2][:, 0:w], source[:, kt, 0:w], ACT.Square).then_inc(sq_ready, 1)

            def inverse_root(k):
                w = T if norm_ctx(k) else NX
                act.wait_ge(sq_used, KT * (k + 1))
                link(act.activation(rstd[:, 0:w], auxw[:, 0, 0:w], ACT.Ln, bias=eps[:, 0:1], scale=1.0 / D))
                act.activation(rstd[:, 0:w], rstd[:, 0:w], ACT.Exp, scale=-0.5).then_inc(rstd_ready, 1)

            def heads(l, n, shift, ctx):
                for kt in range(KT):
                    act.wait_ge(t_ready, KT * n + kt + 1)
                    for t0, t1, s in segments(ctx):
                        ins = act.activation(hhi[:, kt, t0:t1], tmp[kt % 2][:, t0:t1], ACT.Identity,
                                             bias=ada[:, l, shift + kt, s:s + 1])
                    ins.then_inc(h_hi, 1)

            def read_projection(l, tile, g):
                w = T if l < DEPTH - 1 or tile in WITH_CTX else NX
                act.wait_ge(mm_done, g + 1)
                act.activation(proj[:, tile, 0:w], acc[:, g % 2, 0:w], ACT.Copy,
                               scale=DK ** -0.5 if tile == TGQ else 1.0).then_inc(acc_free[g % 2], 1)

            def pair_exp(l, n):
                w = T if l < DEPTH - 1 else NX
                act.wait_ge(e_args, len(LEVELS) * l + n + 1)
                act.activation(pair[n % 2][:, :, 0:w], pair[n % 2][:, :, 0:w], ACT.Exp,
                               scale=1.0 / TAU).then_inc(e_exp, 1)

            def gla_step(l, n):
                w = T if l < DEPTH - 1 else NX
                if n == 0:
                    act.wait_ge(z_full, l + 1)
                    for d in range(2):
                        ins = act.activation(pair[0][:, d, :], auxw[:, d, 0:T], ACT.Abs,
                                             bias=par[:, l, C_BA + d:C_BA + d + 1])
                    ins.then_inc(z_used, 1)
                    act.wait_ge(z_used, 2 * l + 1)
                    link(act.activation(pair[0], pair[0], ACT.Exp, scale=-1.0))
                    act.activation(pair[0], pair[0], ACT.Ln, bias=1.0).then_inc(z_log, 1)
                elif n == 1:
                    act.wait_ge(v_full, l + 1)
                    act.activation(vtok.rearrange("p b n -> p (b n)"), aux_flat[:, 0:1536], ACT.Copy).then_inc(v_ready, 1)
                    act.wait_ge(cum_ready, l + 1)
                    act.activation(qdec[:, 0, 0:w], cumf[:, 0:w], ACT.Exp, scale=1.0 / TAU)
                    act.activation(qdec[:, 1, 0:w], cumb[:, 0:w], ACT.Exp, scale=1.0 / TAU)
                    act.activation(dec[:, 0, :], cumf[:, CH - 1::CH], ACT.Exp, scale=1.0 / TAU)
                    act.activation(dec[:, 1, :], cumb[:, 0::CH], ACT.Exp, scale=1.0 / TAU)
                    act.wait_ge(kd_args, l + 1)
                    act.activation(pair[1], pair[1], ACT.Exp, scale=1.0 / TAU).then_inc(kd_exp, 1)
                elif n == 2:
                    act.wait_ge(kt_full, l + 1)
                    act.activation(ktok.rearrange("p d b n -> p (d b n)"), aux_flat[:, 0:1536],
                                   ACT.Copy).then_inc(kt_ready, 1)
                if n >= 2:
                    pair_exp(l, n - 2)

            def gla_finish(l):
                w = T if l < DEPTH - 1 else NX
                act.wait_ge(o_full, l + 1)
                for t in range(2):
                    o = aux[:, 2 * t:2 * t + 2, 0:w // 2].rearrange("p s (c i) -> p s c i", i=CH)
                    for func, dst in ((ACT.Copy, bt[:, 6 + t, 0:w]), (ACT.Square, pair[0][:, t, 0:w])):
                        ins = act.activation(dst.rearrange("p (c s i) -> p s c i", s=2, i=CH), o, func)
                ins.then_inc(o_copied, 1)
                act.wait_ge(o_sum, l + 1)
                link(act.activation(pair[1][:, :, 0:w], auxw[:, :, 0:w], ACT.Ln, bias=eps[:, 0:1], scale=1.0 / DV))
                act.activation(pair[1][:, :, 0:w], pair[1][:, :, 0:w], ACT.Exp, scale=-0.5).then_inc(o_rstd, 1)
                act.activation(proj[:, TGR:TGR + 2, 0:w], proj[:, TGR:TGR + 2, 0:w], ACT.Silu).then_inc(r_silu, 1)

            def unit_scores(l, u, r):
                n, nl = head_base[l] + 4 * u + r, P * (len(key_blocks(l, u)) - 2)
                act.wait_ge(s_full, n + 1)
                if r == 0:
                    if u == 0:
                        act.wait_ge(gla_out, l + 1)
                    elif u == 1:
                        act.wait_ge(pool_d, 2 * (l + 1))
                    else:
                        act.wait_ge(pt_full, block_index(l, u - 1, 0))
                act.activation(sco[u % 2][:, r, nl:nl + NC], aux[:, 1, 0:NC], ACT.Copy, scale=HD ** -0.5).then_inc(s_ctx, 1)

            def unit_exp(l, u):
                b, nk = u % 2, P * len(key_blocks(l, u))
                act.wait_ge(m_ready, unit_base[l] + u + 1)
                for r in range(4):
                    act.activation(sco[b][:, r, 0:nk], sco[b][:, r, 0:nk], ACT.Exp, bias=small[:, b, 4 + r:5 + r],
                                   accum_out=small[:, b, 16 + r:17 + r])
                act.activation(small[:, b, 12:16], small[:, b, 8:12], ACT.Exp).then_inc(p_exp, 1)

            def read_gate(g, dst, before):
                act.wait_ge(mm_done, g + 1)
                if before is not None:
                    wait_evac(act, before)
                act.activation(dst, acc[:, g % 2, 0:dst.shape[-1]], ACT.Tanh, scale=0.5).then_inc(acc_free[g % 2], 1)

            def chunk_head(n, par_, jj, w, src, scale, per=0, i=0):
                act.wait_ge(g_val, n + per * i)
                act.activation(gact[:, par_, jj, 0, 0:w], src[:, 0:w], ACT.Copy, scale=scale).then_inc(g_hi, 1)

            def ups(l, c, g, q, par_, w, i=0, per_g=0, per_q=0, per_t=0):
                for n in range(4):
                    kk, dst = n // 2, (conv_a, conv_g)[n % 2][n // 2]
                    f = (2 * c + kk) + NFF * (n % 2)
                    act.wait_ge(mm_done, g + n + 1 + per_g * i)
                    if not (c == 0 and per_t == 0):
                        act.wait_ge(g_ready, g_count(l, "ffn", 2 * c - 1 + kk) + per_t * i)
                    act.activation(dst[:, 0:w], acc[:, (g + n) % 2, 0:w], ACT.Identity,
                                   bias=par[:, l, bass.ds(C_CB + f + per_t * i, 1)],
                                   scale=par[:, l, bass.ds(C_CW + 2 * NFF + f + per_t * i, 1)]).then_inc(conv_mid, 1)
                    split(q + n + SPL, i, per_q, per_g)
                    if n % 2:
                        act.wait_ge(acc_free[(g + n) % 2], (g + n) // 2 + 1 + per_g // 2 * i)
                        act.activation(conv_g[kk][:, 0:w], conv_g[kk][:, 0:w], ACT.Silu).then_inc(silu_ready, 1)
                        chunk_head(g_count(l, "ffn", 2 * c + kk + 1), par_, kk, w, conv_a[kk], 1.0, per_t, i)

            act.wait_ge(consts_in, 16 * 6)
            act.activation(cvec[:, :, :], cvec[:, :, :], ACT.Silu).then_inc(cvec_ready, 1)
            act.wait_ge(eps_set, 1)
            for l, at in enumerate(PLAN.layers):
                ctx = l < DEPTH - 1
                w = T if ctx else NX
                squares(4 * l)
                if l == 0:
                    act.wait_ge(cond_ready, 1)
                inverse_root(4 * l)
                if l == 0:
                    split(0)
                    split(1)
                heads(l, 2 * l, SH1, True)
                if l > 0:
                    act.wait_ge(x_spilled, 16 * l)
                for n, tile in enumerate(EARLY):
                    read_projection(l, tile, at["early_g"] + n)
                    split(at["early_q"] + n + SPL)
                for n, tile in enumerate(LATE):
                    gla_step(l, n)
                    read_projection(l, tile, at["late_g"] + n)
                    split(at["late_q"] + n + SPL)
                gla_finish(l)
                act.wait_ge(va_full, l + 1)
                act.activation(vat.rearrange("p b n -> p (b n)"), aux_flat[:, 512:1280], ACT.Copy).then_inc(va_ready, 1)
                us = units(l)
                for u in range(len(us) + 1):
                    for i in range(5):
                        if u < len(us) and i < 4:
                            unit_scores(l, u, i)
                        if u < KT:
                            if i == 1:
                                if u == 0:
                                    act.wait_ge(rope_done, 5 * (l + 1))
                                read_gate(gate_group(l, u, 0), gates[0][:, 0:w], gate_group(l, u - 1, 1) if u else None)
                                split(at["gate_q"] + 2 * u + SPL)
                            if i == 2 and u == 0:
                                for t in range(2):
                                    g = gate_group(l, 0, 0) + 1 + t
                                    act.wait_ge(mm_done, g + 1)
                                    act.activation(bt[:, 4 + t, 0:w], acc[:, g % 2, 0:w], ACT.Copy,
                                                   scale=par[:, l, C_PSC + t:C_PSC + t + 1]).then_inc(acc_free[g % 2], 1)
                            if i == 3:
                                read_gate(gate_group(l, u, 2), gates[1][:, 0:w], gate_group(l, u - 1, 3) if u else None)
                                split(at["gate_q"] + 2 * u + 1 + SPL)
                        if u > 0 and i < len(key_blocks(l, u - 1)):
                            n = block_index(l, u - 1, i)
                            act.wait_ge(pt_full, n + 1)
                            act.activation(ptb[n % 2], aux[:, 2, :], ACT.Copy).then_inc(pt_ready, 1)
                    if u < len(us):
                        unit_exp(l, u)
                g, q = at["mix_g"], at["mix_q"]
                for c in range(KT // 2 + 1):
                    if c < KT // 2:
                        for jj in range(2):
                            before = (g + 1 - 4 - (8 if c > 1 else 0)) if c else None
                            read_gate(g, mgate[jj][:, 0:w], before)
                            split(q + SPL)
                            chunk_head(g_count(l, "mix", 2 * c + jj + 1), c % 2, jj, w, part[:, 2 * c + jj, :], 0.5)
                            g, q = g + 2, q + 1
                    if c > 0:
                        split(q + SPL)
                        split(q + 1 + SPL)
                        g, q = g + 8, q + 2
                squares(4 * l + 1)
                inverse_root(4 * l + 1)
                squares(4 * l + 2)
                inverse_root(4 * l + 2)
                heads(l, 2 * l + 1, SH2, ctx)
                g, q = at["ffn_g"], at["ffn_q"]
                ups(l, 0, g, q, 0, w)
                g, q = g + 4, q + 4
                with act.Fori(0, FFN_LOOPS) as i:
                    pg, pq = FFN_BODY_G, FFN_BODY_Q
                    ups(l, 1, g, q, 1, w, i, pg, pq, 4)
                    split(q + 4 + SPL, i, pq, pg)
                    split(q + 5 + SPL, i, pq, pg)
                    ups(l, 2, g + 12, q + 6, 0, w, i, pg, pq, 4)
                    split(q + 10 + SPL, i, pq, pg)
                    split(q + 11 + SPL, i, pq, pg)
                q += FFN_BODY_Q * FFN_LOOPS
                split(q + SPL)
                split(q + 1 + SPL)
                squares(4 * l + 3)
                inverse_root(4 * l + 3)

        @block.vector
        def _(v):
            link = Chain(v, dve_link)

            def rest(q, i=0, per_q=0):
                if q >= PLAN.blocks:
                    return
                v.wait_ge(w_hi, q + 1 + per_q * i)
                v.tensor_tensor(wlo[:, q % SPL, :], raw[:, q % RAW, :], whi[:, q % SPL, :].bitcast(F32),
                                ALU.subtract).then_inc(w_split, 1)

            def modulate(l, n, k, post, scale, shift, ctx):
                v.wait_ge(rstd_ready, k + 1)
                for kt in range(KT + 1):
                    if kt < KT:
                        x_valid(v, l, post, kt)
                        if kt >= 2:
                            v.wait_ge(h_ready, KT * n + kt - 1)
                        for t0, t1, s in segments(ctx):
                            ins = v.scalar_tensor_tensor(tmp[kt % 2][:, t0:t1], x[:, kt, t0:t1],
                                                         ada[:, l, scale + kt, s:s + 1], rstd[:, t0:t1], ALU.mult, ALU.mult)
                        ins.then_inc(t_ready, 1)
                    if kt > 0:
                        j = kt - 1
                        v.wait_ge(h_hi, KT * n + j + 1)
                        for t0, t1, s in segments(ctx):
                            ins = v.scalar_tensor_tensor(hlo[:, j, t0:t1], tmp[j % 2][:, t0:t1],
                                                         ada[:, l, shift + j, s:s + 1], hhi[:, j, t0:t1].bitcast(F32),
                                                         ALU.add, ALU.subtract)
                        ins.then_inc(h_ready, 1)

            def residual(l, k, gate, ctx):
                v.wait_ge(rstd_ready, k + 1)
                if k % 4 == 1:
                    v.wait_ge(x_in, 16 * (l + 2))
                for kt in range(KT):
                    if kt >= 2:
                        v.wait_ge(x_ready, KT * (k // 2) + kt - 1)
                    for t0, t1, s in segments(ctx):
                        ins = v.scalar_tensor_tensor(tmp[kt % 2][:, t0:t1], y[:, kt, t0:t1],
                                                     ada[:, l, gate + kt, s:s + 1], rstd[:, t0:t1], ALU.mult, ALU.mult)
                    link(ins)
                    w = T if ctx else NX
                    v.tensor_tensor(x[:, kt, 0:w], x[:, kt, 0:w], tmp[kt % 2][:, 0:w], ALU.add).then_inc(x_ready, 1)

            def halves(ap, width, half, w):
                a = ap[:, 0:w].rearrange("p (n s i) -> p n s i", s=2, i=half)
                return a[:, :, 0, :], a[:, :, 1, :]

            def pair_args(l, n):
                half, w = LEVELS[n], T if l < DEPTH - 1 else NX
                fl, fr = halves(cumf, T, half, w)
                bl, br = halves(cumb, T, half, w)
                al, ar = halves(pair[n % 2][:, 0, :], T, half, w)
                ql, qr = halves(pair[n % 2][:, 1, :], T, half, w)
                shape = list(fl.shape)
                edge_f = fl[:, :, half - 1:half].broadcast_to(shape)
                edge_b = br[:, :, 0:1].broadcast_to(shape)
                v.tensor_tensor(al, edge_f, fl, ALU.subtract)
                v.tensor_tensor(ar, edge_b, br, ALU.subtract)
                v.tensor_tensor(qr, fr, edge_f, ALU.subtract)
                v.tensor_tensor(ql, bl, edge_b, ALU.subtract).then_inc(e_args, 1)

            def pair_scale(l, n):
                w = T if l < DEPTH - 1 else NX
                v.wait_ge(e_exp, len(LEVELS) * l + n + 1)
                v.tensor_tensor(pair[n % 2][:, 0, 0:w], pair[n % 2][:, 0, 0:w], proj[:, TGK, 0:w], ALU.mult)
                v.tensor_tensor(pair[n % 2][:, 1, 0:w], pair[n % 2][:, 1, 0:w], proj[:, TGQ, 0:w],
                                ALU.mult).then_inc(ab_ready, 1)

            def take_level(l, n):
                cc = NCH // 2 if l < DEPTH - 1 else NX // CH // 2
                v.wait_ge(gram_full, NGRAM * l + n + 1)
                if n:
                    v.wait_ge(gram_used, NGRAM * l + n)
                mask = gmask[:, n, :].rearrange("p (a b i) -> p a b i", a=1, b=1).broadcast_to([P, GLA_H, cc, CH])
                v.copy_predicated(attg[:, :, 0:cc, :], mask,
                                  aux[:, :, 0:cc * CH].rearrange("p h (c i) -> p h c i", i=CH)).then_inc(gram_used, 1)

            def gla_step(l, n):
                w = T if l < DEPTH - 1 else NX
                if n == 0:
                    v.wait_ge(z_used, 2 * l + 1)
                    for d in range(2):
                        ins = v.tensor_scalar(pair[1][:, d, :], auxw[:, d, 0:T], par[:, l, C_BA + d:C_BA + d + 1], 0.0,
                                              ALU.add, ALU.min)
                    ins.then_inc(z_used, 1)
                    v.wait_ge(z_used, 2 * (l + 1))
                    v.wait_ge(z_log, l + 1)
                    link(v.tensor_tensor(pair[0], pair[1], pair[0], ALU.subtract))
                    v.wait_ge(scanm_in, 16 * (l + 1))
                    v.tensor_tensor_scan(cumf, scanm, pair[0][:, 0, :], 0.0, ALU.mult, ALU.add)
                    v.tensor_tensor_scan(cumb[:, ::-1], scanm, pair[0][:, 1, ::-1], 0.0, ALU.mult,
                                         ALU.add).then_inc(cum_ready, 1)
                elif n == 1:
                    v.wait_ge(cum_ready, l + 1)
                    cf, cb = (a.rearrange("p (c i) -> p c i", i=CH) for a in (cumf, cumb))
                    kf, kb = (pair[1][:, d, :].rearrange("p (c i) -> p c i", i=CH) for d in range(2))
                    v.tensor_tensor(kf, cf[:, :, CH - 1:CH].broadcast_to([P, NCH, CH]), cf, ALU.subtract)
                    v.tensor_tensor(kb, cb[:, :, 0:1].broadcast_to([P, NCH, CH]), cb, ALU.subtract).then_inc(kd_args, 1)
                    v.wait_ge(kd_exp, l + 1)
                    v.tensor_tensor(pair[1][:, 0, :], pair[1][:, 0, :], proj[:, TGK, :], ALU.mult)
                    v.tensor_tensor(pair[1][:, 1, :], pair[1][:, 1, :], proj[:, TGK, :], ALU.mult).then_inc(kd_ready, 1)
                    for d in range(2):
                        v.tensor_tensor(qdec[:, d, 0:w], qdec[:, d, 0:w], proj[:, TGQ, 0:w], ALU.mult)
                elif n == 3:
                    orders = ([8, 9, 10, 11] + list(range(8)), [11, 10, 9, 8] + list(range(7, -1, -1)))
                    for order, d in zip(orders, range(2)):
                        ins = v.memset(state[:, d, order[0], :], 0.0)
                    link(ins)
                    v.wait_ge(u_full, l + 1)
                    for m in range(NCH - 1):
                        for d in range(2):
                            a, b = orders[d][m], orders[d][m + 1]
                            ins = v.scalar_tensor_tensor(state[:, d, b, :], state[:, d, a, :], dec[:, d, a:a + 1],
                                                         aux[:, 2 * d + a % 2, (a // 2) * DV:(a // 2) * DV + DV],
                                                         ALU.mult, ALU.add)
                        if m < NCH - 2:
                            link(ins)
                    ins.then_inc(states_ready, 1)
                if n >= 4:
                    take_level(l, n - 4)
                if n >= 2:
                    if n == 3:
                        v.wait_ge(kt_full, l + 1)
                    pair_args(l, n - 2)
                    pair_scale(l, n - 2)

            def gla_finish(l):
                w = T if l < DEPTH - 1 else NX
                take_level(l, 4)
                v.tensor_scalar(pair[0][:, 1, 0:w], proj[:, TGQ, 0:w], 2.0, None, ALU.mult).then_inc(ab_ready, 1)
                take_level(l, 5)
                take_level(l, 6)
                v.wait_ge(o_rstd, l + 1)
                link(v.tensor_tensor(bt[:, 6:8, 0:w], bt[:, 6:8, 0:w], pair[1][:, :, 0:w], ALU.mult))
                v.wait_ge(r_silu, l + 1)
                for t in range(2):
                    ins = v.scalar_tensor_tensor(bt[:, 6 + t, 0:w], bt[:, 6 + t, 0:w], par[:, l, C_GN + t:C_GN + t + 1],
                                                 proj[:, TGR + t, 0:w], ALU.mult, ALU.mult)
                ins.then_inc(gla_out, 1)

            def rope(l):
                v.wait_ge(tables_in, 48 * (l + 1))
                for n, tile in enumerate((TK, 0, 1, 2, 3)):
                    v.wait_ge(rot_full, 5 * l + n + 1)
                    if n > 0:
                        v.wait_ge(rope_done, 5 * l + n)
                    v.tensor_tensor(gtmp[:, 0:NX], aux[:, n % 4, :], ropes, ALU.mult).then_inc(rot_used, 1)
                    link(v.tensor_tensor(proj[:, tile, 0:NX], proj[:, tile, 0:NX], ropec, ALU.mult))
                    v.wait_ge(rot_used, 5 * l + n + 1)
                    v.tensor_tensor(proj[:, tile, 0:NX], proj[:, tile, 0:NX], gtmp[:, 0:NX], ALU.add).then_inc(rope_done, 1)

            def unit_scores(l, u, r):
                qb, _ = units(l)[u]
                nl = P * len(local_blocks(qb))
                if nl:
                    n = head_base[l] + 4 * u + r
                    v.wait_ge(s_full, n + 1)
                    if r == 0 and u == 1:
                        v.wait_ge(pool_d, 2 * (l + 1))
                    elif r == 0 and u > 1:
                        v.wait_ge(pt_full, block_index(l, u - 1, 0))
                    m0 = 0 if qb > 0 else P
                    v.scalar_tensor_tensor(sco[u % 2][:, r, 0:nl], aux[:, 0, 0:nl], HD ** -0.5, amask[:, m0:m0 + nl],
                                           ALU.mult, ALU.add).then_inc(s_local, 1)

            def unit_max(l, u):
                b, nk, (qb, g) = u % 2, P * len(key_blocks(l, u)), units(l)[u]
                v.wait_ge(s_ctx, head_base[l] + 4 * (u + 1))
                if qb < 4:
                    v.wait_ge(s_local, lhead_base[l] + 4 * (u + 1))
                sink = par[:, l, C_SINK + 4 * g:C_SINK + 4 * g + 4]
                link(v.tensor_reduce(small[:, b, 0:4], sco[b][:, :, 0:nk], AX_X, ALU.max))
                link(v.tensor_tensor(small[:, b, 0:4], small[:, b, 0:4], sink, ALU.max))
                v.tensor_scalar(small[:, b, 4:8], small[:, b, 0:4], -1.0, None, ALU.mult)
                v.tensor_tensor(small[:, b, 8:12], sink, small[:, b, 0:4], ALU.subtract).then_inc(m_ready, 1)

            def unit_inverse(l, u):
                b = u % 2
                v.wait_ge(p_exp, unit_base[l] + u + 1)
                link(v.tensor_tensor(small[:, b, 16:20], small[:, b, 16:20], small[:, b, 12:16], ALU.add))
                if unit_base[l] + u >= 2:
                    v.wait_ge(p_ready, unit_base[l] + u - 1)
                v.reciprocal(small[:, b, 20:24], small[:, b, 16:20]).then_inc(r_ready, 1)

            def unit_output(l, u):
                qb, g = units(l)[u]
                rows = slice(g * HD, g * HD + HD)
                v.wait_ge(pv_full, unit_base[l] + u + 1)
                if u == 0:
                    v.wait_ge(pool_d, 2 * (l + 1))
                v.tensor_copy(bt[rows, 0:NQT, qb * P:qb * P + P],
                              aux[rows, 3, :].rearrange("p (r q) -> p r q", r=4)).then_inc(pv_used, 1)

            def gated(g, gate_g, gate, dst, w):
                v.wait_ge(mm_done, g + 1)
                wait_evac(v, gate_g)
                v.scalar_tensor_tensor(dst[:, 0:w], gate[:, 0:w], 1.0, acc[:, g % 2, 0:w], ALU.add,
                                       ALU.mult).then_inc(acc_free[g % 2], 1)
                wait_evac(v, g)

            def chunk_rest(n, par_, jj, w, src, scale, per=0, i=0):
                v.wait_ge(g_hi, n + per * i)
                v.scalar_tensor_tensor(gact[:, par_, jj, 1, 0:w], src[:, 0:w], scale,
                                       gact[:, par_, jj, 0, 0:w].bitcast(F32), ALU.mult, ALU.subtract).then_inc(g_ready, 1)

            def add_down(g, q, w, i=0, per_g=0, per_q=0):
                for m in range(KT):
                    gg = g + m
                    v.wait_ge(mm_done, gg + 1 + per_g * i)
                    v.tensor_tensor(y[:, m, 0:w], y[:, m, 0:w], acc[:, gg % 2, 0:w], ALU.add).then_inc(acc_free[gg % 2], 1)
                    if m % 4 == 3:
                        rest(q + m // 4 + SPL, i, per_q)

            def ups(l, c, g, q, par_, w, i=0, per_g=0, per_q=0, per_t=0):
                ctx = w == T
                for n in range(4):
                    kk, dst = n // 2, (conv_a, conv_g)[n % 2][n // 2]
                    f = (2 * c + kk) + NFF * (n % 2)
                    b = (g + n) % 2
                    v.wait_ge(conv_mid, 2 * NFF * l + 4 * c + n + 1 + 2 * per_t * i)
                    for tap, d0, d1, s0, s1 in ((0, 1, 0, 0, 1), (2, 0, 1, 1, 0)):
                        wt = par[:, l, bass.ds(C_CW + 2 * NFF * tap + f + per_t * i, 1)]
                        for t0, t1, _ in segments(ctx):
                            ins = v.scalar_tensor_tensor(dst[:, t0 + d0:t1 - d1], acc[:, b, t0 + s0:t1 - s1], wt,
                                                         dst[:, t0 + d0:t1 - d1], ALU.mult, ALU.add)
                        if tap == 0:
                            link(ins)
                    ins.then_inc(acc_free[b], 1)
                    rest(q + n + SPL, i, per_q)
                    if n % 2:
                        t = g_count(l, "ffn", 2 * c + kk + 1)
                        v.wait_ge(silu_ready, NFF * l + 2 * c + kk + 1 + per_t * i)
                        v.tensor_tensor(conv_a[kk][:, 0:w], conv_a[kk][:, 0:w], conv_g[kk][:, 0:w],
                                        ALU.mult).then_inc(g_val, 1)
                        v.wait_ge(g_val, t + per_t * i)
                        chunk_rest(t, par_, kk, w, conv_a[kk], 1.0, per_t, i)

            v.memset(eps[:, :], EPS).then_inc(eps_set, 1)
            v.wait_ge(consts_in, 16 * 6)
            v.wait_ge(ada_used, DEPTH * 48)
            link(v.tensor_tensor(ada[:, :, :, :], aux[:, 0, 0:DEPTH * 96].rearrange("p (l n s) -> p l n s", l=DEPTH, s=2),
                                 par[:, :, C_BADA:C_BADA + 48].unsqueeze(3).broadcast_to([P, DEPTH, 48, 2]), ALU.add))
            for l in range(DEPTH):
                for row, gain, bias in ((SC1, C_GPRE, 1.0), (G1, C_GPOST, 0.0), (SC2, C_GPRE2, 1.0), (G2, C_GPOST2, 0.0)):
                    a = ada[:, l, row:row + KT, :]
                    ins = v.scalar_tensor_tensor(a, a, bias, par[:, l, gain:gain + KT].unsqueeze(2).broadcast_to([P, KT, 2]),
                                                 ALU.add, ALU.mult)
            ins.then_inc(cond_ready, 1)
            v.wait_ge(cond_ready, 1)
            for l, at in enumerate(PLAN.layers):
                ctx = l < DEPTH - 1
                w = T if ctx else NX
                if l == 0:
                    rest(0)
                    rest(1)
                modulate(l, 2 * l, 4 * l, 2 * l, SC1, SH1, True)
                for n in range(len(EARLY)):
                    rest(at["early_q"] + n + SPL)
                for n in range(len(LATE)):
                    gla_step(l, n)
                    rest(at["late_q"] + n + SPL)
                gla_finish(l)
                rope(l)
                us = units(l)
                for u in range(len(us) + 1):
                    for i in range(5):
                        if u < len(us) and i < 4:
                            unit_scores(l, u, i)
                        if i == 0 and u > 0:
                            unit_inverse(l, u - 1)
                        if u < KT:
                            q = at["gate_q"] + 2 * u
                            if i == 1:
                                rest(q + SPL)
                            if i == 2:
                                gated(gate_group(l, u, 1), gate_group(l, u, 0), gates[0], part[:, u, :], w)
                            if i == 3:
                                rest(q + 1 + SPL)
                            if i == 4:
                                gated(gate_group(l, u, 3), gate_group(l, u, 2), gates[1], gtmp, w)
                                link(v.tensor_tensor(part[:, u, 0:w], part[:, u, 0:w], gtmp[:, 0:w], ALU.add))
                    if u > 0:
                        unit_output(l, u - 1)
                    if u < len(us):
                        unit_max(l, u)
                g, q = at["mix_g"], at["mix_q"]
                for c in range(KT // 2 + 1):
                    if c < KT // 2:
                        for jj in range(2):
                            rest(q + SPL)
                            gated(g + 1, g, mgate[jj], mtmp, w)
                            j, t = 2 * c + jj, g_count(l, "mix", 2 * c + jj + 1)
                            v.tensor_tensor(part[:, j, 0:w], part[:, j, 0:w], mtmp[:, 0:w], ALU.add).then_inc(g_val, 1)
                            v.wait_ge(g_val, t)
                            chunk_rest(t, c % 2, jj, w, part[:, j, :], 0.5)
                            g, q = g + 2, q + 1
                    if c > 0:
                        v.wait_ge(y_zero, 2 * l + 1)
                        if c > 1:
                            wait_evac(v, g - 4 - 1 if c < KT // 2 else g - 1)
                        add_down(g, q, w)
                        g, q = g + 8, q + 2
                residual(l, 4 * l + 1, G1, ctx)
                modulate(l, 2 * l + 1, 4 * l + 2, 2 * l + 1, SC2, SH2, ctx)
                v.wait_ge(y_zero, 2 * l + 2)
                g, q = at["ffn_g"], at["ffn_q"]
                ups(l, 0, g, q, 0, w)
                g, q = g + 4, q + 4
                with v.Fori(0, FFN_LOOPS) as i:
                    pg, pq = FFN_BODY_G, FFN_BODY_Q
                    link.enter(i, 8)
                    ups(l, 1, g, q, 1, w, i, pg, pq, 4)
                    add_down(g + 4, q + 4, w, i, pg, pq)
                    ups(l, 2, g + 12, q + 6, 0, w, i, pg, pq, 4)
                    add_down(g + 16, q + 10, w, i, pg, pq)
                    link.leave(FFN_LOOPS)
                g, q = g + FFN_BODY_G * FFN_LOOPS, q + FFN_BODY_Q * FFN_LOOPS
                add_down(g, q, w)
                residual(l, 4 * l + 3, G2, ctx)

        @block.gpsimd
        def _(pool):
            link = Chain(pool, pool_link)

            def pooling(l):
                ctx = l < DEPTH - 1
                segs = [(8, 0, NX)] + ([(NX + 24, NX, NC)] if ctx else [])
                n = segs[-1][0] + segs[-1][2] + 8
                pool.wait_ge(tables_in, 48 * (l + 1))
                pool.wait_ge(gla_out, l + 1)
                for t in range(2):
                    u = proj[:, TPOOL + t, :]
                    wait_evac(pool, PLAN.layers[l]["late_g"] + LATE.index(TPOOL + t))
                    link(pool.memset(up[:, 0:n], 0.0))
                    for p0, t0, m in segs:
                        ins = pool.tensor_scalar(up[:, p0:p0 + m], u[:, t0:t0 + m], 1.0, None, ALU.mult)
                    link(ins)
                    link(pool.tensor_tensor(pa[:, 1:n], up[:, 0:n - 1], up[:, 1:n], ALU.add))
                    if t == 0:
                        pool.tensor_tensor(pb[64:128, 2:n - 1], pa[64:128, 1:n - 2], pa[64:128, 3:n], ALU.add)
                        link(pool.tensor_scalar(pb[0:64, 8:n - 8], pa[0:64, 8:n - 8], 1.0, None, ALU.mult))
                    else:
                        link(pool.tensor_tensor(pb[:, 2:n - 1], pa[:, 1:n - 2], pa[:, 3:n], ALU.add))
                        link(pool.tensor_tensor(pa[:, 4:n - 4], pb[:, 2:n - 6], pb[:, 6:n - 2], ALU.add))
                        pool.tensor_scalar(pb[0:64, 8:n - 8], pa[0:64, 8:n - 8], 1.0, None, ALU.mult)
                        link(pool.tensor_tensor(pb[64:128, 8:n - 8], pa[64:128, 4:n - 12], pa[64:128, 12:n - 4], ALU.add))
                    for p0, t0, m in segs:
                        ins = pool.tensor_tensor(pb[:, p0:p0 + m], pb[:, p0:p0 + m], inv[:, t, t0:t0 + m], ALU.mult)
                    link(ins)
                    for p0, t0, m in segs:
                        ins = pool.tensor_tensor(u[:, t0:t0 + m], pb[:, p0:p0 + m], u[:, t0:t0 + m], ALU.subtract)
                    ins.then_inc(pool_d, 1)
                    pool.wait_ge(pool_d, 2 * l + t + 1)

            for l in range(DEPTH):
                pooling(l)
                for u in range(len(units(l))):
                    b, nk = u % 2, P * len(key_blocks(l, u))
                    pool.wait_ge(r_ready, unit_base[l] + u + 1)
                    for r in range(4):
                        ins = pool.tensor_scalar(sco[b][:, r, 0:nk], sco[b][:, r, 0:nk], small[:, b, 20 + r:21 + r], None,
                                                 ALU.mult)
                    ins.then_inc(p_ready, 1)
                pool.wait_ge(pv_used, unit_base[l + 1])
                pool.memset(y[:, :, :], 0.0).then_inc(y_zero, 1)
                pool.wait_ge(x_ready, KT * (2 * l + 1))
                pool.memset(y[:, :, :], 0.0).then_inc(y_zero, 1)


def _tiles(a):
    return np.ascontiguousarray(a.reshape(-1, P, a.shape[-1]).transpose(1, 0, 2))


def _rows(a):
    return a.reshape(-1, P).T


def _block(w, cols):
    return w[:, cols].reshape(KT, P, P).transpose(1, 0, 2).reshape(P, BLK)


def _chunk(w, c, half):
    return w[2 * c * P:2 * (c + 1) * P, half * 512:half * 512 + 512].reshape(2, P, 512).transpose(1, 0, 2).reshape(P, BLK)


def _weight_stream(w_in, w_o, w_up, w_down):
    at = dict(q=0, k=512, v=640, pool=768, gq=1024, gk=1152, gv=1280, gr=1536, lr=1792, mg=1824)
    run = lambda o: np.arange(o, o + P)
    heads = lambda t: np.concatenate([np.arange(t * HD, t * HD + HD), np.arange((t + 4) * HD, (t + 5) * HD)])
    cols = {TK: run(at["k"]), TV: run(at["v"]), TGQ: run(at["gq"]), TGK: run(at["gk"])}
    cols.update({t: heads(t) for t in range(NQT)})
    for t in range(2):
        cols[TPOOL + t], cols[TGV + t], cols[TGR + t] = run(at["pool"] + t * P), run(at["gv"] + t * P), run(at["gr"] + t * P)
    out = []
    for l in range(DEPTH):
        lr = np.concatenate([w_in[l][:, at["lr"]:at["mg"]], np.zeros((D, P - 32), w_in.dtype)], axis=1)
        for tile in EARLY + LATE:
            out.append(_block(lr, run(0)) if tile == TLR else _block(w_in[l], cols[tile]))
        gate = lambda b, j: _block(w_in[l], run(at["mg"] + b * D + j * P))
        for j in range(KT):
            out += [gate(1, j), gate(2, j)]
        for c in range(KT // 2 + 1):
            if c < KT // 2:
                out += [gate(0, 2 * c), gate(0, 2 * c + 1)]
            if c > 0:
                out += [_chunk(w_o[l], c - 1, 0), _chunk(w_o[l], c - 1, 1)]
        for c in range(NFF // 2 + 1):
            if c < NFF // 2:
                for j in (2 * c, 2 * c + 1):
                    out += [_block(w_up[l], run(j * P)), _block(w_up[l], run((NFF + j) * P))]
            if c > 0:
                out += [_chunk(w_down[l], c - 1, 0), _chunk(w_down[l], c - 1, 1)]
    return np.stack(out)


def _branch_stream(w_att, w_pool, w_gla):
    out = []
    for l in range(DEPTH):
        both = np.concatenate([w_pool[l], w_gla[l]], axis=0)
        order = np.concatenate([np.arange(h * HD, h * HD + HD) for t in range(NQT) for h in (t, t + 4)])
        for w in (both, w_att[l][order]):
            w = w.reshape(4, P, KT, P)
            for b in range(KT // 2):
                out.append(w[:, :, 2 * b:2 * b + 2, :].transpose(1, 2, 0, 3))
    return np.ascontiguousarray(np.stack(out))


def _parameters(i):
    f = i["b_ada"].dtype
    par = np.zeros((P, DEPTH, NPAR), f)
    for l in range(DEPTH):
        for c, v in ((C_BADA, i["b_ada"][l]), (C_GPRE, i["g_pre_mix"][l]), (C_GPOST, i["g_post_mix"][l]),
                     (C_GPRE2, i["g_pre_ffn"][l]), (C_GPOST2, i["g_post_ffn"][l]), (C_PSC, i["pool_scale"][l]),
                     (C_BA, i["gla_ba"][l].reshape(-1)), (C_GN, i["gla_norm"][l].reshape(-1)),
                     (C_CW, i["conv_w"][l].reshape(-1)), (C_CB, i["conv_b"][l])):
            r = _rows(v)
            par[:, l, c:c + r.shape[1]] = r
        par[:, l, C_SINK:C_SINK + 8] = i["att_sink"][l][None, :]
    return par


def _small_weights(gla_wa2, pool_w):
    wa2 = np.zeros((32, DEPTH, 256), gla_wa2.dtype)
    poolw = np.zeros((P, DEPTH, 256), pool_w.dtype)
    for l in range(DEPTH):
        for d in range(2):
            wa2[16 * d:16 * d + 16, l, P * d:P * d + P] = gla_wa2[l, d]
        for g in range(4):
            r = 64 * (g % 2)
            poolw[r:r + 64, l, (g // 2) * P + r:(g // 2) * P + r + 64] = pool_w[l, g]
    return wa2, poolw


def _constants():
    con = np.zeros((P, NCON), np.float32)
    p = np.arange(P)
    con[:, K_ONES:K_ONES + P] = 1.0
    con[:, K_BONES:K_BONES + P] = p[:, None] // 64 == p[None, :] // 64
    half = HD // 2
    for m in range(P):
        if m % HD < half:
            con[m + half, K_ROT + m] = -1.0
        else:
            con[m - half, K_ROT + m] = 1.0
    con[:, K_ID:K_ID + P] = np.eye(P)
    scanm = np.broadcast_to((np.arange(T) % CH != 0).astype(np.float32), (P, T)).copy()
    gm = np.zeros((P, NGRAM, CH), np.int32)
    a, b = (p % CH)[:, None], np.arange(CH)[None, :]
    for n, half_ in enumerate(LEVELS):
        gm[:, n, :] = (a // (2 * half_) == b // (2 * half_)) & (a // half_ != b // half_)
    gm[:, NGRAM - 1, :] = a == b
    am = np.zeros((P, 3 * P), np.float32)
    am[:, 0:P] = np.where(p[None, :] >= p[:, None], 0.0, NEG)
    am[:, 2 * P:] = np.where(p[None, :] <= p[:, None], 0.0, NEG)
    n = HD // 4
    base = (10000.0 ** (-np.arange(n) / n)).astype(np.float32)
    tok = np.arange(NX)
    ang = np.concatenate([(tok // GRID_W).astype(np.float32)[:, None] * base,
                          (tok % GRID_W).astype(np.float32)[:, None] * base], axis=-1).T
    rope = np.concatenate([np.tile(np.cos(ang), (4, 1)), np.tile(np.sin(ang), (4, 1))], axis=1).astype(np.float32)
    inv = np.zeros((P, 2, T), np.float32)
    for g, w in enumerate((2, 4, 8, 16)):
        for t0, m in ((0, NX), (NX, NC)):
            t = np.arange(m)
            cnt = np.clip(t + w - w // 2, 0, m) - np.clip(t - w // 2, 0, m)
            inv[64 * (g % 2):64 * (g % 2) + 64, g // 2, t0:t0 + m] = (1.0 / cnt).astype(np.float32)
    return con, scanm, gm, am, rope, inv


def kernel(**inputs):
    import concourse.bacc as bacc
    from concourse.bass_utils import run_bass_kernel_spmd

    i = {k: np.asarray(v) for k, v in inputs.items()}
    x_t = _tiles(np.concatenate([i["x"][0].T, i["ctx"][0].T], axis=1))
    c_t = np.ascontiguousarray(np.stack([_rows(i["c"][0]), _rows(i["c_ctx"])], axis=2))
    ada = np.stack([_block(i["w_ada"][l], np.arange(n * P, n * P + P)) for l in range(DEPTH) for n in range(48)])
    wa2, poolw = _small_weights(i["gla_wa2"], i["pool_w"])
    con, scanm, gm, am, rope, inv = _constants()
    arrays = {
        "x_t": x_t, "c_t": c_t, "par_d": _parameters(i), "con_d": con, "ada_d": ada,
        "wst_d": _weight_stream(i["w_in"], i["w_o"], i["w_up"], i["w_down"]),
        "brw_d": _branch_stream(i["w_br_att"], i["w_br_pool"], i["w_br_gla"]),
        "wa2_d": wa2, "poolw_d": poolw, "scanm_d": scanm, "gmask_d": gm, "amask_d": am, "rope_d": rope, "inv_d": inv,
    }
    nc = bacc.Bacc("TRN2", target_bir_lowering=False, num_devices=1)
    aps = {n: nc.dram_tensor(n, a.shape, mybir.dt.from_np(a.dtype), kind="ExternalInput").ap() for n, a in arrays.items()}
    out = nc.dram_tensor("out", (P, KT, NX), F32, kind="ExternalOutput").ap()
    build(nc, out=out, **aps)
    r = run_bass_kernel_spmd(nc, [arrays], core_ids=[0])
    return np.ascontiguousarray(r.results[0]["out"].transpose(1, 0, 2).reshape(D, NX).T)[None]
```

```python
from contextlib import ExitStack

import numpy as np

import concourse.bass as bass
from concourse import mybir

ALU = mybir.AluOpType
ACT = mybir.ActivationFunctionType
F32 = mybir.dt.float32
F32R = mybir.dt.float32r
I32 = mybir.dt.int32
AX_X = mybir.AxisListType.X

P = 128
DEPTH = 2
D = 1024
KT = D // P
NX, NC = 512, 256
T = NX + NC
EPS = 1e-6
GRID_W = 64
HD = 64
NQT = 4
GLA_H, DK, DV, CH = 4, 32, 64, 64
NCH = T // CH
TAU = 16.0
NFF = 2816 // P
BLK = 1024
RAW, SPL = 4, 2
NEG = -3.0e38
UNITS = 6 * D // 512
FIRST_UNITS = 4
EDGE = 8
LEVELS = (32, 16, 8, 4, 2, 1)
NGRAM = 1 + len(LEVELS)

TQ, TK, TV, TPOOL, TGQ, TGK, TGV, TGR, TLR = 0, 4, 5, 6, 8, 9, 10, 12, 14
NPROJ = 15
ORDER = (TLR, TGV, TGV + 1, TGK, TGQ, TGR, TGR + 1, TPOOL, TPOOL + 1, TK, TV, 0, 1, 2, 3)
WITH_CTX = (TLR, TGK, TGV, TGV + 1, TK, TV)
STEP_Z, STEP_V, STEP_KD, STEP_KEYS, STEP_STATE, STEP_GRAM = 2, 4, 5, 6, 7, 8
(C_BADA, C_GPRE, C_GPOST, C_GPRE2, C_GPOST2, C_PSC, C_BA, C_GN, C_CW, C_CB, C_SINK, NPAR) = np.cumsum(
    [0, 48, 8, 8, 8, 8, 2, 2, 2, 3 * 2 * NFF, 2 * NFF, 8]).tolist()
K_ONES, K_BONES, K_ROT, K_ID, K_SEL, K_EDGE, NCON = 0, 128, 256, 384, 512, 514, 514 + 4 * EDGE
SH1, SC1, G1, SH2, SC2, G2 = range(0, 48, 8)


class Plan:

    def __init__(self):
        self.group_end = []
        self.branch_end = []
        self.quad = []
        self.turn = []
        self.layers = []
        self.g = 0

        def block(groups=1):
            self.g += groups
            self.group_end.append(self.g)

        for _ in range(FIRST_UNITS):
            self.add_quad(), self.add_quad(), self.add_turn()
        for l in range(DEPTH):
            at = {"q": len(self.group_end), "proj_g": []}
            for n in range(len(ORDER) + 1):
                if l == 0:
                    if n >= 2 and n % 2 == 0:
                        self.add_turn()
                    self.add_quad()
                if n < len(ORDER):
                    at["proj_g"].append(self.g)
                    block()
            if l == 0:
                self.add_turn()
            at["gate_q"], at["gate_g"], at["gate_b"] = len(self.group_end), self.g, len(self.branch_end)
            self.g += 2
            for j in range(KT):
                block()
                block(2)
                self.g += 1
                if j % 2:
                    self.branch_end.append(self.g)
            at["mix_q"], at["mix_g"], at["mix_b"] = len(self.group_end), self.g, len(self.branch_end)
            for c in range(KT // 2 + 1):
                if c < KT // 2:
                    block()
                    block(2)
                    self.g += 1
                    self.branch_end.append(self.g)
                if c > 0:
                    block(4)
                    block(4)
            at["ffn_q"], at["ffn_g"] = len(self.group_end), self.g
            for c in range(NFF // 2 + 1):
                if c < NFF // 2:
                    for n in range(4):
                        block()
                        if l == 0 and n in (0, 2):
                            self.add_quad()
                    if l == 0:
                        self.add_turn()
                if c > 0:
                    block(4)
                    block(4)
            at["down_g"] = self.g - KT
            if l == 0:
                self.add_quad(), self.add_quad(), self.add_turn()
            at["end_g"] = self.g
            self.layers.append(at)
        self.blocks = len(self.group_end)
        self.branches = len(self.branch_end)
        assert len(self.turn) == DEPTH * UNITS and len(self.quad) == 2 * len(self.turn)

    def add_quad(self):
        self.quad.append(self.g)
        self.g += 1

    def add_turn(self):
        self.turn.append(self.g)
        self.g += 1


PLAN = Plan()
FFN_BODY_Q, FFN_LOOPS = 12, (NFF // 2 - 1) // 2
LATE_QUAD = 2 * FIRST_UNITS
FFN_QUAD = LATE_QUAD + len(ORDER) + 1
UP_GROUPS = {True: (0, 2, 3, 5), False: (0, 1, 2, 3)}
UP_COUNT = {True: 7, False: 4}


def late_turns(n):
    return FIRST_UNITS + n // 2 - 1 if n >= 2 and n % 2 == 0 else None


def pieces(l, units_, u, i):
    lo, hi, n = 2, 5 * KT, 5 * units_
    step = 5 * u + i
    a, b = (lo + (hi - lo) * step // n, lo + (hi - lo) * (step + 1) // n)
    return [divmod(k, 5) for k in range(a, b)]


POOL_WINDOWS = ((2, 4), (8, 16))


class Chain:

    def __init__(self, eng, sem):
        self.eng, self.sem, self.n, self.shift = eng, sem, 0, 0

    def __call__(self, ins):
        ins.then_inc(self.sem, 1)
        self.n += 1
        self.eng.wait_ge(self.sem, self.n + self.shift)

    def enter(self, reg, per):
        self.start, self.per, self.shift = self.n, per, reg * per

    def leave(self, loops):
        assert self.n - self.start == self.per, (self.n - self.start, self.per)
        self.n, self.shift = self.start + self.per * loops, 0


def segments(ctx):
    return [(0, NX, 0), (NX, T, 1)] if ctx else [(0, NX, 0)]


def build(nc, x_t, c_t, par_d, con_d, ada_d, wst_d, brw_d, wa2_d, poolw_d, scanm_d, gmask_d, amask_d, rope_d, out):
    spill = nc.dram_tensor("x_spill", (P, KT * T), F32).ap()
    with ExitStack() as es:
        def sem(name):
            return es.enter_context(nc.semaphore(name))

        def sb(name, shape, dt=F32, stack=es):
            return stack.enter_context(nc.sbuf_tensor(name, shape, dt))

        hhi = sb("hhi", [P, KT, T], F32R)
        hlo = sb("hlo", [P, KT, T], F32R)
        whi = sb("whi", [P, SPL, BLK], F32R)
        wlo = sb("wlo", [P, SPL, BLK], F32R)
        raw = sb("raw", [P, RAW, BLK])
        brw = sb("brw", [P, 2, 2, 4, P])
        par = sb("par", [P, DEPTH, NPAR])
        con = sb("con", [P, NCON])
        cvec = sb("cvec", [P, KT, 32])
        ada = sb("ada", [P, DEPTH, 48, 2])
        wa2 = sb("wa2", [32, 256])
        poolw = sb("poolw", [P, 256])
        gmask = sb("gmask", [P, NGRAM, CH], I32)
        small = sb("small", [P, 2, 24])
        eps = sb("eps", [P, 1])
        dec = sb("dec", [P, 2, NCH])
        bt = sb("bt", [P, KT, T])
        y = sb("y", [P, KT, T])
        over = ExitStack()
        gact = sb("gact", [P, 2, 2, 2, T], F32R, over)
        over.close()
        ext = sb("ext", [P, 3840])
        proj = sb("proj", [P, NPROJ, T])
        x = proj[:, TPOOL + 1:NPROJ, :]
        part = x

        ones, bones = con[:, K_ONES:K_ONES + P], con[:, K_BONES:K_BONES + P]
        rot, ident = con[:, K_ROT:K_ROT + P], con[:, K_ID:K_ID + P]

        sq = [bt[:, 0, :], bt[:, 1, :]]
        rstd = bt[:, 2, :]
        tmp = [bt[:, 3, :], bt[:, 4, :]]
        conv_a = [bt[:, 3, :], bt[:, 4, :]]
        conv_g = [bt[:, 5, :], bt[:, 6, :]]
        first_w = [y[:, :, :].rearrange("p a b -> p (a b)")[:, n * 2048:n * 2048 + 2048] for n in range(3)]
        later_w = brw[:, :, :, :, :].rearrange("p s t k n -> p (s t k n)")
        row_first = [bt[:, 5, 0:512], bt[:, 6, 0:512]]
        row_early = [bt[:, 0, 0:512], bt[:, 7, 256:768]]
        row_late = [ext[:, 3072:3584], bt[:, 7, 256:768]]
        row_ffn = [bt[:, 7, 0:512], bt[:, 0, 0:512]]
        ffn_w = [later_w, proj[:, 3:6, :].rearrange("p a b -> p (a b)")[:, 0:2048]]
        cumf, cumb = y[:, 0, :], y[:, 1, :]
        pair = [y[:, 2:4, :], y[:, 4:6, :]]
        qdec = y[:, 6:8, :]
        vtok = ext[:, 0:6 * 256].rearrange("p (b n) -> p b n", b=6)
        ktok = ext[:, 1536:3072].rearrange("p (d b n) -> p d b n", d=2, b=6)
        scanm = ext[:, 3072:3072 + T]
        attg = bt[:, 0:2, :].rearrange("p a b -> p (a b)").rearrange("p (h c i) -> p h c i", h=GLA_H, c=6)
        state = bt[:, 2:4, :].rearrange("p d (c e) -> p d c e", c=NCH)
        yf = y[:, :, :].rearrange("p a b -> p (a b)")
        sco = [yf[:, 0:2560].rearrange("p (r k) -> p r k", r=4), yf[:, 2560:5120].rearrange("p (r k) -> p r k", r=4)]
        vat = yf[:, 5120:5120 + 768].rearrange("p (b n) -> p b n", b=6)
        ptb = [ext[:, 0:512], ext[:, 512:1024]]
        gates = [ext[:, 1024:1024 + T], ext[:, 1792:1792 + T]]
        gtmp = ext[:, 2560:2560 + T]
        amask = ext[:, 3328:3328 + 3 * P]
        ropec, ropes = ext[:, 0:512], ext[:, 512:1024]
        up, pa, pb = (bt[:, 4:8, :].rearrange("p a b -> p (a b)")[:, i * 800:i * 800 + 800] for i in range(3))
        mgate = [proj[:, 3, :], proj[:, 4, :]]
        mtmp = proj[:, 5, :]

        acc = es.enter_context(nc.psum_tensor("acc", [P, 2, 1024], F32))
        aux = es.enter_context(nc.psum_tensor("aux", [P, 4, 512], F32))
        auxw = aux[:, :, :].rearrange("p (t b) n -> p t (b n)", b=2)

        aux_flat = aux[:, :, :].rearrange("p b n -> p (b n)")

        consts_in = sem("consts_in")
        x_in = sem("x_in")
        x_spilled = sem("x_spilled")
        tables_in = sem("tables_in")
        scanm_in = sem("scanm_in")
        out_done = sem("out_done")
        w_landed = [sem(f"w_landed{i}") for i in range(RAW)]
        b_landed = [sem(f"b_landed{i}") for i in range(2)]
        ada_landed = [sem(f"ada_landed{i}") for i in range(5)]
        cond_ready = sem("cond_ready")
        small_in = sem("small_in")
        cvec_ready = sem("cvec_ready")
        w_hi = sem("w_hi")
        w_split = sem("w_split")
        mm_done = sem("mm_done")
        acc_free = [sem("acc_free0"), sem("acc_free1")]
        sq_ready = sem("sq_ready")
        sq_used = sem("sq_used")
        rstd_ready = sem("rstd_ready")
        t_ready = sem("t_ready")
        h_hi = sem("h_hi")
        h_ready = sem("h_ready")
        x_ready = sem("x_ready")
        y_zero = sem("y_zero")
        z_full, z_used, z_log = sem("z_full"), sem("z_used"), sem("z_log")
        cum_ready = sem("cum_ready")
        v_full, v_ready = sem("v_full"), sem("v_ready")
        kd_args, kd_exp, kd_ready = sem("kd_args"), sem("kd_exp"), sem("kd_ready")
        kt_full, kt_ready = sem("kt_full"), sem("kt_ready")
        u_full, states_ready = sem("u_full"), sem("states_ready")
        e_args, e_exp, ab_ready = sem("e_args"), sem("e_exp"), sem("ab_ready")
        gram_full, gram_used = sem("gram_full"), sem("gram_used")
        o_full, o_copied, o_sum, o_rstd, gla_out = (sem(n) for n in ("o_full", "o_copied", "o_sum", "o_rstd", "gla_out"))
        pool_d = sem("pool_d")
        rot_full, rot_used, rope_done = sem("rot_full"), sem("rot_used"), sem("rope_done")
        va_full, va_ready = sem("va_full"), sem("va_ready")
        s_full, s_local, s_ctx = sem("s_full"), sem("s_local"), sem("s_ctx")
        m_ready, p_exp, p_ready = sem("m_ready"), sem("p_exp"), sem("p_ready")
        pt_full, pt_ready = sem("pt_full"), sem("pt_ready")
        pv_full, pv_used = sem("pv_full"), sem("pv_used")
        r_silu = sem("r_silu")
        conv_mid = sem("conv_mid")
        g_val, g_hi, g_ready = sem("g_val"), sem("g_hi"), sem("g_ready")
        silu_ready = sem("silu_ready")
        eps_set = sem("eps_set")
        dve_link, act_link, pool_link = sem("dve_link"), sem("act_link"), sem("pool_link")

        def units(l):
            return [(qb, g) for qb in range(4 if l == DEPTH - 1 else 6) for g in range(2)]

        def local_blocks(qb):
            return list(range(max(qb - 1, 0), min(qb + 2, 4))) if qb < 4 else []

        unit_base, head_base, lhead_base, blk_base = [0], [0], [0], [0]
        for l in range(DEPTH):
            us = units(l)
            unit_base.append(unit_base[-1] + len(us))
            head_base.append(head_base[-1] + 4 * len(us))
            lhead_base.append(lhead_base[-1] + 4 * sum(qb < 4 for qb, _ in us))
            blk_base.append(blk_base[-1] + sum(len(local_blocks(qb)) + 2 for qb, _ in us))

        def gate_group(l, j, n):
            return PLAN.layers[l]["gate_g"] + 2 + 4 * j + n

        def quad_place(a):
            if a < LATE_QUAD:
                return a % 3, a // 3
            if a < FFN_QUAD:
                return 3, a - LATE_QUAD
            return (3, FFN_QUAD - LATE_QUAD + (a - FFN_QUAD) // 2) if a % 2 == 0 else (4, (a - FFN_QUAD) // 2)

        def quad_weights(a):
            return first_w[a % 3] if a < LATE_QUAD else later_w if a < FFN_QUAD else ffn_w[a % 2]

        def late_rows(m):
            return row_early if m < FIRST_UNITS + 4 else row_late

        def proj_group(l, tile):
            return PLAN.layers[l]["proj_g"][ORDER.index(tile)]

        def key_blocks(l, u):
            return local_blocks(units(l)[u][0]) + [4, 5]

        def block_index(l, u, b):
            return blk_base[l] + sum(len(key_blocks(l, v)) for v in range(u)) + b

        def g_count(l, part_, tiles):
            return l * (KT + NFF) + (KT if part_ == "ffn" else 0) + tiles

        def wait_evac(eng, g):
            eng.wait_ge(acc_free[g % 2], g // 2 + 1)

        def x_valid(eng, l, post, kt):
            if post == 0:
                eng.wait_ge(x_in, 16)
            else:
                eng.wait_ge(x_ready, KT * (post - 1) + kt + 1)

        def norm_ctx(k):
            return k % 4 == 0 or k // 4 < DEPTH - 1

        def norm_source_ready(eng, k, kt):
            l, part_ = divmod(k, 4)
            if part_ in (0, 2):
                x_valid(eng, l, 2 * l + part_ // 2, kt)
            else:
                wait_evac(eng, (PLAN.layers[l]["ffn_g"] - KT if part_ == 1 else PLAN.layers[l]["down_g"]) + kt)

        block = es.enter_context(nc.Block())

        @block.sync
        def _(sp):
            for dst, src in ((cvec[:, :, :], c_t), (con[:, :], con_d), (par[:, :, :], par_d), (gmask[:, :, :], gmask_d)):
                sp.dma_start(dst, src).then_inc(consts_in, 16)
            sp.dma_start(x, x_t).then_inc(x_in, 16)

            def weights(q, i=0, per=0):
                if q >= RAW:
                    sp.wait_ge(w_split, q - RAW + 1 + per * i)
                sp.dma_start(raw[:, q % RAW, :], wst_d[q + per * i]).then_inc(w_landed[q % RAW], 16)

            def branch(b):
                if b >= 2:
                    sp.wait_ge(mm_done, PLAN.branch_end[b - 2])
                sp.dma_start(brw[:, b % 2, :, :, :], brw_d[b]).then_inc(b_landed[b % 2], 16)

            def quad(a, i=0, per_g=0):
                before = a - 3 if a < LATE_QUAD else a - 1 if a < FFN_QUAD else a - 2
                if a >= FFN_QUAD + 2 or LATE_QUAD < a < FFN_QUAD or 3 <= a < LATE_QUAD:
                    sp.wait_ge(mm_done, PLAN.quad[before] + 1 + per_g * i)
                sp.dma_start(quad_weights(a), ada_d[a + 4 * i if per_g else a]).then_inc(ada_landed[quad_place(a)[0]], 16)

            for a in range(LATE_QUAD):
                quad(a)
            for l, at in enumerate(PLAN.layers):
                for q in range(at["q"], at["q"] + RAW):
                    weights(q)
                if l == 0:
                    quad(LATE_QUAD)
                if l > 0:
                    for kt in range(KT):
                        x_valid(sp, l, 2 * l, kt)
                    sp.dma_start(spill, x).then_inc(x_spilled, 16)
                    sp.wait_ge(mm_done, PLAN.layers[l - 1]["end_g"])
                sp.dma_start(scanm, scanm_d).then_inc(scanm_in, 16)
                sp.dma_start(wa2[:, :], wa2_d[l]).then_inc(small_in, 16)
                sp.dma_start(poolw[:, :], poolw_d[l]).then_inc(small_in, 16)
                for n in range(1, len(ORDER) + 1):
                    if at["q"] + RAW - 1 + n < at["gate_q"]:
                        weights(at["q"] + RAW - 1 + n)
                    if l == 0:
                        quad(LATE_QUAD + n)
                weights(at["gate_q"])
                weights(at["gate_q"] + 1)
                if l == 0:
                    sp.wait_ge(mm_done, PLAN.quad[FFN_QUAD - 1] + 1)
                branch(at["gate_b"])
                sp.wait_ge(o_full, l + 1)
                if l == 0:
                    sp.wait_ge(mm_done, PLAN.turn[FIRST_UNITS + 7] + 1)
                sp.dma_start(ext[:, 0:1024], rope_d).then_inc(tables_in, 16)
                sp.dma_start(amask, amask_d).then_inc(tables_in, 16)
                for n, q in enumerate(range(at["gate_q"] + 2, at["mix_q"])):
                    if n % 4 == 0 and 0 < n // 4 + 1 < 4:
                        branch(at["gate_b"] + n // 4 + 1)
                    weights(q)
                for q in range(at["mix_q"], at["ffn_q"]):
                    n = q - at["mix_q"]
                    if n in (0, 2, 4, 6):
                        branch(at["mix_b"] + n // 2)
                    weights(q)
                sp.wait_ge(g_ready, g_count(l, "mix", KT))
                if l == 0:
                    sp.dma_start(x, x_t).then_inc(x_in, 16)
                else:
                    sp.wait_ge(x_spilled, 16 * l)
                    sp.dma_start(x, spill).then_inc(x_in, 16)
                q0, a0 = at["ffn_q"], FFN_QUAD
                body_g = 2 * (UP_COUNT[l == 0] + KT)
                for q in range(q0, q0 + 4):
                    weights(q)
                if l == 0:
                    sp.wait_ge(mm_done, PLAN.branch_end[at["mix_b"] + KT // 2 - 1])
                    quad(a0)
                    quad(a0 + 1)
                with sp.Fori(0, FFN_LOOPS) as i:
                    for p in range(FFN_BODY_Q):
                        weights(q0 + 4 + p, i, FFN_BODY_Q)
                        if l == 0 and p in (2, 4, 6, 8):
                            quad(a0 + 1 + p // 2, i, body_g)
                end = PLAN.layers[l + 1]["q"] if l + 1 < DEPTH else PLAN.blocks
                for q in range(q0 + 4 + FFN_BODY_Q * FFN_LOOPS, end):
                    weights(q)
                if l == 0:
                    quad(a0 + 2 + 4 * FFN_LOOPS)
                    quad(a0 + 3 + 4 * FFN_LOOPS)
            for kt in range(KT):
                x_valid(sp, DEPTH, 2 * DEPTH, kt)
                sp.dma_start(out[:, kt, :], x[:, kt, 0:NX]).then_inc(out_done, 16)
            sp.wait_ge(out_done, 16 * KT)

        @block.tensor
        def _(pe):
            def product(g, q, ctx, ks, i=0, per_g=0, first=True, last=True, h=None):
                s = q % SPL
                for k in ks:
                    if h is not None:
                        pe.wait_ge(h_ready, KT * h + k + 1)
                    for w_, a_ in ((whi, hhi), (whi, hlo), (wlo, hhi)):
                        start = first and k == ks[0] and w_ is whi and a_ is hhi
                        stop = last and k == ks[-1] and w_ is wlo
                        for t0, t1, _ in segments(ctx):
                            mm = pe.matmul(acc[:, g % 2, t0:t1], w_[:, s, k * P:k * P + P], a_[:, k, t0:t1],
                                           start=start, stop=stop)
                if last:
                    mm.then_inc(mm_done, 1)

            def open_group(g, i=0, per=0):
                if g >= 2:
                    pe.wait_ge(acc_free[g % 2], g // 2 + (per // 2) * i)

            def block_split(q, i=0, per=0):
                pe.wait_ge(w_split, q + 1 + per * i)

            def norm_tile(k, kt):
                n = KT * k + kt
                if kt == 0 and k > 0:
                    pe.wait_ge(rstd_ready, k)
                pe.wait_ge(sq_ready, n + 1)
                for t0, t1, b in segments(norm_ctx(k)):
                    mm = pe.matmul(aux[:, b, 0:t1 - t0], ones, sq[n % 2][:, t0:t1], start=kt == 0, stop=kt == KT - 1)
                mm.then_inc(sq_used, 1)

            def quad(a, i=0, per_g=0):
                g, w_, (place, load) = PLAN.quad[a], quad_weights(a), quad_place(a)
                pe.wait_ge(ada_landed[place], 16 * (load + 1) + (32 * i if per_g else 0))
                open_group(g, i, per_g)
                for j in range(4):
                    mm = pe.matmul(acc[32 * j:32 * j + 32, g % 2, 0:512], cvec[:, 4 * (a % 2) + j, :],
                                   w_[:, 512 * j:512 * j + 512], start=True, stop=True)
                mm.then_inc(mm_done, 1)

            def turn(m, rows, i=0, per_g=0):
                g = PLAN.turn[m]
                for a in (2 * m, 2 * m + 1):
                    pe.wait_ge(acc_free[PLAN.quad[a] % 2], PLAN.quad[a] // 2 + 1 + per_g // 2 * i)
                open_group(g, i, per_g)
                for t in range(4):
                    for h in range(2):
                        mm = pe.matmul(acc[:, g % 2, 2 * t:2 * t + 2], rows[h][:, t * P:t * P + P],
                                       con[:, K_SEL:K_SEL + 2], start=h == 0, stop=h == 1)
                mm.then_inc(mm_done, 1)

            def project(l, n):
                at = PLAN.layers[l]
                g, q = at["proj_g"][n], at["q"] + n
                block_split(q)
                open_group(g)
                product(g, q, l < DEPTH - 1 or ORDER[n] in WITH_CTX, range(KT), h=2 * l if n == 0 else None)

            def gla_z(l):
                wait_evac(pe, proj_group(l, TLR))
                pe.wait_ge(small_in, 32 * (l + 1))
                pe.wait_ge(rstd_ready, 4 * l + 1)
                for d in range(2):
                    for t0, t1, b in segments(True):
                        mm = pe.matmul(aux[:, 2 * d + b, 0:t1 - t0], wa2[:, d * P:d * P + P],
                                       proj[0:32, TLR, t0:t1], start=True, stop=True)
                mm.then_inc(z_full, 1)

            def gla_values(l):
                for t in range(2):
                    wait_evac(pe, proj_group(l, TGV + t))
                pe.wait_ge(z_used, 2 * (l + 1))
                for b in range(6):
                    for t in range(2):
                        mm = pe.transpose(aux[:, b // 2, (b % 2) * 256 + t * P:(b % 2) * 256 + t * P + P],
                                          proj[:, TGV + t, b * P:b * P + P], ident)
                mm.then_inc(v_full, 1)

            def gla_keys(l):
                pe.wait_ge(kd_ready, l + 1)
                pe.wait_ge(v_ready, l + 1)
                for d in range(2):
                    for b in range(6):
                        n = 6 * d + b
                        mm = pe.transpose(aux[:, n // 4, (n % 4) * P:(n % 4) * P + P],
                                          pair[1][:, d, b * P:b * P + P], ident)
                mm.then_inc(kt_full, 1)

            def gla_updates(l):
                pe.wait_ge(kt_ready, l + 1)
                for d in range(2):
                    for c in range(NCH):
                        rows = slice((c % 2) * 64, (c % 2) * 64 + 64)
                        for h in range(GLA_H):
                            mm = pe.matmul(aux[h * DK:h * DK + DK, 2 * d + c % 2, (c // 2) * DV:(c // 2) * DV + DV],
                                           ktok[rows, d, c // 2, h * DK:h * DK + DK],
                                           vtok[rows, c // 2, h * DV:h * DV + DV], start=True, stop=True)
                mm.then_inc(u_full, 1)

            def gla_gram(l, n):
                pe.wait_ge(ab_ready, NGRAM * l + n + 1)
                if n == 0:
                    pe.wait_ge(states_ready, l + 1)
                else:
                    pe.wait_ge(gram_used, NGRAM * l + n)
                chunks = NCH if l < DEPTH - 1 else NX // CH
                for c in range(chunks):
                    for h in range(GLA_H):
                        rows, cols = slice(h * DK, h * DK + DK), slice(c * CH, c * CH + CH)
                        left = pair[n % 2][rows, 0, cols] if n else proj[rows, TGK, cols]
                        mm = pe.matmul(aux[(c % 2) * 64:(c % 2) * 64 + 64, h, (c // 2) * CH:(c // 2) * CH + CH],
                                       left, pair[n % 2][rows, 1, cols], start=True, stop=True)
                mm.then_inc(gram_full, 1)

            def gla_outputs(l):
                pe.wait_ge(gram_used, NGRAM * (l + 1))
                chunks = NCH if l < DEPTH - 1 else NX // CH
                for h in range(GLA_H):
                    for c in range(chunks):
                        o = aux[(h % 2) * DV:(h % 2) * DV + DV, 2 * (h // 2) + c % 2, (c // 2) * CH:(c // 2) * CH + CH]
                        rows, krows = slice((c % 2) * 64, (c % 2) * 64 + 64), slice(h * DK, h * DK + DK)
                        pe.matmul(o, vtok[rows, c // 2, h * DV:h * DV + DV], attg[rows, h, c // 2, :],
                                  start=True, stop=False)
                        for d in range(2):
                            mm = pe.matmul(o, state[krows, d, c, :], qdec[krows, d, c * CH:c * CH + CH],
                                           start=False, stop=d == 1)
                mm.then_inc(o_full, 1)

            def gla_norm_sum(l):
                pe.wait_ge(o_copied, l + 1)
                for t in range(2):
                    for t0, t1, b in segments(l < DEPTH - 1):
                        mm = pe.matmul(auxw[:, t, t0:t1], bones, pair[0][:, t, t0:t1], start=True, stop=True)
                mm.then_inc(o_sum, 1)

            def attention_prepare(l):
                pe.wait_ge(o_rstd, l + 1)
                for n, tile in enumerate((TK, 0, 1, 2, 3)):
                    if n == 4:
                        pe.wait_ge(rot_used, 5 * l + 1)
                    pe.matmul(aux[:, n % 4, :], rot, proj[:, tile, 0:NX], start=True, stop=True).then_inc(rot_full, 1)
                pe.wait_ge(rot_used, 5 * l + 3)
                for b in range(6):
                    mm = pe.transpose(aux[:, 1 + b // 4, (b % 4) * P:(b % 4) * P + P], proj[:, TV, b * P:b * P + P], ident)
                mm.then_inc(va_full, 1)

            def pool_mix(l):
                for t in range(2):
                    g = PLAN.layers[l]["gate_g"] + t
                    pe.wait_ge(pool_d, 2 * l + t + 1)
                    open_group(g)
                    for t0, t1, _ in segments(l < DEPTH - 1):
                        mm = pe.matmul(acc[:, g % 2, t0:t1], poolw[:, t * P:t * P + P], proj[:, TPOOL + t, t0:t1],
                                       start=True, stop=True)
                    mm.then_inc(mm_done, 1)

            def scores(l, u, r):
                qb, g = units(l)[u]
                n, rows = head_base[l] + 4 * u + r, slice(g * HD, g * HD + HD)
                blocks = local_blocks(qb)
                if n > head_base[l]:
                    pe.wait_ge(s_ctx, n)
                if blocks and u + r > 0:
                    pe.wait_ge(s_local, lhead_base[l] + 4 * u + r)
                lhs = proj[rows, r, qb * P:qb * P + P]
                if blocks:
                    pe.matmul(aux[:, 0, 0:P * len(blocks)], lhs, proj[rows, TK, P * blocks[0]:P * blocks[-1] + P],
                              start=True, stop=True)
                pe.matmul(aux[:, 1, 0:NC], lhs, proj[rows, TK, NX:T], start=True, stop=True).then_inc(s_full, 1)

            def turn_probs(l, u, b):
                n = block_index(l, u, b)
                if b == 0:
                    pe.wait_ge(p_ready, unit_base[l] + u + 1)
                if n > blk_base[l]:
                    pe.wait_ge(pt_ready, n)
                for r in range(4):
                    mm = pe.transpose(aux[:, 2, r * P:r * P + P], sco[u % 2][:, r, b * P:b * P + P], ident)
                mm.then_inc(pt_full, 1)

            def attend(l, u, b):
                n, g = block_index(l, u, b), units(l)[u][1]
                blocks = key_blocks(l, u)
                pe.wait_ge(pt_ready, n + 1)
                if b == 0 and unit_base[l] + u >= 2:
                    pe.wait_ge(pv_used, unit_base[l] + u - 1)
                mm = pe.matmul(aux[g * HD:g * HD + HD, 3, :], vat[:, blocks[b], g * HD:g * HD + HD], ptb[n % 2],
                               start=b == 0, stop=b == len(blocks) - 1)
                if b == len(blocks) - 1:
                    mm.then_inc(pv_full, 1)

            def gate_piece(l, j, i):
                at, ctx = PLAN.layers[l], l < DEPTH - 1
                q, b = at["gate_q"] + 2 * j, at["gate_b"] + j // 2
                if i == 0:
                    block_split(q)
                    open_group(gate_group(l, j, 0))
                    product(gate_group(l, j, 0), q, ctx, range(0, 4), last=False)
                elif i == 1:
                    product(gate_group(l, j, 0), q, ctx, range(4, 8), first=False)
                elif i == 2:
                    if j == 0:
                        wait_evac(pe, at["gate_g"])
                        wait_evac(pe, at["gate_g"] + 1)
                    pe.wait_ge(b_landed[b % 2], 16 * (b // 2 + 1))
                    project_branch(gate_group(l, j, 1), b, j % 2, (0, 1), 4, ctx)
                    block_split(q + 1)
                    open_group(gate_group(l, j, 2))
                    product(gate_group(l, j, 2), q + 1, ctx, range(0, 4), last=False)
                elif i == 3:
                    product(gate_group(l, j, 2), q + 1, ctx, range(4, 8), first=False)
                else:
                    if j == 0:
                        pe.wait_ge(gla_out, l + 1)
                    project_branch(gate_group(l, j, 3), b, j % 2, (2, 3), 4, ctx)

            def project_branch(g, b, jj, ks, tile0, ctx):
                open_group(g)
                for n, k in enumerate(ks):
                    for t0, t1, _ in segments(ctx):
                        mm = pe.matmul(acc[:, g % 2, t0:t1], brw[:, b % 2, jj, k, :], bt[:, tile0 + k, t0:t1],
                                       start=n == 0, stop=n == len(ks) - 1)
                mm.then_inc(mm_done, 1)

            def down(l, g, q, par_, ctx, ready, i=0, per_g=0, per_q=0, per_t=0, norm=None):
                pe.wait_ge(g_ready, ready + per_t * i)
                for m in range(KT):
                    half = m // 4
                    if m % 4 == 0:
                        block_split(q + half, i, per_q)
                    s = (q + half) % SPL
                    gg = g + m
                    open_group(gg, i, per_g)
                    for kk in range(2):
                        for w_, a_ in ((whi, 0), (whi, 1), (wlo, 0)):
                            for t0, t1, _ in segments(ctx):
                                c0 = kk * 512 + (m % 4) * P
                                mm = pe.matmul(acc[:, gg % 2, t0:t1], w_[:, s, c0:c0 + P],
                                               gact[:, par_, kk, a_, t0:t1], start=kk == 0 and w_ is whi and a_ == 0,
                                               stop=kk == 1 and w_ is wlo)
                    mm.then_inc(mm_done, 1)
                    if norm is not None and m >= 2:
                        norm_tile(norm, m - 2)
                if norm is not None:
                    norm_tile(norm, KT - 2)
                    norm_tile(norm, KT - 1)

            def ups(l, g, q, ctx, i=0, per_g=0, per_q=0, h=None, unit=None):
                for n in range(4):
                    block_split(q + n, i, per_q)
                    gg = g + UP_GROUPS[unit is not None][n]
                    open_group(gg, i, per_g)
                    product(gg, q + n, ctx, range(KT), h=h if n == 0 else None)
                    if unit is not None and n in (0, 2):
                        quad(2 * unit + n // 2, i, per_g)
                if unit is not None:
                    turn(unit, row_ffn, i, per_g)

            pe.wait_ge(cvec_ready, 1)
            for kt in range(KT):
                norm_tile(0, kt)
            for m in range(FIRST_UNITS):
                quad(2 * m)
                quad(2 * m + 1)
                turn(m, row_first)
            for l, at in enumerate(PLAN.layers):
                ctx = l < DEPTH - 1
                for n in range(len(ORDER) + 1):
                    if l == 0:
                        if late_turns(n) is not None:
                            turn(late_turns(n), late_rows(late_turns(n)))
                        quad(LATE_QUAD + n)
                    if n == STEP_Z:
                        gla_z(l)
                    elif n == STEP_V:
                        gla_values(l)
                    elif n == STEP_KEYS:
                        gla_keys(l)
                    elif n == STEP_STATE:
                        gla_updates(l)
                    elif n >= STEP_GRAM and n - STEP_GRAM < NGRAM:
                        gla_gram(l, n - STEP_GRAM)
                    if n < len(ORDER):
                        project(l, n)
                if l == 0:
                    turn(FIRST_UNITS + 7, row_late)
                pool_mix(l)
                gla_outputs(l)
                gate_piece(l, 0, 0)
                gla_norm_sum(l)
                gate_piece(l, 0, 1)
                attention_prepare(l)
                us = units(l)
                pe.wait_ge(rope_done, 5 * (l + 1))
                pe.wait_ge(va_ready, l + 1)
                for u in range(len(us) + 1):
                    blocks = len(key_blocks(l, u - 1)) if u else 0
                    for i in range(7):
                        if u < len(us) and i < 4:
                            scores(l, u, i)
                        if u < len(us) and i < 5:
                            for j, f in pieces(l, len(us), u, i):
                                gate_piece(l, j, f)
                        if 0 < i <= blocks:
                            turn_probs(l, u - 1, i - 1)
                        if 1 < i <= blocks + 1:
                            attend(l, u - 1, i - 2)
                g, q = at["mix_g"], at["mix_q"]
                for c in range(KT // 2 + 1):
                    if c < KT // 2:
                        b = at["mix_b"] + c
                        for jj in range(2):
                            block_split(q)
                            open_group(g)
                            product(g, q, ctx, range(KT))
                            if c == 0 and jj == 0:
                                pe.wait_ge(pv_used, unit_base[l + 1])
                            if jj == 0:
                                pe.wait_ge(b_landed[b % 2], 16 * (b // 2 + 1))
                            project_branch(g + 1, b, jj, range(4), 0, ctx)
                            g, q = g + 2, q + 1
                    if c > 0:
                        down(l, g, q, (c - 1) % 2, ctx, g_count(l, "mix", 2 * c),
                             norm=4 * l + 1 if c == KT // 2 else None)
                        g, q = g + 8, q + 2
                for kt in range(KT):
                    norm_tile(4 * l + 2, kt)
                g, q, up_n = at["ffn_g"], at["ffn_q"], UP_COUNT[l == 0]
                pg, pq, unit = 2 * (up_n + KT), FFN_BODY_Q, UNITS if l == 0 else None
                ups(l, g, q, ctx, h=2 * l + 1, unit=unit)
                g, q = g + up_n, q + 4
                with pe.Fori(0, FFN_LOOPS) as i:
                    ups(l, g, q, ctx, i, pg, pq, unit=unit and unit + 1)
                    down(l, g + up_n, q + 4, 0, ctx, g_count(l, "ffn", 2), i, pg, pq, 4)
                    ups(l, g + up_n + KT, q + 6, ctx, i, pg, pq, unit=unit and unit + 2)
                    down(l, g + 2 * up_n + KT, q + 10, 1, ctx, g_count(l, "ffn", 4), i, pg, pq, 4)
                g, q = g + pg * FFN_LOOPS, q + pq * FFN_LOOPS
                down(l, g, q, 0, ctx, g_count(l, "ffn", NFF), norm=4 * l + 3)
                if l == 0:
                    quad(4 * UNITS - 2)
                    quad(4 * UNITS - 1)
                    turn(2 * UNITS - 1, row_ffn)
                if l + 1 < DEPTH:
                    for kt in range(KT):
                        norm_tile(4 * l + 4, kt)

        @block.scalar
        def _(act):
            link = Chain(act, act_link)

            def split(q, i=0, per_q=0, per_g=0):
                if q >= PLAN.blocks:
                    return
                act.wait_ge(w_landed[q % RAW], 16 * (q // RAW + 1) + 16 * (per_q // RAW) * i)
                if q >= SPL:
                    act.wait_ge(mm_done, PLAN.group_end[q - SPL] + per_g * i)
                act.activation(whi[:, q % SPL, :], raw[:, q % RAW, :], ACT.Copy).then_inc(w_hi, 1)

            def squares(k):
                w = T if norm_ctx(k) else NX
                for kt in range(KT):
                    n = KT * k + kt
                    norm_source_ready(act, k, kt)
                    if n >= 2:
                        act.wait_ge(sq_used, n - 1)
                    source = x if k % 2 == 0 else y
                    act.activation(sq[n % 2][:, 0:w], source[:, kt, 0:w], ACT.Square).then_inc(sq_ready, 1)

            def inverse_root(k):
                w = T if norm_ctx(k) else NX
                act.wait_ge(sq_used, KT * (k + 1))
                link(act.activation(rstd[:, 0:w], auxw[:, 0, 0:w], ACT.Ln, bias=eps[:, 0:1], scale=1.0 / D))
                act.activation(rstd[:, 0:w], rstd[:, 0:w], ACT.Exp, scale=-0.5).then_inc(rstd_ready, 1)

            def heads(l, n, shift, ctx):
                for kt in range(KT):
                    act.wait_ge(t_ready, KT * n + kt + 1)
                    for t0, t1, s in segments(ctx):
                        ins = act.activation(hhi[:, kt, t0:t1], tmp[kt % 2][:, t0:t1], ACT.Identity,
                                             bias=ada[:, l, shift + kt, s:s + 1])
                    ins.then_inc(h_hi, 1)

            def read_projection(l, tile, g):
                w = T if l < DEPTH - 1 or tile in WITH_CTX else NX
                act.wait_ge(mm_done, g + 1)
                act.activation(proj[:, tile, 0:w], acc[:, g % 2, 0:w], ACT.Copy,
                               scale=DK ** -0.5 if tile == TGQ else 1.0).then_inc(acc_free[g % 2], 1)

            def pair_exp(l, n):
                w = T if l < DEPTH - 1 else NX
                act.wait_ge(e_args, len(LEVELS) * l + n)
                act.activation(pair[n % 2][:, :, 0:w], pair[n % 2][:, :, 0:w], ACT.Exp,
                               scale=1.0 / TAU).then_inc(e_exp, 1)

            def gla_step(l, n):
                w = T if l < DEPTH - 1 else NX
                if n == STEP_Z:
                    act.wait_ge(z_full, l + 1)
                    for d in range(2):
                        ins = act.activation(pair[0][:, d, :], auxw[:, d, 0:T], ACT.Abs,
                                             bias=par[:, l, C_BA + d:C_BA + d + 1])
                    ins.then_inc(z_used, 1)
                    act.wait_ge(z_used, 2 * l + 1)
                    link(act.activation(pair[0], pair[0], ACT.Exp, scale=-1.0))
                    act.activation(pair[0], pair[0], ACT.Ln, bias=1.0).then_inc(z_log, 1)
                elif n == STEP_V:
                    act.wait_ge(v_full, l + 1)
                    act.activation(vtok.rearrange("p b n -> p (b n)"), aux_flat[:, 0:1536], ACT.Copy).then_inc(v_ready, 1)
                    act.wait_ge(cum_ready, l + 1)
                    act.activation(qdec[:, 0, 0:w], cumf[:, 0:w], ACT.Exp, scale=1.0 / TAU)
                    act.activation(qdec[:, 1, 0:w], cumb[:, 0:w], ACT.Exp, scale=1.0 / TAU)
                    act.activation(dec[:, 0, :], cumf[:, CH - 1::CH], ACT.Exp, scale=1.0 / TAU)
                    act.activation(dec[:, 1, :], cumb[:, 0::CH], ACT.Exp, scale=1.0 / TAU)
                elif n == STEP_KD:
                    act.wait_ge(kd_args, l + 1)
                    act.activation(pair[1], pair[1], ACT.Exp, scale=1.0 / TAU).then_inc(kd_exp, 1)
                elif n == STEP_KEYS:
                    act.wait_ge(kt_full, l + 1)
                    act.activation(ktok.rearrange("p d b n -> p (d b n)"), aux_flat[:, 0:1536],
                                   ACT.Copy).then_inc(kt_ready, 1)
                if STEP_STATE <= n < STEP_STATE + len(LEVELS):
                    pair_exp(l, n - STEP_STATE + 1)

            def gla_finish(l):
                w = T if l < DEPTH - 1 else NX
                act.wait_ge(o_full, l + 1)
                if l == 0:
                    act.wait_ge(mm_done, PLAN.turn[FIRST_UNITS + 7] + 1)
                for t in range(2):
                    o = aux[:, 2 * t:2 * t + 2, 0:w // 2].rearrange("p s (c i) -> p s c i", i=CH)
                    for func, dst in ((ACT.Copy, bt[:, 6 + t, 0:w]), (ACT.Square, pair[0][:, t, 0:w])):
                        ins = act.activation(dst.rearrange("p (c s i) -> p s c i", s=2, i=CH), o, func)
                ins.then_inc(o_copied, 1)
                act.wait_ge(o_sum, l + 1)
                link(act.activation(pair[1][:, :, 0:w], auxw[:, :, 0:w], ACT.Ln, bias=eps[:, 0:1], scale=1.0 / DV))
                act.activation(pair[1][:, :, 0:w], pair[1][:, :, 0:w], ACT.Exp, scale=-0.5).then_inc(o_rstd, 1)

            def gla_gate(l):
                w = T if l < DEPTH - 1 else NX
                act.activation(proj[:, TGR:TGR + 2, 0:w], proj[:, TGR:TGR + 2, 0:w], ACT.Silu).then_inc(r_silu, 1)

            def unit_scores(l, u, r):
                n, nl = head_base[l] + 4 * u + r, P * (len(key_blocks(l, u)) - 2)
                act.wait_ge(s_full, n + 1)
                if r == 0:
                    if u == 0:
                        act.wait_ge(gla_out, l + 1)
                    elif u > 1:
                        act.wait_ge(pt_full, block_index(l, u - 1, 0))
                act.activation(sco[u % 2][:, r, nl:nl + NC], aux[:, 1, 0:NC], ACT.Copy, scale=HD ** -0.5).then_inc(s_ctx, 1)

            def unit_exp(l, u):
                b, nk = u % 2, P * len(key_blocks(l, u))
                act.wait_ge(m_ready, unit_base[l] + u + 1)
                for r in range(4):
                    act.activation(sco[b][:, r, 0:nk], sco[b][:, r, 0:nk], ACT.Exp, bias=small[:, b, 4 + r:5 + r],
                                   accum_out=small[:, b, 16 + r:17 + r])
                act.activation(small[:, b, 12:16], small[:, b, 8:12], ACT.Exp).then_inc(p_exp, 1)

            def read_gate(g, dst, before):
                act.wait_ge(mm_done, g + 1)
                if before is not None:
                    wait_evac(act, before)
                act.activation(dst, acc[:, g % 2, 0:dst.shape[-1]], ACT.Tanh, scale=0.5).then_inc(acc_free[g % 2], 1)

            def chunk_head(n, par_, jj, w, src, scale, per=0, i=0):
                act.wait_ge(g_val, n + per * i)
                act.activation(gact[:, par_, jj, 0, 0:w], src[:, 0:w], ACT.Copy, scale=scale).then_inc(g_hi, 1)

            def read_quad(a, row, i=0, per_g=0):
                g = PLAN.quad[a]
                act.wait_ge(mm_done, g + 1 + per_g * i)
                act.activation(row[a % 2], acc[:, g % 2, 0:512], ACT.Copy).then_inc(acc_free[g % 2], 1)

            def ups(l, c, g, q, par_, w, i=0, per_g=0, per_q=0, per_t=0, unit=None):
                for n in range(4):
                    kk, dst = n // 2, (conv_a, conv_g)[n % 2][n // 2]
                    f = (2 * c + kk) + NFF * (n % 2)
                    gg = g + UP_GROUPS[unit is not None][n]
                    act.wait_ge(mm_done, gg + 1 + per_g * i)
                    if not (c == 0 and per_t == 0):
                        act.wait_ge(g_ready, g_count(l, "ffn", 2 * c - 1 + kk) + per_t * i)
                    act.activation(dst[:, 0:w], acc[:, gg % 2, 0:w], ACT.Identity,
                                   bias=par[:, l, bass.ds(C_CB + f + per_t * i, 1)],
                                   scale=par[:, l, bass.ds(C_CW + 2 * NFF + f + per_t * i, 1)]).then_inc(conv_mid, 1)
                    split(q + n + SPL, i, per_q, per_g)
                    if unit is not None and n in (0, 2):
                        read_quad(2 * unit + n // 2, row_ffn, i, per_g)
                    if n % 2:
                        act.wait_ge(acc_free[gg % 2], gg // 2 + 1 + per_g // 2 * i)
                        act.activation(conv_g[kk][:, 0:w], conv_g[kk][:, 0:w], ACT.Silu).then_inc(silu_ready, 1)
                        if n == 1:
                            chunk_head(g_count(l, "ffn", 2 * c + 1), par_, 0, w, conv_a[0], 1.0, per_t, i)

            def read_gate_piece(l, j, f, w):
                if f == 1:
                    read_gate(gate_group(l, j, 0), gates[0][:, 0:w], gate_group(l, j - 1, 1) if j else None)
                    split(PLAN.layers[l]["gate_q"] + 2 * j + SPL)
                if f == 3:
                    read_gate(gate_group(l, j, 2), gates[1][:, 0:w], gate_group(l, j - 1, 3) if j else None)
                    split(PLAN.layers[l]["gate_q"] + 2 * j + 1 + SPL)

            act.wait_ge(consts_in, 16 * 4)
            act.activation(cvec[:, :, :], cvec[:, :, :], ACT.Silu).then_inc(cvec_ready, 1)
            act.wait_ge(eps_set, 1)
            squares(0)
            inverse_root(0)
            for m in range(FIRST_UNITS):
                for a in (2 * m, 2 * m + 1):
                    read_quad(a, row_first)
            for l, at in enumerate(PLAN.layers):
                ctx = l < DEPTH - 1
                w = T if ctx else NX
                if l == 0:
                    split(0)
                    split(1)
                heads(l, 2 * l, SH1, True)
                if l > 0:
                    act.wait_ge(x_spilled, 16 * l)
                for n in range(len(ORDER) + 1):
                    if l == 0:
                        if n == 8:
                            act.wait_ge(cum_ready, 1)
                        read_quad(LATE_QUAD + n, late_rows(FIRST_UNITS + n // 2))
                    gla_step(l, n)
                    if n < len(ORDER):
                        read_projection(l, ORDER[n], at["proj_g"][n])
                        split(at["q"] + n + SPL)
                act.wait_ge(pool_d, 2 * (l + 1))
                for t in range(2):
                    g = at["gate_g"] + t
                    act.wait_ge(mm_done, g + 1)
                    act.activation(bt[:, 4 + t, 0:w], acc[:, g % 2, 0:w], ACT.Copy,
                                   scale=par[:, l, C_PSC + t:C_PSC + t + 1]).then_inc(acc_free[g % 2], 1)
                gla_finish(l)
                gla_gate(l)
                read_gate_piece(l, 0, 1, w)
                act.wait_ge(va_full, l + 1)
                act.activation(vat.rearrange("p b n -> p (b n)"), aux_flat[:, 512:1280], ACT.Copy).then_inc(va_ready, 1)
                us = units(l)
                for u in range(len(us) + 1):
                    for i in range(6):
                        if u < len(us) and i < 4:
                            unit_scores(l, u, i)
                        if u < len(us) and i < 5:
                            for j, f in pieces(l, len(us), u, i):
                                read_gate_piece(l, j, f, w)
                        if u > 0 and 0 < i <= len(key_blocks(l, u - 1)):
                            n = block_index(l, u - 1, i - 1)
                            if u == 1 and i <= 2:
                                act.wait_ge(rope_done, 5 * (l + 1))
                            act.wait_ge(pt_full, n + 1)
                            act.activation(ptb[n % 2], aux[:, 2, :], ACT.Copy).then_inc(pt_ready, 1)
                    if u < len(us):
                        unit_exp(l, u)
                g, q = at["mix_g"], at["mix_q"]
                for c in range(KT // 2 + 1):
                    if c < KT // 2:
                        for jj in range(2):
                            before = (g + 1 - 4 - (8 if c > 1 else 0)) if c else None
                            read_gate(g, mgate[jj][:, 0:w], before)
                            split(q + SPL)
                            chunk_head(g_count(l, "mix", 2 * c + jj + 1), c % 2, jj, w, part[:, 2 * c + jj, :], 0.5)
                            g, q = g + 2, q + 1
                    if c == KT // 2:
                        squares(4 * l + 1)
                        inverse_root(4 * l + 1)
                    if c > 0:
                        split(q + SPL)
                        split(q + 1 + SPL)
                        g, q = g + 8, q + 2
                squares(4 * l + 2)
                inverse_root(4 * l + 2)
                heads(l, 2 * l + 1, SH2, ctx)
                g, q, up_n = at["ffn_g"], at["ffn_q"], UP_COUNT[l == 0]
                pg, pq, unit = 2 * (up_n + KT), FFN_BODY_Q, UNITS if l == 0 else None
                ups(l, 0, g, q, 0, w, unit=unit)
                chunk_head(g_count(l, "ffn", 2), 0, 1, w, conv_a[1], 1.0)
                g, q = g + up_n, q + 4
                with act.Fori(0, FFN_LOOPS) as i:
                    ups(l, 1, g, q, 1, w, i, pg, pq, 4, unit=unit and unit + 1)
                    split(q + 4 + SPL, i, pq, pg)
                    chunk_head(g_count(l, "ffn", 4), 1, 1, w, conv_a[1], 1.0, 4, i)
                    split(q + 5 + SPL, i, pq, pg)
                    ups(l, 2, g + up_n + KT, q + 6, 0, w, i, pg, pq, 4, unit=unit and unit + 2)
                    split(q + 10 + SPL, i, pq, pg)
                    chunk_head(g_count(l, "ffn", 6), 0, 1, w, conv_a[1], 1.0, 4, i)
                    split(q + 11 + SPL, i, pq, pg)
                q += FFN_BODY_Q * FFN_LOOPS
                squares(4 * l + 3)
                inverse_root(4 * l + 3)
                split(q + SPL)
                split(q + 1 + SPL)
                if l == 0:
                    for a in (4 * UNITS - 2, 4 * UNITS - 1):
                        read_quad(a, row_ffn)
                    act.wait_ge(mm_done, PLAN.turn[2 * UNITS - 1] + 1)
                if l + 1 < DEPTH:
                    squares(4 * l + 4)
                    inverse_root(4 * l + 4)

        @block.vector
        def _(v):
            link = Chain(v, dve_link)

            def rest(q, i=0, per_q=0):
                if q >= PLAN.blocks:
                    return
                v.wait_ge(w_hi, q + 1 + per_q * i)
                v.tensor_tensor(wlo[:, q % SPL, :], raw[:, q % RAW, :], whi[:, q % SPL, :].bitcast(F32),
                                ALU.subtract).then_inc(w_split, 1)

            def modulate(l, n, k, post, scale, shift, ctx):
                v.wait_ge(rstd_ready, k + 1)
                for kt in range(KT + 1):
                    if kt < KT:
                        x_valid(v, l, post, kt)
                        if kt >= 2:
                            v.wait_ge(h_ready, KT * n + kt - 1)
                        for t0, t1, s in segments(ctx):
                            ins = v.scalar_tensor_tensor(tmp[kt % 2][:, t0:t1], x[:, kt, t0:t1],
                                                         ada[:, l, scale + kt, s:s + 1], rstd[:, t0:t1], ALU.mult, ALU.mult)
                        ins.then_inc(t_ready, 1)
                    if kt > 0:
                        j = kt - 1
                        v.wait_ge(h_hi, KT * n + j + 1)
                        for t0, t1, s in segments(ctx):
                            ins = v.scalar_tensor_tensor(hlo[:, j, t0:t1], tmp[j % 2][:, t0:t1],
                                                         ada[:, l, shift + j, s:s + 1], hhi[:, j, t0:t1].bitcast(F32),
                                                         ALU.add, ALU.subtract)
                        ins.then_inc(h_ready, 1)

            def residual(l, k, gate, ctx):
                v.wait_ge(rstd_ready, k + 1)
                if k % 4 == 1:
                    v.wait_ge(x_in, 16 * (l + 2))
                for kt in range(KT):
                    if kt >= 2:
                        v.wait_ge(x_ready, KT * (k // 2) + kt - 1)
                    for t0, t1, s in segments(ctx):
                        ins = v.scalar_tensor_tensor(tmp[kt % 2][:, t0:t1], y[:, kt, t0:t1],
                                                     ada[:, l, gate + kt, s:s + 1], rstd[:, t0:t1], ALU.mult, ALU.mult)
                    link(ins)
                    w = T if ctx else NX
                    v.tensor_tensor(x[:, kt, 0:w], x[:, kt, 0:w], tmp[kt % 2][:, 0:w], ALU.add).then_inc(x_ready, 1)

            def halves(ap, width, half, w):
                a = ap[:, 0:w].rearrange("p (n s i) -> p n s i", s=2, i=half)
                return a[:, :, 0, :], a[:, :, 1, :]

            def pair_args(l, n):
                half, w = LEVELS[n - 1], T if l < DEPTH - 1 else NX
                fl, fr = halves(cumf, T, half, w)
                bl, br = halves(cumb, T, half, w)
                al, ar = halves(pair[n % 2][:, 0, :], T, half, w)
                ql, qr = halves(pair[n % 2][:, 1, :], T, half, w)
                shape = list(fl.shape)
                edge_f = fl[:, :, half - 1:half].broadcast_to(shape)
                edge_b = br[:, :, 0:1].broadcast_to(shape)
                v.tensor_tensor(al, edge_f, fl, ALU.subtract)
                v.tensor_tensor(ar, edge_b, br, ALU.subtract)
                v.tensor_tensor(qr, fr, edge_f, ALU.subtract)
                v.tensor_tensor(ql, bl, edge_b, ALU.subtract).then_inc(e_args, 1)

            def pair_scale(l, n):
                w = T if l < DEPTH - 1 else NX
                v.wait_ge(e_exp, len(LEVELS) * l + n)
                v.tensor_tensor(pair[n % 2][:, 0, 0:w], pair[n % 2][:, 0, 0:w], proj[:, TGK, 0:w], ALU.mult)
                v.tensor_tensor(pair[n % 2][:, 1, 0:w], pair[n % 2][:, 1, 0:w], proj[:, TGQ, 0:w],
                                ALU.mult).then_inc(ab_ready, 1)

            def take_level(l, n):
                cc = NCH // 2 if l < DEPTH - 1 else NX // CH // 2
                v.wait_ge(gram_full, NGRAM * l + n + 1)
                if n:
                    v.wait_ge(gram_used, NGRAM * l + n)
                mask = gmask[:, n, :].rearrange("p (a b i) -> p a b i", a=1, b=1).broadcast_to([P, GLA_H, cc, CH])
                v.copy_predicated(attg[:, :, 0:cc, :], mask,
                                  aux[:, :, 0:cc * CH].rearrange("p h (c i) -> p h c i", i=CH)).then_inc(gram_used, 1)

            def gla_step(l, n):
                w = T if l < DEPTH - 1 else NX
                if n == STEP_Z:
                    v.wait_ge(z_used, 2 * l + 1)
                    for d in range(2):
                        ins = v.tensor_scalar(pair[1][:, d, :], auxw[:, d, 0:T], par[:, l, C_BA + d:C_BA + d + 1], 0.0,
                                              ALU.add, ALU.min)
                    ins.then_inc(z_used, 1)
                    v.wait_ge(z_used, 2 * (l + 1))
                    v.wait_ge(z_log, l + 1)
                    link(v.tensor_tensor(pair[0], pair[1], pair[0], ALU.subtract))
                    v.wait_ge(scanm_in, 16 * (l + 1))
                    v.tensor_tensor_scan(cumf, scanm, pair[0][:, 0, :], 0.0, ALU.mult, ALU.add)
                    v.tensor_tensor_scan(cumb[:, ::-1], scanm, pair[0][:, 1, ::-1], 0.0, ALU.mult,
                                         ALU.add).then_inc(cum_ready, 1)
                    v.wait_ge(cum_ready, l + 1)
                    cf, cb = (a.rearrange("p (c i) -> p c i", i=CH) for a in (cumf, cumb))
                    kf, kb = (pair[1][:, d, :].rearrange("p (c i) -> p c i", i=CH) for d in range(2))
                    v.tensor_tensor(kf, cf[:, :, CH - 1:CH].broadcast_to([P, NCH, CH]), cf, ALU.subtract)
                    v.tensor_tensor(kb, cb[:, :, 0:1].broadcast_to([P, NCH, CH]), cb, ALU.subtract).then_inc(kd_args, 1)
                elif n == STEP_KD:
                    wait_evac(v, proj_group(l, TGK))
                    v.wait_ge(kd_exp, l + 1)
                    v.tensor_tensor(pair[1][:, 0, :], pair[1][:, 0, :], proj[:, TGK, :], ALU.mult)
                    v.tensor_tensor(pair[1][:, 1, :], pair[1][:, 1, :], proj[:, TGK, :], ALU.mult).then_inc(kd_ready, 1)
                elif n == STEP_KEYS:
                    wait_evac(v, proj_group(l, TGQ))
                    v.tensor_scalar(pair[0][:, 1, 0:w], proj[:, TGQ, 0:w], 2.0, None, ALU.mult).then_inc(ab_ready, 1)
                    for d in range(2):
                        v.tensor_tensor(qdec[:, d, 0:w], qdec[:, d, 0:w], proj[:, TGQ, 0:w], ALU.mult)
                elif n == STEP_STATE:
                    v.wait_ge(kt_full, l + 1)
                    pair_args(l, 1)
                    orders = ([8, 9, 10, 11] + list(range(8)), [11, 10, 9, 8] + list(range(7, -1, -1)))
                    for order, d in zip(orders, range(2)):
                        ins = v.memset(state[:, d, order[0], :], 0.0)
                    link(ins)
                    v.wait_ge(u_full, l + 1)
                    for m in range(NCH - 1):
                        for d in range(2):
                            a, b = orders[d][m], orders[d][m + 1]
                            ins = v.scalar_tensor_tensor(state[:, d, b, :], state[:, d, a, :], dec[:, d, a:a + 1],
                                                         aux[:, 2 * d + a % 2, (a // 2) * DV:(a // 2) * DV + DV],
                                                         ALU.mult, ALU.add)
                        if m < NCH - 2:
                            link(ins)
                    ins.then_inc(states_ready, 1)
                    pair_scale(l, 1)
                elif STEP_GRAM <= n < STEP_GRAM + NGRAM:
                    m = n - STEP_GRAM
                    take_level(l, m)
                    if m + 2 < NGRAM:
                        pair_args(l, m + 2)
                        pair_scale(l, m + 2)

            def gla_finish(l):
                w = T if l < DEPTH - 1 else NX
                v.wait_ge(o_rstd, l + 1)
                link(v.tensor_tensor(bt[:, 6:8, 0:w], bt[:, 6:8, 0:w], pair[1][:, :, 0:w], ALU.mult))
                v.wait_ge(r_silu, l + 1)
                for t in range(2):
                    ins = v.scalar_tensor_tensor(bt[:, 6 + t, 0:w], bt[:, 6 + t, 0:w], par[:, l, C_GN + t:C_GN + t + 1],
                                                 proj[:, TGR + t, 0:w], ALU.mult, ALU.mult)
                ins.then_inc(gla_out, 1)

            def rope(l):
                v.wait_ge(tables_in, 32 * (l + 1))
                for n, tile in enumerate((TK, 0, 1, 2, 3)):
                    v.wait_ge(rot_full, 5 * l + n + 1)
                    if n > 0:
                        v.wait_ge(rope_done, 5 * l + n)
                    v.tensor_tensor(gtmp[:, 0:NX], aux[:, n % 4, :], ropes, ALU.mult).then_inc(rot_used, 1)
                    link(v.tensor_tensor(proj[:, tile, 0:NX], proj[:, tile, 0:NX], ropec, ALU.mult))
                    v.wait_ge(rot_used, 5 * l + n + 1)
                    v.tensor_tensor(proj[:, tile, 0:NX], proj[:, tile, 0:NX], gtmp[:, 0:NX], ALU.add).then_inc(rope_done, 1)

            def unit_scores(l, u, r):
                qb, _ = units(l)[u]
                nl = P * len(local_blocks(qb))
                if nl:
                    n = head_base[l] + 4 * u + r
                    v.wait_ge(s_full, n + 1)
                    if r == 0 and u > 1:
                        v.wait_ge(pt_full, block_index(l, u - 1, 0))
                    m0 = 0 if qb > 0 else P
                    v.scalar_tensor_tensor(sco[u % 2][:, r, 0:nl], aux[:, 0, 0:nl], HD ** -0.5, amask[:, m0:m0 + nl],
                                           ALU.mult, ALU.add).then_inc(s_local, 1)

            def head_max(l, u, r):
                b, nk, qb = u % 2, P * len(key_blocks(l, u)), units(l)[u][0]
                v.wait_ge(s_ctx, head_base[l] + 4 * u + r + 1)
                if qb < 4:
                    v.wait_ge(s_local, lhead_base[l] + 4 * u + r + 1)
                return v.tensor_reduce(small[:, b, r:r + 1], sco[b][:, r, 0:nk], AX_X, ALU.max)

            def unit_max(l, u):
                b, g = u % 2, units(l)[u][1]
                sink = par[:, l, C_SINK + 4 * g:C_SINK + 4 * g + 4]
                link(head_max(l, u, 3))
                link(v.tensor_tensor(small[:, b, 0:4], small[:, b, 0:4], sink, ALU.max))
                v.tensor_scalar(small[:, b, 4:8], small[:, b, 0:4], -1.0, None, ALU.mult)
                v.tensor_tensor(small[:, b, 8:12], sink, small[:, b, 0:4], ALU.subtract).then_inc(m_ready, 1)

            def unit_normalise(l, u):
                b, nk = u % 2, P * len(key_blocks(l, u))
                v.wait_ge(p_exp, unit_base[l] + u + 1)
                link(v.tensor_tensor(small[:, b, 16:20], small[:, b, 16:20], small[:, b, 12:16], ALU.add))
                link(v.reciprocal(small[:, b, 20:24], small[:, b, 16:20]))
                for r in range(4):
                    ins = v.tensor_scalar(sco[b][:, r, 0:nk], sco[b][:, r, 0:nk], small[:, b, 20 + r:21 + r], None,
                                          ALU.mult)
                ins.then_inc(p_ready, 1)

            def unit_output(l, u):
                qb, g = units(l)[u]
                rows = slice(g * HD, g * HD + HD)
                v.wait_ge(pv_full, unit_base[l] + u + 1)
                v.tensor_copy(bt[rows, 0:NQT, qb * P:qb * P + P],
                              aux[rows, 3, :].rearrange("p (r q) -> p r q", r=4)).then_inc(pv_used, 1)

            def gated(g, gate_g, gate, dst, w):
                v.wait_ge(mm_done, g + 1)
                wait_evac(v, gate_g)
                v.scalar_tensor_tensor(dst[:, 0:w], gate[:, 0:w], 1.0, acc[:, g % 2, 0:w], ALU.add,
                                       ALU.mult).then_inc(acc_free[g % 2], 1)
                wait_evac(v, g)

            def chunk_rest(n, par_, jj, w, src, scale, per=0, i=0):
                v.wait_ge(g_hi, n + per * i)
                v.scalar_tensor_tensor(gact[:, par_, jj, 1, 0:w], src[:, 0:w], scale,
                                       gact[:, par_, jj, 0, 0:w].bitcast(F32), ALU.mult, ALU.subtract).then_inc(g_ready, 1)

            def gate_step(l, j, f, w):
                q = PLAN.layers[l]["gate_q"] + 2 * j
                if f == 1:
                    rest(q + SPL)
                elif f == 2:
                    gated(gate_group(l, j, 1), gate_group(l, j, 0), gates[0], part[:, j, :], w)
                elif f == 3:
                    rest(q + 1 + SPL)
                elif f == 4:
                    gated(gate_group(l, j, 3), gate_group(l, j, 2), gates[1], gtmp, w)
                    link(v.tensor_tensor(part[:, j, 0:w], part[:, j, 0:w], gtmp[:, 0:w], ALU.add))

            def take_turn(m, i=0, per_g=0):
                g, (l, u) = PLAN.turn[m], divmod(m, UNITS)
                row = 4 * u + (8 * i if per_g else 0)
                v.wait_ge(mm_done, g + 1 + per_g * i)
                v.tensor_tensor(ada[:, l, bass.ds(row, 4), :], acc[:, g % 2, 0:8].rearrange("p (n s) -> p n s", s=2),
                                par[:, l, bass.ds(C_BADA + row, 4)].unsqueeze(2).broadcast_to([P, 4, 2]),
                                ALU.add).then_inc(acc_free[g % 2], 1)

            def fold(l, rows, count):
                for row, gain, bias in rows:
                    a = ada[:, l, row:row + KT, :]
                    ins = v.scalar_tensor_tensor(a, a, bias, par[:, l, gain:gain + KT].unsqueeze(2).broadcast_to([P, KT, 2]),
                                                 ALU.add, ALU.mult)
                ins.then_inc(cond_ready, 1)
                v.wait_ge(cond_ready, count)

            def add_down(g, q, w, i=0, per_g=0, per_q=0, tile=None, last=False):
                for m in range(KT):
                    gg = g + m
                    v.wait_ge(mm_done, gg + 1 + per_g * i)
                    v.tensor_tensor(y[:, m, 0:w], y[:, m, 0:w], acc[:, gg % 2, 0:w], ALU.add).then_inc(acc_free[gg % 2], 1)
                    if m == 1 and tile is not None:
                        tile_product(*tile)
                    if m % 4 == 3 and not last:
                        rest(q + m // 4 + SPL, i, per_q)
                    if m == 4 and tile is not None:
                        tile_rest(*tile)
                if last:
                    rest(q + SPL)
                    rest(q + 1 + SPL)

            def tile_product(l, c, kk, par_, w, i=0, per_t=0):
                v.wait_ge(silu_ready, NFF * l + 2 * c + kk + 1 + per_t * i)
                v.tensor_tensor(conv_a[kk][:, 0:w], conv_a[kk][:, 0:w], conv_g[kk][:, 0:w], ALU.mult).then_inc(g_val, 1)

            def tile_rest(l, c, kk, par_, w, i=0, per_t=0):
                t = g_count(l, "ffn", 2 * c + kk + 1)
                v.wait_ge(g_val, t + per_t * i)
                chunk_rest(t, par_, kk, w, conv_a[kk], 1.0, per_t, i)

            def ups(l, c, g, q, par_, w, i=0, per_g=0, per_q=0, per_t=0, unit=None):
                ctx = w == T
                for n in range(4):
                    kk, dst = n // 2, (conv_a, conv_g)[n % 2][n // 2]
                    f = (2 * c + kk) + NFF * (n % 2)
                    b = (g + UP_GROUPS[unit is not None][n]) % 2
                    v.wait_ge(conv_mid, 2 * NFF * l + 4 * c + n + 1 + 2 * per_t * i)
                    for tap, d0, d1, s0, s1 in ((0, 1, 0, 0, 1), (2, 0, 1, 1, 0)):
                        wt = par[:, l, bass.ds(C_CW + 2 * NFF * tap + f + per_t * i, 1)]
                        for t0, t1, _ in segments(ctx):
                            ins = v.scalar_tensor_tensor(dst[:, t0 + d0:t1 - d1], acc[:, b, t0 + s0:t1 - s1], wt,
                                                         dst[:, t0 + d0:t1 - d1], ALU.mult, ALU.add)
                        if tap == 0:
                            link(ins)
                    ins.then_inc(acc_free[b], 1)
                    rest(q + n + SPL, i, per_q)
                    if n == 1:
                        tile_product(l, c, 0, par_, w, i, per_t)
                        tile_rest(l, c, 0, par_, w, i, per_t)
                if unit is not None:
                    take_turn(unit, i, per_g)

            v.memset(eps[:, :], EPS).then_inc(eps_set, 1)
            v.wait_ge(consts_in, 16 * 4)
            for m in range(FIRST_UNITS):
                take_turn(m)
            wait_evac(v, PLAN.turn[FIRST_UNITS - 1])
            scale1 = ((SC1, C_GPRE, 1.0),)
            others = ((G1, C_GPOST, 0.0), (SC2, C_GPRE2, 1.0), (G2, C_GPOST2, 0.0))
            fold(0, scale1, 1)
            for l, at in enumerate(PLAN.layers):
                ctx = l < DEPTH - 1
                w = T if ctx else NX
                if l == 0:
                    rest(0)
                    rest(1)
                modulate(l, 2 * l, 4 * l, 2 * l, SC1, SH1, True)
                for n in range(len(ORDER) + 1):
                    if l == 0 and late_turns(n) is not None:
                        take_turn(late_turns(n))
                    gla_step(l, n)
                    if n < len(ORDER):
                        rest(at["q"] + n + SPL)
                if l == 0:
                    take_turn(FIRST_UNITS + 7)
                    wait_evac(v, PLAN.turn[FIRST_UNITS + 7])
                    fold(0, others, 2)
                gla_finish(l)
                gate_step(l, 0, 1, w)
                rope(l)
                us = units(l)
                for u in range(len(us) + 1):
                    for i in range(5):
                        if u < len(us) and i < 4:
                            unit_scores(l, u, i)
                            if i > 0:
                                head_max(l, u, i - 1)
                        if i == 0 and u > 0:
                            unit_normalise(l, u - 1)
                        if u < len(us):
                            for j, f in pieces(l, len(us), u, i):
                                gate_step(l, j, f, w)
                            if i == 3:
                                unit_max(l, u)
                    if u > 0:
                        unit_output(l, u - 1)
                g, q = at["mix_g"], at["mix_q"]
                for c in range(KT // 2 + 1):
                    if c < KT // 2:
                        for jj in range(2):
                            rest(q + SPL)
                            gated(g + 1, g, mgate[jj], mtmp, w)
                            j, t = 2 * c + jj, g_count(l, "mix", 2 * c + jj + 1)
                            v.tensor_tensor(part[:, j, 0:w], part[:, j, 0:w], mtmp[:, 0:w], ALU.add).then_inc(g_val, 1)
                            v.wait_ge(g_val, t)
                            chunk_rest(t, c % 2, jj, w, part[:, j, :], 0.5)
                            g, q = g + 2, q + 1
                    if c > 0:
                        v.wait_ge(y_zero, 2 * l + 1)
                        if c > 1:
                            wait_evac(v, g - 4 - 1 if c < KT // 2 else g - 1)
                        add_down(g, q, w, last=c == KT // 2)
                        g, q = g + 8, q + 2
                residual(l, 4 * l + 1, G1, ctx)
                modulate(l, 2 * l + 1, 4 * l + 2, 2 * l + 1, SC2, SH2, ctx)
                v.wait_ge(y_zero, 2 * l + 2)
                g, q = at["ffn_g"], at["ffn_q"]
                up_n = UP_COUNT[l == 0]
                pg, pq, unit = 2 * (up_n + KT), FFN_BODY_Q, UNITS if l == 0 else None
                ups(l, 0, g, q, 0, w, unit=unit)
                tile_product(l, 0, 1, 0, w)
                tile_rest(l, 0, 1, 0, w)
                g, q = g + up_n, q + 4
                with v.Fori(0, FFN_LOOPS) as i:
                    link.enter(i, 8)
                    ups(l, 1, g, q, 1, w, i, pg, pq, 4, unit=unit and unit + 1)
                    add_down(g + up_n, q + 4, w, i, pg, pq, tile=(l, 1, 1, 1, w, i, 4))
                    ups(l, 2, g + up_n + KT, q + 6, 0, w, i, pg, pq, 4, unit=unit and unit + 2)
                    add_down(g + 2 * up_n + KT, q + 10, w, i, pg, pq, tile=(l, 2, 1, 0, w, i, 4))
                    link.leave(FFN_LOOPS)
                g, q = g + pg * FFN_LOOPS, q + pq * FFN_LOOPS
                add_down(g, q, w, last=True)
                residual(l, 4 * l + 3, G2, ctx)
                if l == 0:
                    take_turn(2 * UNITS - 1)
                    wait_evac(v, PLAN.turn[2 * UNITS - 1])
                    fold(1, scale1 + others, 3)

        @block.gpsimd
        def _(pool):
            link = Chain(pool, pool_link)

            def pooling(l):
                ctx = l < DEPTH - 1
                segs = [(8, 0, NX)] + ([(NX + 24, NX, NC)] if ctx else [])
                n = segs[-1][0] + segs[-1][2] + 8
                pool.wait_ge(consts_in, 16 * 4)
                for t in range(2):
                    u = proj[:, TPOOL + t, :]
                    wait_evac(pool, proj_group(l, TPOOL + t))
                    link(pool.memset(up[:, 0:n], 0.0))
                    for p0, t0, m in segs:
                        ins = pool.tensor_scalar(up[:, p0:p0 + m], u[:, t0:t0 + m], 1.0, None, ALU.mult)
                    link(ins)
                    link(pool.tensor_tensor(pa[:, 1:n], up[:, 0:n - 1], up[:, 1:n], ALU.add))
                    upper, lower = POOL_WINDOWS[t]
                    if t == 0:
                        pool.tensor_tensor(pb[64:128, 2:n - 1], pa[64:128, 1:n - 2], pa[64:128, 3:n], ALU.add)
                        link(pool.tensor_scalar(pb[0:64, 8:n - 8], pa[0:64, 8:n - 8], 1.0 / upper, None, ALU.mult))
                    else:
                        link(pool.tensor_tensor(pb[:, 2:n - 1], pa[:, 1:n - 2], pa[:, 3:n], ALU.add))
                        link(pool.tensor_tensor(pa[:, 4:n - 4], pb[:, 2:n - 6], pb[:, 6:n - 2], ALU.add))
                        pool.tensor_scalar(pb[0:64, 8:n - 8], pa[0:64, 8:n - 8], 1.0 / upper, None, ALU.mult)
                        link(pool.tensor_tensor(pb[64:128, 8:n - 8], pa[64:128, 4:n - 12], pa[64:128, 12:n - 4], ALU.add))
                    link(pool.tensor_scalar(pb[64:128, 8:n - 8], pb[64:128, 8:n - 8], 1.0 / lower, None, ALU.mult))
                    for p0, _, m in segs:
                        for side, c0 in enumerate((p0, p0 + m - EDGE)):
                            k0 = K_EDGE + (2 * t + side) * EDGE
                            ins = pool.tensor_tensor(pb[:, c0:c0 + EDGE], pb[:, c0:c0 + EDGE], con[:, k0:k0 + EDGE], ALU.mult)
                    link(ins)
                    for p0, t0, m in segs:
                        ins = pool.tensor_tensor(u[:, t0:t0 + m], pb[:, p0:p0 + m], u[:, t0:t0 + m], ALU.subtract)
                    ins.then_inc(pool_d, 1)
                    pool.wait_ge(pool_d, 2 * l + t + 1)

            for l in range(DEPTH):
                pooling(l)
                pool.wait_ge(pv_used, unit_base[l + 1])
                pool.memset(y[:, :, :], 0.0).then_inc(y_zero, 1)
                pool.wait_ge(x_ready, KT * (2 * l + 1))
                pool.memset(y[:, :, :], 0.0).then_inc(y_zero, 1)


def _tiles(a):
    return np.ascontiguousarray(a.reshape(-1, P, a.shape[-1]).transpose(1, 0, 2))


def _rows(a):
    return a.reshape(-1, P).T


def _block(w, cols):
    return w[:, cols].reshape(KT, P, P).transpose(1, 0, 2).reshape(P, BLK)


def _chunk(w, c, half):
    return w[2 * c * P:2 * (c + 1) * P, half * 512:half * 512 + 512].reshape(2, P, 512).transpose(1, 0, 2).reshape(P, BLK)


def _weight_stream(w_in, w_o, w_up, w_down):
    at = dict(q=0, k=512, v=640, pool=768, gq=1024, gk=1152, gv=1280, gr=1536, lr=1792, mg=1824)
    run = lambda o: np.arange(o, o + P)
    heads = lambda t: np.concatenate([np.arange(t * HD, t * HD + HD), np.arange((t + 4) * HD, (t + 5) * HD)])
    cols = {TK: run(at["k"]), TV: run(at["v"]), TGQ: run(at["gq"]), TGK: run(at["gk"])}
    cols.update({t: heads(t) for t in range(NQT)})
    for t in range(2):
        cols[TPOOL + t], cols[TGV + t], cols[TGR + t] = run(at["pool"] + t * P), run(at["gv"] + t * P), run(at["gr"] + t * P)
    out = []
    for l in range(DEPTH):
        lr = np.concatenate([w_in[l][:, at["lr"]:at["mg"]], np.zeros((D, P - 32), w_in.dtype)], axis=1)
        for tile in ORDER:
            out.append(_block(lr, run(0)) if tile == TLR else _block(w_in[l], cols[tile]))
        gate = lambda b, j: _block(w_in[l], run(at["mg"] + b * D + j * P))
        for j in range(KT):
            out += [gate(1, j), gate(2, j)]
        for c in range(KT // 2 + 1):
            if c < KT // 2:
                out += [gate(0, 2 * c), gate(0, 2 * c + 1)]
            if c > 0:
                out += [_chunk(w_o[l], c - 1, 0), _chunk(w_o[l], c - 1, 1)]
        for c in range(NFF // 2 + 1):
            if c < NFF // 2:
                for j in (2 * c, 2 * c + 1):
                    out += [_block(w_up[l], run(j * P)), _block(w_up[l], run((NFF + j) * P))]
            if c > 0:
                out += [_chunk(w_down[l], c - 1, 0), _chunk(w_down[l], c - 1, 1)]
    return np.stack(out)


def _branch_stream(w_att, w_pool, w_gla):
    out = []
    for l in range(DEPTH):
        both = np.concatenate([w_pool[l], w_gla[l]], axis=0)
        order = np.concatenate([np.arange(h * HD, h * HD + HD) for t in range(NQT) for h in (t, t + 4)])
        for w in (both, w_att[l][order]):
            w = w.reshape(4, P, KT, P)
            for b in range(KT // 2):
                out.append(w[:, :, 2 * b:2 * b + 2, :].transpose(1, 2, 0, 3))
    return np.ascontiguousarray(np.stack(out))


def _parameters(i):
    f = i["b_ada"].dtype
    par = np.zeros((P, DEPTH, NPAR), f)
    for l in range(DEPTH):
        for c, v in ((C_BADA, i["b_ada"][l]), (C_GPRE, i["g_pre_mix"][l]), (C_GPOST, i["g_post_mix"][l]),
                     (C_GPRE2, i["g_pre_ffn"][l]), (C_GPOST2, i["g_post_ffn"][l]), (C_PSC, i["pool_scale"][l]),
                     (C_BA, i["gla_ba"][l].reshape(-1)), (C_GN, i["gla_norm"][l].reshape(-1)),
                     (C_CW, i["conv_w"][l].reshape(-1)), (C_CB, i["conv_b"][l])):
            r = _rows(v)
            par[:, l, c:c + r.shape[1]] = r
        par[:, l, C_SINK:C_SINK + 8] = i["att_sink"][l][None, :]
    return par


def _small_weights(gla_wa2, pool_w):
    wa2 = np.zeros((DEPTH, 32, 256), gla_wa2.dtype)
    poolw = np.zeros((DEPTH, P, 256), pool_w.dtype)
    for l in range(DEPTH):
        for d in range(2):
            wa2[l, 16 * d:16 * d + 16, P * d:P * d + P] = gla_wa2[l, d]
        for g in range(4):
            r = 64 * (g % 2)
            poolw[l, r:r + 64, (g // 2) * P + r:(g // 2) * P + r + 64] = pool_w[l, g]
    return wa2, poolw


def _constants():
    con = np.zeros((P, NCON), np.float32)
    p = np.arange(P)
    con[:, K_ONES:K_ONES + P] = 1.0
    con[:, K_BONES:K_BONES + P] = p[:, None] // 64 == p[None, :] // 64
    half = HD // 2
    for m in range(P):
        if m % HD < half:
            con[m + half, K_ROT + m] = -1.0
        else:
            con[m - half, K_ROT + m] = 1.0
    con[:, K_ID:K_ID + P] = np.eye(P)
    for v in range(2):
        con[v::32, K_SEL + v] = 1.0
    scanm = np.broadcast_to((np.arange(T) % CH != 0).astype(np.float32), (P, T)).copy()
    gm = np.zeros((P, NGRAM, CH), np.int32)
    a, b = (p % CH)[:, None], np.arange(CH)[None, :]
    for n, half_ in enumerate(LEVELS):
        gm[:, n + 1, :] = (a // (2 * half_) == b // (2 * half_)) & (a // half_ != b // half_)
    gm[:, 0, :] = a == b
    am = np.zeros((P, 3 * P), np.float32)
    am[:, 0:P] = np.where(p[None, :] >= p[:, None], 0.0, NEG)
    am[:, 2 * P:] = np.where(p[None, :] <= p[:, None], 0.0, NEG)
    n = HD // 4
    base = (10000.0 ** (-np.arange(n) / n)).astype(np.float32)
    tok = np.arange(NX)
    ang = np.concatenate([(tok // GRID_W).astype(np.float32)[:, None] * base,
                          (tok % GRID_W).astype(np.float32)[:, None] * base], axis=-1).T
    rope = np.concatenate([np.tile(np.cos(ang), (4, 1)), np.tile(np.sin(ang), (4, 1))], axis=1).astype(np.float32)
    for t, windows in enumerate(POOL_WINDOWS):
        for half_, w in enumerate(windows):
            for side in range(2):
                tok = np.arange(EDGE) + side * (NC - EDGE)
                cnt = np.clip(tok + w - w // 2, 0, NC) - np.clip(tok - w // 2, 0, NC)
                c = K_EDGE + (2 * t + side) * EDGE
                con[64 * half_:64 * half_ + 64, c:c + EDGE] = (w / cnt).astype(np.float32)
    return con, scanm, gm, am, rope


def _conditioning(w_ada):
    w = w_ada.reshape(DEPTH, 2, 4, P, UNITS, 512)
    return np.ascontiguousarray(w.transpose(0, 4, 1, 3, 2, 5)).reshape(DEPTH * UNITS * 2, P, 2048)


def kernel(**inputs):
    import concourse.bacc as bacc
    from concourse.bass_utils import run_bass_kernel_spmd

    i = {k: np.asarray(v) for k, v in inputs.items()}
    x_t = _tiles(np.concatenate([i["x"][0].T, i["ctx"][0].T], axis=1))
    c_t = np.zeros((P, KT, 32), i["c"].dtype)
    c_t[:, :, 0], c_t[:, :, 1] = _rows(i["c"][0]), _rows(i["c_ctx"])
    wa2, poolw = _small_weights(i["gla_wa2"], i["pool_w"])
    con, scanm, gm, am, rope = _constants()
    arrays = {
        "x_t": x_t, "c_t": c_t, "par_d": _parameters(i), "con_d": con, "ada_d": _conditioning(i["w_ada"]),
        "wst_d": _weight_stream(i["w_in"], i["w_o"], i["w_up"], i["w_down"]),
        "brw_d": _branch_stream(i["w_br_att"], i["w_br_pool"], i["w_br_gla"]),
        "wa2_d": wa2, "poolw_d": poolw, "scanm_d": scanm, "gmask_d": gm, "amask_d": am, "rope_d": rope,
    }
    nc = bacc.Bacc("TRN2", target_bir_lowering=False, num_devices=1)
    aps = {n: nc.dram_tensor(n, a.shape, mybir.dt.from_np(a.dtype), kind="ExternalInput").ap() for n, a in arrays.items()}
    out = nc.dram_tensor("out", (P, KT, NX), F32, kind="ExternalOutput").ap()
    build(nc, out=out, **aps)
    r = run_bass_kernel_spmd(nc, [arrays], core_ids=[0])
    return np.ascontiguousarray(r.results[0]["out"].transpose(1, 0, 2).reshape(D, NX).T)[None]
```

```python
from contextlib import ExitStack

import numpy as np

import concourse.bass as bass
from concourse import mybir

ALU = mybir.AluOpType
ACT = mybir.ActivationFunctionType
F32 = mybir.dt.float32
F32R = mybir.dt.float32r
I32 = mybir.dt.int32
AX_X = mybir.AxisListType.X

P = 128
DEPTH = 2
D = 1024
KT = D // P
NX, NC = 512, 256
T = NX + NC
EPS = 1e-6
GRID_W = 64
HD = 64
NQT = 4
GLA_H, DK, DV, CH = 4, 32, 64, 64
NCH = T // CH
TAU = 16.0
NFF = 2816 // P
BLK = 1024
RAW, SPL = 4, 2
NEG = -3.0e38
ACCS = 3
UNITS = 6 * D // 512
FIRST_UNITS = 4
FIRST_PLACES = 6
EDGE = 8
LEVELS = (32, 16, 8, 4, 2, 1)
NGRAM = 1 + len(LEVELS)

TQ, TK, TV, TPOOL, TGQ, TGK, TGV, TGR, TLR = 0, 4, 5, 6, 8, 9, 10, 12, 14
NPROJ = 15
ORDER = (TLR, TGV, TGV + 1, TGK, TGQ, TGR, TGR + 1, TPOOL, TPOOL + 1, TK, TV, 0, 1, 2, 3)
WITH_CTX = (TLR, TGK, TGV, TGV + 1, TK, TV)
STEP_Z, STEP_V, STEP_KD, STEP_KEYS, STEP_STATE, STEP_GRAM = 2, 4, 5, 6, 7, 8
(C_BADA, C_GPRE, C_GPOST, C_GPRE2, C_GPOST2, C_PSC, C_BA, C_GN, C_CW, C_CB, C_SINK, NPAR) = np.cumsum(
    [0, 48, 8, 8, 8, 8, 2, 2, 2, 3 * 2 * NFF, 2 * NFF, 8]).tolist()
K_ONES, K_BONES, K_ROT, K_ID, K_SEL, K_EDGE, NCON = 0, 128, 256, 384, 512, 514, 514 + 4 * EDGE
SH1, SC1, G1, SH2, SC2, G2 = range(0, 48, 8)


class Plan:

    def __init__(self):
        self.group_end = []
        self.branch_end = []
        self.quad = []
        self.turn = []
        self.layers = []
        self.slot = []
        self.had = [0] * ACCS
        self.ring(2)

        def block(groups=1):
            self.open(groups)
            self.group_end.append(self.g)

        for _ in range(FIRST_UNITS):
            self.add_quad(), self.add_quad(), self.add_turn()
        for l in range(DEPTH):
            at = {"q": len(self.group_end), "proj_g": []}
            for n in range(len(ORDER) + 1):
                if l == 0:
                    if n >= 2 and n % 2 == 0:
                        self.add_turn()
                    self.add_quad()
                if n < len(ORDER):
                    at["proj_g"].append(self.g)
                    block()
            if l == 0:
                self.add_turn()
            at["gate_q"], at["gate_g"], at["gate_b"] = len(self.group_end), self.g, len(self.branch_end)
            self.open(2)
            for j in range(KT):
                block()
                block(2)
                self.open()
                if j % 2:
                    self.branch_end.append(self.g)
            at["mix_q"], at["mix_g"], at["mix_b"] = len(self.group_end), self.g, len(self.branch_end)
            self.ring(ACCS)
            for c in range(KT // 2 + 1):
                if c < KT // 2:
                    block()
                    block(2)
                    self.open()
                    self.branch_end.append(self.g)
                if c > 0:
                    block(4)
                    block(4)
            at["ffn_q"], at["ffn_g"] = len(self.group_end), self.g
            self.ring(ACCS)
            for c in range(NFF // 2 + 1):
                if c < NFF // 2:
                    for n in range(4):
                        block()
                        if l == 0 and n in (0, 2):
                            self.add_quad()
                    if l == 0:
                        self.add_turn()
                elif l == 0:
                    self.add_quad(), self.add_quad(), self.add_turn()
                if c > 0:
                    block(4)
                    block(4)
            at["down_g"] = self.g - KT
            at["end_g"] = self.g
            self.ring(2)
            self.layers.append(at)
        self.blocks = len(self.group_end)
        self.branches = len(self.branch_end)
        assert len(self.turn) == DEPTH * UNITS and len(self.quad) == 2 * len(self.turn)

    @property
    def g(self):
        return len(self.slot)

    def ring(self, n):
        order = list(range(n))
        if self.slot and self.slot[-1][0] == 0:
            order = order[1:2] + order[:1] + order[2:]
        self.order, self.at = order, 0

    def open(self, groups=1):
        for _ in range(groups):
            a = self.order[self.at]
            self.slot.append((a, self.had[a]))
            self.had[a] += 1
            self.at = (self.at + 1) % len(self.order)

    def add_quad(self):
        self.quad.append(self.g)
        self.open()

    def add_turn(self):
        self.turn.append(self.g)
        self.open()


PLAN = Plan()


def slot(g):
    return PLAN.slot[g][0]


FFN_BODY_Q, FFN_LOOPS = 12, (NFF // 2 - 1) // 2
LATE_QUAD = 2 * FIRST_UNITS
FFN_QUAD = LATE_QUAD + len(ORDER) + 1
UP_GROUPS = {True: (0, 2, 3, 5), False: (0, 1, 2, 3)}
UP_COUNT = {True: 7, False: 4}


def late_turns(n):
    return FIRST_UNITS + n // 2 - 1 if n >= 2 and n % 2 == 0 else None


def pieces(units_, u, i):
    a, b = (4 + (5 * KT - 4) * v // units_ for v in (u, u + 1))
    return [divmod(a + k, 5) for k, step in enumerate(PIECE_STEPS[b - a]) if step == i]


PIECE_STEPS = {3: (0, 1, 5), 4: (0, 1, 4, 6), 5: (0, 1, 2, 4, 6)}
STEPS = 7
POOL_WINDOWS = ((2, 4), (8, 16))


class Chain:

    def __init__(self, eng, sem):
        self.eng, self.sem, self.n, self.shift = eng, sem, 0, 0

    def __call__(self, ins):
        ins.then_inc(self.sem, 1)
        self.n += 1
        self.eng.wait_ge(self.sem, self.n + self.shift)

    def enter(self, reg, per):
        self.start, self.per, self.shift = self.n, per, reg * per

    def leave(self, loops):
        assert self.n - self.start == self.per, (self.n - self.start, self.per)
        self.n, self.shift = self.start + self.per * loops, 0


def segments(ctx):
    return [(0, NX, 0), (NX, T, 1)] if ctx else [(0, NX, 0)]


def build(nc, x_t, c_t, par_d, con_d, ada_d, wst_d, brw_d, wa2_d, poolw_d, scanm_d, gmask_d, amask_d, rope_d, out):
    spill = nc.dram_tensor("x_spill", (P, KT * T), F32).ap()
    with ExitStack() as es:
        def sem(name):
            return es.enter_context(nc.semaphore(name))

        def sb(name, shape, dt=F32, stack=es):
            return stack.enter_context(nc.sbuf_tensor(name, shape, dt))

        hhi = sb("hhi", [P, KT, T], F32R)
        hlo = sb("hlo", [P, KT, T], F32R)
        whi = sb("whi", [P, SPL, BLK], F32R)
        wlo = sb("wlo", [P, SPL, BLK], F32R)
        raw = sb("raw", [P, RAW, BLK])
        brw = sb("brw", [P, 2, 2, 4, P])
        par = sb("par", [P, DEPTH, NPAR])
        con = sb("con", [P, NCON])
        cvec = sb("cvec", [P, KT, 32])
        ada = sb("ada", [P, DEPTH, 48, 2])
        wa2 = sb("wa2", [32, 256])
        poolw = sb("poolw", [P, 256])
        gmask = sb("gmask", [P, NGRAM, CH], I32)
        small = sb("small", [P, 2, 24])
        eps = sb("eps", [P, 1])
        warm = sb("warm", [P, 1])
        dec = sb("dec", [P, 2, NCH])
        bt = sb("bt", [P, KT, T])
        y = sb("y", [P, KT, T])
        over = ExitStack()
        gact = sb("gact", [P, 2, 2, 2, T], F32R, over)
        over.close()
        ext = sb("ext", [P, 3840])
        proj = sb("proj", [P, NPROJ, T])
        x = proj[:, TPOOL + 1:NPROJ, :]
        part = x

        ones, bones = con[:, K_ONES:K_ONES + P], con[:, K_BONES:K_BONES + P]
        rot, ident = con[:, K_ROT:K_ROT + P], con[:, K_ID:K_ID + P]

        sq = [bt[:, 0, :], bt[:, 1, :]]
        sq_sum = bt[:, 3, :]
        rstd = bt[:, 2, :]
        tmp = [bt[:, 3, :], bt[:, 4, :]]
        mod = [bt[:, 3 + n, :] for n in range(4)]
        conv_a = [bt[:, 3, :], bt[:, 4, :]]
        conv_g = [bt[:, 5, :], bt[:, 6, :]]
        late_u = bt[:, 0, :]
        first_w = [y[:, :, :].rearrange("p a b -> p (a b)")[:, n * 2048:n * 2048 + 2048] for n in range(3)]
        first_w += [proj[:, 3 * n:3 * n + 3, :].rearrange("p a b -> p (a b)")[:, 0:2048] for n in range(2)]
        first_w.append(ext[:, 0:2048])
        later_w = brw[:, :, :, :, :].rearrange("p s t k n -> p (s t k n)")
        row = bt[:, 7, 256:768]
        ffn_w = [later_w, proj[:, 3:6, :].rearrange("p a b -> p (a b)")[:, 0:2048]]
        cumf, cumb = y[:, 0, :], y[:, 1, :]
        pair = [y[:, 2:4, :], y[:, 4:6, :]]
        qdec = y[:, 6:8, :]
        vtok = ext[:, 0:6 * 256].rearrange("p (b n) -> p b n", b=6)
        ktok = ext[:, 1536:3072].rearrange("p (d b n) -> p d b n", d=2, b=6)
        scanm = ext[:, 3072:3072 + T]
        attg = bt[:, 0:2, :].rearrange("p a b -> p (a b)").rearrange("p (h c i) -> p h c i", h=GLA_H, c=6)
        state = bt[:, 2:4, :].rearrange("p d (c e) -> p d c e", c=NCH)
        yf = y[:, :, :].rearrange("p a b -> p (a b)")
        sco = [yf[:, 0:2560].rearrange("p (r k) -> p r k", r=4), yf[:, 2560:5120].rearrange("p (r k) -> p r k", r=4)]
        vat = yf[:, 5120:5120 + 768].rearrange("p (b n) -> p b n", b=6)
        ptb = [ext[:, 0:512], ext[:, 512:1024]]
        gates = [ext[:, 1024:1024 + T], ext[:, 1792:1792 + T]]
        gtmp = ext[:, 2560:2560 + T]
        amask = ext[:, 3328:3328 + 3 * P]
        ropec, ropes = ext[:, 0:512], ext[:, 512:1024]
        up, pa, pb = (bt[:, 4:8, :].rearrange("p a b -> p (a b)")[:, i * 800:i * 800 + 800] for i in range(3))
        mgate = [proj[:, 3, :], proj[:, 4, :]]
        mtmp = proj[:, 5, :]

        acc = es.enter_context(nc.psum_tensor("acc", [P, 2, 1024], F32))
        aux = es.enter_context(nc.psum_tensor("aux", [P, 4, 512], F32))
        auxw = aux[:, :, :].rearrange("p (t b) n -> p t (b n)", b=2)

        accs = [acc[:, 0, :], acc[:, 1, :], auxw[:, 1, :]]
        aux_flat = aux[:, :, :].rearrange("p b n -> p (b n)")

        consts_in = sem("consts_in")
        x_in = sem("x_in")
        x_spilled = sem("x_spilled")
        tables_in = sem("tables_in")
        scanm_in = sem("scanm_in")
        out_done = sem("out_done")
        w_landed = [sem(f"w_landed{i}") for i in range(RAW)]
        b_landed = [sem(f"b_landed{i}") for i in range(2)]
        ada_landed = [sem(f"ada_landed{i}") for i in range(FIRST_PLACES + 2)]
        cond_ready = sem("cond_ready")
        small_in = sem("small_in")
        cvec_ready = sem("cvec_ready")
        w_hi = sem("w_hi")
        w_split = sem("w_split")
        mm_done = sem("mm_done")
        acc_free = [sem(f"acc_free{i}") for i in range(ACCS)]
        sq_ready = sem("sq_ready")
        sq_used = sem("sq_used")
        rstd_ready = sem("rstd_ready")
        t_ready = [sem("t_ready0"), sem("t_ready1")]
        h_hi = sem("h_hi")
        h_ready = sem("h_ready")
        y_scaled = sem("y_scaled")
        x_ready = [sem("x_ready0"), sem("x_ready1")]
        y_zero = sem("y_zero")
        z_full, z_used, z_log = sem("z_full"), sem("z_used"), sem("z_log")
        cum_ready = sem("cum_ready")
        v_full, v_ready = sem("v_full"), sem("v_ready")
        kd_args, kd_exp, kd_ready = sem("kd_args"), sem("kd_exp"), sem("kd_ready")
        kt_full, kt_ready = sem("kt_full"), sem("kt_ready")
        u_full, states_ready = sem("u_full"), sem("states_ready")
        e_args, e_exp, ab_ready = sem("e_args"), sem("e_exp"), sem("ab_ready")
        gram_full, gram_used = sem("gram_full"), sem("gram_used")
        o_full, o_copied, o_sum, o_rstd, gla_out = (sem(n) for n in ("o_full", "o_copied", "o_sum", "o_rstd", "gla_out"))
        pool_d = sem("pool_d")
        rot_full, rot_used, rope_done = sem("rot_full"), sem("rot_used"), sem("rope_done")
        va_full, va_ready = sem("va_full"), sem("va_ready")
        s_full, s_local, s_ctx = sem("s_full"), sem("s_local"), sem("s_ctx")
        m_ready, p_exp, p_ready = sem("m_ready"), sem("p_exp"), sem("p_ready")
        pt_full, pt_ready = sem("pt_full"), sem("pt_ready")
        pv_full, pv_used = sem("pv_full"), sem("pv_used")
        r_silu = sem("r_silu")
        conv_mid = sem("conv_mid")
        taps_added = sem("taps_added")
        g_val, g_hi, g_ready = sem("g_val"), sem("g_hi"), sem("g_ready")
        silu_ready = sem("silu_ready")
        eps_set = sem("eps_set")
        dve_link, act_link, pool_link = sem("dve_link"), sem("act_link"), sem("pool_link")

        def units(l):
            return [(qb, g) for qb in range(4 if l == DEPTH - 1 else 6) for g in range(2)]

        def local_blocks(qb):
            return list(range(max(qb - 1, 0), min(qb + 2, 4))) if qb < 4 else []

        unit_base, head_base, lhead_base, blk_base = [0], [0], [0], [0]
        for l in range(DEPTH):
            us = units(l)
            unit_base.append(unit_base[-1] + len(us))
            head_base.append(head_base[-1] + 4 * len(us))
            lhead_base.append(lhead_base[-1] + 4 * sum(qb < 4 for qb, _ in us))
            blk_base.append(blk_base[-1] + sum(len(local_blocks(qb)) + 2 for qb, _ in us))

        def gate_group(l, j, n):
            return PLAN.layers[l]["gate_g"] + 2 + 4 * j + n

        def quad_place(a):
            if a < LATE_QUAD:
                return a % FIRST_PLACES, a // FIRST_PLACES
            if a < FFN_QUAD:
                return FIRST_PLACES, a - LATE_QUAD
            if a % 2 == 0:
                return FIRST_PLACES, FFN_QUAD - LATE_QUAD + (a - FFN_QUAD) // 2
            return FIRST_PLACES + 1, (a - FFN_QUAD) // 2

        def quad_weights(a):
            return first_w[a % FIRST_PLACES] if a < LATE_QUAD else later_w if a < FFN_QUAD else ffn_w[a % 2]

        def proj_group(l, tile):
            return PLAN.layers[l]["proj_g"][ORDER.index(tile)]

        def key_blocks(l, u):
            return local_blocks(units(l)[u][0]) + [4, 5]

        def block_index(l, u, b):
            return blk_base[l] + sum(len(key_blocks(l, v)) for v in range(u)) + b

        def g_count(l, part_, tiles):
            return l * (KT + NFF) + (KT if part_ == "ffn" else 0) + tiles

        def wait_evac(eng, g, i=0, per_g=0):
            a, n = PLAN.slot[g]
            eng.wait_ge(acc_free[a], n + 1 + per_g // ACCS * i)

        def x_valid(eng, l, post, kt):
            if post == 0:
                eng.wait_ge(x_in, 16)
            else:
                eng.wait_ge(x_ready[kt % 2], KT // 2 * (post - 1) + kt // 2 + 1)

        def norm_ctx(k):
            return k % 4 == 0 or k // 4 < DEPTH - 1

        def norm_source_ready(eng, k, kt):
            l, part_ = divmod(k, 4)
            if part_ in (0, 2):
                x_valid(eng, l, 2 * l + part_ // 2, kt)
            else:
                wait_evac(eng, (PLAN.layers[l]["ffn_g"] - KT if part_ == 1 else PLAN.layers[l]["down_g"]) + kt)

        block = es.enter_context(nc.Block())

        @block.sync
        def _(sp):
            for dst, src in ((cvec[:, :, :], c_t), (con[:, :], con_d), (par[:, :, :], par_d), (gmask[:, :, :], gmask_d)):
                sp.dma_start(dst, src).then_inc(consts_in, 16)
            def weights(q, i=0, per=0):
                if q >= RAW:
                    sp.wait_ge(w_split, q - RAW + 1 + per * i)
                sp.dma_start(raw[:, q % RAW, :], wst_d[q + per * i]).then_inc(w_landed[q % RAW], 16)

            def branch(b):
                if b >= 2:
                    sp.wait_ge(mm_done, PLAN.branch_end[b - 2])
                sp.dma_start(brw[:, b % 2, :, :, :], brw_d[b]).then_inc(b_landed[b % 2], 16)

            def quad(a, i=0, per_g=0):
                before = a - FIRST_PLACES if a < LATE_QUAD else a - 1 if a < FFN_QUAD else a - 2
                if a >= FFN_QUAD + 2 or LATE_QUAD < a < FFN_QUAD or FIRST_PLACES <= a < LATE_QUAD:
                    sp.wait_ge(mm_done, PLAN.quad[before] + 1 + per_g * i)
                sp.dma_start(quad_weights(a), ada_d[a + 4 * i if per_g else a]).then_inc(ada_landed[quad_place(a)[0]], 16)

            for a in range(LATE_QUAD):
                if a == 2:
                    sp.dma_start(x, x_t).then_inc(x_in, 16)
                quad(a)
            for l, at in enumerate(PLAN.layers):
                for q in range(at["q"], at["q"] + RAW):
                    weights(q)
                if l == 0:
                    quad(LATE_QUAD)
                if l > 0:
                    for kt in range(KT):
                        x_valid(sp, l, 2 * l, kt)
                    sp.dma_start(spill, x).then_inc(x_spilled, 16)
                    sp.wait_ge(mm_done, PLAN.layers[l - 1]["end_g"])
                sp.dma_start(scanm, scanm_d).then_inc(scanm_in, 16)
                sp.dma_start(wa2[:, :], wa2_d[l]).then_inc(small_in, 16)
                sp.dma_start(poolw[:, :], poolw_d[l]).then_inc(small_in, 16)
                for n in range(1, len(ORDER) + 1):
                    if at["q"] + RAW - 1 + n < at["gate_q"]:
                        weights(at["q"] + RAW - 1 + n)
                    if l == 0:
                        quad(LATE_QUAD + n)
                weights(at["gate_q"])
                weights(at["gate_q"] + 1)
                if l == 0:
                    sp.wait_ge(mm_done, PLAN.quad[FFN_QUAD - 1] + 1)
                branch(at["gate_b"])
                sp.wait_ge(o_full, l + 1)
                if l == 0:
                    sp.wait_ge(mm_done, PLAN.turn[FIRST_UNITS + 7] + 1)
                sp.dma_start(ext[:, 0:1024], rope_d).then_inc(tables_in, 16)
                sp.dma_start(amask, amask_d).then_inc(tables_in, 16)
                for n, q in enumerate(range(at["gate_q"] + 2, at["mix_q"])):
                    if n % 4 == 0 and 0 < n // 4 + 1 < 4:
                        branch(at["gate_b"] + n // 4 + 1)
                    weights(q)
                for q in range(at["mix_q"], at["ffn_q"]):
                    n = q - at["mix_q"]
                    if n in (0, 2, 4, 6):
                        branch(at["mix_b"] + n // 2)
                    weights(q)
                sp.wait_ge(g_ready, g_count(l, "mix", KT))
                if l == 0:
                    sp.dma_start(x, x_t).then_inc(x_in, 16)
                else:
                    sp.wait_ge(x_spilled, 16 * l)
                    sp.dma_start(x, spill).then_inc(x_in, 16)
                q0, a0 = at["ffn_q"], FFN_QUAD
                body_g = 2 * (UP_COUNT[l == 0] + KT)
                for q in range(q0, q0 + 4):
                    weights(q)
                if l == 0:
                    sp.wait_ge(mm_done, PLAN.branch_end[at["mix_b"] + KT // 2 - 1])
                    quad(a0)
                    quad(a0 + 1)
                with sp.Fori(0, FFN_LOOPS) as i:
                    for p in range(FFN_BODY_Q):
                        weights(q0 + 4 + p, i, FFN_BODY_Q)
                        if l == 0 and p in (2, 4, 6, 8):
                            quad(a0 + 1 + p // 2, i, body_g)
                if l == 0:
                    quad(a0 + 2 + 4 * FFN_LOOPS)
                    quad(a0 + 3 + 4 * FFN_LOOPS)
                end = PLAN.layers[l + 1]["q"] if l + 1 < DEPTH else PLAN.blocks
                for q in range(q0 + 4 + FFN_BODY_Q * FFN_LOOPS, end):
                    weights(q)
            for kt in range(KT):
                x_valid(sp, DEPTH, 2 * DEPTH, kt)
                sp.dma_start(out[:, kt, :], x[:, kt, 0:NX]).then_inc(out_done, 16)
            sp.wait_ge(out_done, 16 * KT)

        @block.tensor
        def _(pe):
            def product(g, q, ctx, ks, i=0, per_g=0, first=True, last=True, h=None):
                s = q % SPL
                for k in ks:
                    if h is not None:
                        pe.wait_ge(h_ready, KT * h + k + 1)
                    for w_, a_ in ((whi, hhi), (whi, hlo), (wlo, hhi)):
                        start = first and k == ks[0] and w_ is whi and a_ is hhi
                        stop = last and k == ks[-1] and w_ is wlo
                        for t0, t1, _ in segments(ctx):
                            mm = pe.matmul(accs[slot(g)][:, t0:t1], w_[:, s, k * P:k * P + P], a_[:, k, t0:t1],
                                           start=start, stop=stop)
                if last:
                    mm.then_inc(mm_done, 1)

            def open_group(g, i=0, per=0):
                a, n = PLAN.slot[g]
                if n > 0:
                    pe.wait_ge(acc_free[a], n + (per // ACCS) * i)

            def block_split(q, i=0, per=0):
                pe.wait_ge(w_split, q + 1 + per * i)

            def norm_tile(k, kt):
                n = KT * k + kt
                if kt == 0 and k > 0:
                    pe.wait_ge(rstd_ready, k)
                pe.wait_ge(sq_ready, n + 1)
                for t0, t1, b in segments(norm_ctx(k)):
                    mm = pe.matmul(aux[:, b, 0:t1 - t0], ones, sq[n % 2][:, t0:t1], start=kt == 0, stop=kt == KT - 1)
                mm.then_inc(sq_used, 1)

            def quad(a, i=0, per_g=0):
                g, w_, (place, load) = PLAN.quad[a], quad_weights(a), quad_place(a)
                pe.wait_ge(ada_landed[place], 16 * (load + 1) + (32 * i if per_g else 0))
                open_group(g, i, per_g)
                for j in range(4):
                    mm = pe.matmul(accs[slot(g)][32 * j:32 * j + 32, 0:512], cvec[:, 4 * (a % 2) + j, :],
                                   w_[:, 512 * j:512 * j + 512], start=True, stop=True)
                mm.then_inc(mm_done, 1)

            def turn(m, i=0, per_g=0):
                g = PLAN.turn[m]
                wait_evac(pe, PLAN.quad[2 * m + 1], i, per_g)
                open_group(g, i, per_g)
                for t in range(4):
                    mm = pe.matmul(accs[slot(g)][:, 2 * t:2 * t + 2], row[:, t * P:t * P + P],
                                   con[:, K_SEL:K_SEL + 2], start=True, stop=True)
                mm.then_inc(mm_done, 1)

            def project(l, n):
                at = PLAN.layers[l]
                g, q = at["proj_g"][n], at["q"] + n
                block_split(q)
                open_group(g)
                product(g, q, l < DEPTH - 1 or ORDER[n] in WITH_CTX, range(KT), h=2 * l if n == 0 else None)

            def gla_z(l):
                wait_evac(pe, proj_group(l, TLR))
                pe.wait_ge(small_in, 32 * (l + 1))
                pe.wait_ge(rstd_ready, 4 * l + 1)
                for d in range(2):
                    for t0, t1, b in segments(True):
                        mm = pe.matmul(aux[:, 2 * d + b, 0:t1 - t0], wa2[:, d * P:d * P + P],
                                       proj[0:32, TLR, t0:t1], start=True, stop=True)
                mm.then_inc(z_full, 1)

            def gla_values(l):
                for t in range(2):
                    wait_evac(pe, proj_group(l, TGV + t))
                pe.wait_ge(z_used, 2 * (l + 1))
                for b in range(6):
                    for t in range(2):
                        mm = pe.transpose(aux[:, b // 2, (b % 2) * 256 + t * P:(b % 2) * 256 + t * P + P],
                                          proj[:, TGV + t, b * P:b * P + P], ident)
                mm.then_inc(v_full, 1)

            def gla_keys(l):
                pe.wait_ge(kd_ready, l + 1)
                pe.wait_ge(v_ready, l + 1)
                for d in range(2):
                    for b in range(6):
                        n = 6 * d + b
                        mm = pe.transpose(aux[:, n // 4, (n % 4) * P:(n % 4) * P + P],
                                          pair[1][:, d, b * P:b * P + P], ident)
                mm.then_inc(kt_full, 1)

            def gla_updates(l):
                pe.wait_ge(kt_ready, l + 1)
                for d in range(2):
                    for c in range(NCH):
                        rows = slice((c % 2) * 64, (c % 2) * 64 + 64)
                        for h in range(GLA_H):
                            mm = pe.matmul(aux[h * DK:h * DK + DK, 2 * d + c % 2, (c // 2) * DV:(c // 2) * DV + DV],
                                           ktok[rows, d, c // 2, h * DK:h * DK + DK],
                                           vtok[rows, c // 2, h * DV:h * DV + DV], start=True, stop=True)
                mm.then_inc(u_full, 1)

            def gla_gram(l, n):
                pe.wait_ge(ab_ready, NGRAM * l + n + 1)
                if n == 0:
                    pe.wait_ge(states_ready, l + 1)
                else:
                    pe.wait_ge(gram_used, NGRAM * l + n)
                chunks = NCH if l < DEPTH - 1 else NX // CH
                for c in range(chunks):
                    for h in range(GLA_H):
                        rows, cols = slice(h * DK, h * DK + DK), slice(c * CH, c * CH + CH)
                        left = pair[n % 2][rows, 0, cols] if n else proj[rows, TGK, cols]
                        mm = pe.matmul(aux[(c % 2) * 64:(c % 2) * 64 + 64, h, (c // 2) * CH:(c // 2) * CH + CH],
                                       left, pair[n % 2][rows, 1, cols], start=True, stop=True)
                mm.then_inc(gram_full, 1)

            def gla_outputs(l):
                pe.wait_ge(gram_used, NGRAM * (l + 1))
                chunks = NCH if l < DEPTH - 1 else NX // CH
                for h in range(GLA_H):
                    for c in range(chunks):
                        o = aux[(h % 2) * DV:(h % 2) * DV + DV, 2 * (h // 2) + c % 2, (c // 2) * CH:(c // 2) * CH + CH]
                        rows, krows = slice((c % 2) * 64, (c % 2) * 64 + 64), slice(h * DK, h * DK + DK)
                        pe.matmul(o, vtok[rows, c // 2, h * DV:h * DV + DV], attg[rows, h, c // 2, :],
                                  start=True, stop=False)
                        for d in range(2):
                            mm = pe.matmul(o, state[krows, d, c, :], qdec[krows, d, c * CH:c * CH + CH],
                                           start=False, stop=d == 1)
                mm.then_inc(o_full, 1)

            def gla_norm_sum(l):
                pe.wait_ge(o_copied, l + 1)
                for t in range(2):
                    for t0, t1, b in segments(l < DEPTH - 1):
                        mm = pe.matmul(auxw[:, t, t0:t1], bones, pair[0][:, t, t0:t1], start=True, stop=True)
                mm.then_inc(o_sum, 1)

            def rotate(l, n, tile):
                if n == 0:
                    pe.wait_ge(o_rstd, l + 1)
                if n == 4:
                    pe.wait_ge(rot_used, 5 * l + 4)
                pe.matmul(aux[:, min(n, 3), :], rot, proj[:, tile, 0:NX], start=True, stop=True).then_inc(rot_full, 1)

            def attention_values(l):
                pe.wait_ge(rot_used, 5 * l + 3)
                for b in range(6):
                    mm = pe.transpose(aux[:, 1 + b // 4, (b % 4) * P:(b % 4) * P + P], proj[:, TV, b * P:b * P + P], ident)
                mm.then_inc(va_full, 1)

            def pool_mix(l):
                for t in range(2):
                    g = PLAN.layers[l]["gate_g"] + t
                    pe.wait_ge(pool_d, 2 * l + t + 1)
                    open_group(g)
                    for t0, t1, _ in segments(l < DEPTH - 1):
                        mm = pe.matmul(accs[slot(g)][:, t0:t1], poolw[:, t * P:t * P + P], proj[:, TPOOL + t, t0:t1],
                                       start=True, stop=True)
                    mm.then_inc(mm_done, 1)

            def scores(l, u, r):
                qb, g = units(l)[u]
                n, rows = head_base[l] + 4 * u + r, slice(g * HD, g * HD + HD)
                blocks = local_blocks(qb)
                if n > head_base[l]:
                    pe.wait_ge(s_ctx, n)
                if blocks and u + r > 0:
                    pe.wait_ge(s_local, lhead_base[l] + 4 * u + r)
                if u == 0:
                    pe.wait_ge(rope_done, 5 * l + 2 + r)
                    if r == 0:
                        pe.wait_ge(va_ready, l + 1)
                lhs = proj[rows, r, qb * P:qb * P + P]
                if blocks:
                    pe.matmul(aux[:, 0, 0:P * len(blocks)], lhs, proj[rows, TK, P * blocks[0]:P * blocks[-1] + P],
                              start=True, stop=True)
                pe.matmul(aux[:, 1, 0:NC], lhs, proj[rows, TK, NX:T], start=True, stop=True).then_inc(s_full, 1)

            def turn_probs(l, u, b):
                n = block_index(l, u, b)
                if b == 0:
                    pe.wait_ge(p_ready, unit_base[l] + u + 1)
                if n > blk_base[l]:
                    pe.wait_ge(pt_ready, n)
                for r in range(4):
                    mm = pe.transpose(aux[:, 2, r * P:r * P + P], sco[u % 2][:, r, b * P:b * P + P], ident)
                mm.then_inc(pt_full, 1)

            def attend(l, u, b):
                n, g = block_index(l, u, b), units(l)[u][1]
                blocks = key_blocks(l, u)
                pe.wait_ge(pt_ready, n + 1)
                if b == 0 and unit_base[l] + u >= 2:
                    pe.wait_ge(pv_used, unit_base[l] + u - 1)
                mm = pe.matmul(aux[g * HD:g * HD + HD, 3, :], vat[:, blocks[b], g * HD:g * HD + HD], ptb[n % 2],
                               start=b == 0, stop=b == len(blocks) - 1)
                if b == len(blocks) - 1:
                    mm.then_inc(pv_full, 1)

            def gate_piece(l, j, i):
                at, ctx = PLAN.layers[l], l < DEPTH - 1
                q, b = at["gate_q"] + 2 * j, at["gate_b"] + j // 2
                if i == 0:
                    block_split(q)
                    open_group(gate_group(l, j, 0))
                    product(gate_group(l, j, 0), q, ctx, range(0, 4), last=False)
                elif i == 1:
                    product(gate_group(l, j, 0), q, ctx, range(4, 8), first=False)
                elif i == 2:
                    if j == 0:
                        wait_evac(pe, at["gate_g"])
                        wait_evac(pe, at["gate_g"] + 1)
                    pe.wait_ge(b_landed[b % 2], 16 * (b // 2 + 1))
                    project_branch(gate_group(l, j, 1), b, j % 2, (0, 1), 4, ctx)
                    block_split(q + 1)
                    open_group(gate_group(l, j, 2))
                    product(gate_group(l, j, 2), q + 1, ctx, range(0, 4), last=False)
                elif i == 3:
                    product(gate_group(l, j, 2), q + 1, ctx, range(4, 8), first=False)
                else:
                    if j == 0:
                        pe.wait_ge(gla_out, l + 1)
                    project_branch(gate_group(l, j, 3), b, j % 2, (2, 3), 4, ctx)

            def project_branch(g, b, jj, ks, tile0, ctx):
                open_group(g)
                for n, k in enumerate(ks):
                    for t0, t1, _ in segments(ctx):
                        mm = pe.matmul(accs[slot(g)][:, t0:t1], brw[:, b % 2, jj, k, :], bt[:, tile0 + k, t0:t1],
                                       start=n == 0, stop=n == len(ks) - 1)
                mm.then_inc(mm_done, 1)

            def down(l, g, q, par_, ctx, ready, i=0, per_g=0, per_q=0, per_t=0, norm=None):
                pe.wait_ge(g_ready, ready + per_t * i)
                for m in range(KT):
                    half = m // 4
                    if m % 4 == 0:
                        block_split(q + half, i, per_q)
                    s = (q + half) % SPL
                    gg = g + m
                    open_group(gg, i, per_g)
                    for kk in range(2):
                        for w_, a_ in ((whi, 0), (whi, 1), (wlo, 0)):
                            for t0, t1, _ in segments(ctx):
                                c0 = kk * 512 + (m % 4) * P
                                mm = pe.matmul(accs[slot(gg)][:, t0:t1], w_[:, s, c0:c0 + P],
                                               gact[:, par_, kk, a_, t0:t1], start=kk == 0 and w_ is whi and a_ == 0,
                                               stop=kk == 1 and w_ is wlo)
                    mm.then_inc(mm_done, 1)
                    if norm is not None and m >= 2:
                        norm_tile(norm, m - 2)
                if norm is not None:
                    norm_tile(norm, KT - 2)
                    norm_tile(norm, KT - 1)

            def ups(l, g, q, ctx, i=0, per_g=0, per_q=0, h=None, unit=None):
                for n in range(4):
                    block_split(q + n, i, per_q)
                    gg = g + UP_GROUPS[unit is not None][n]
                    open_group(gg, i, per_g)
                    product(gg, q + n, ctx, range(KT), h=h if n == 0 else None)
                    if unit is not None and n in (0, 2):
                        quad(2 * unit + n // 2, i, per_g)
                if unit is not None:
                    turn(unit, i, per_g)

            pe.wait_ge(cvec_ready, 1)
            for m in range(FIRST_UNITS):
                if m == FIRST_UNITS - 1:
                    pe.wait_ge(sq_used, KT - 1)
                    for t0, t1, b in segments(True):
                        mm = pe.matmul(aux[:, b, 0:t1 - t0], ones, sq_sum[:, t0:t1], start=True, stop=True)
                    mm.then_inc(sq_used, 1)
                quad(2 * m)
                quad(2 * m + 1)
                turn(m)
            for l, at in enumerate(PLAN.layers):
                ctx = l < DEPTH - 1
                for n in range(len(ORDER) + 1):
                    if l == 0:
                        if late_turns(n) is not None:
                            turn(late_turns(n))
                        quad(LATE_QUAD + n)
                    if n == STEP_Z:
                        gla_z(l)
                    elif n == STEP_V:
                        gla_values(l)
                    elif n == STEP_KEYS:
                        gla_keys(l)
                    elif n == STEP_STATE:
                        gla_updates(l)
                    elif n >= STEP_GRAM and n - STEP_GRAM < NGRAM:
                        gla_gram(l, n - STEP_GRAM)
                    if n < len(ORDER):
                        project(l, n)
                if l == 0:
                    turn(FIRST_UNITS + 7)
                pool_mix(l)
                gla_outputs(l)
                gate_piece(l, 0, 0)
                gla_norm_sum(l)
                gate_piece(l, 0, 1)
                for n, tile in enumerate((TK, 0, 1, 2)):
                    rotate(l, n, tile)
                gate_piece(l, 0, 2)
                attention_values(l)
                rotate(l, 4, 3)
                gate_piece(l, 0, 3)
                us = units(l)
                for u in range(len(us) + 1):
                    blocks = len(key_blocks(l, u - 1)) if u else 0
                    for i in range(STEPS):
                        if u < len(us) and i < 4:
                            scores(l, u, i)
                        if u < len(us):
                            for j, f in pieces(len(us), u, i):
                                gate_piece(l, j, f)
                        elif i < 4:
                            if i == 0:
                                block_split(at["mix_q"])
                                open_group(at["mix_g"])
                            product(at["mix_g"], at["mix_q"], ctx, (2 * i, 2 * i + 1), first=i == 0, last=i == 3)
                        if 0 < i <= blocks:
                            turn_probs(l, u - 1, i - 1)
                        if 1 < i <= blocks + 1:
                            attend(l, u - 1, i - 2)
                g, q = at["mix_g"], at["mix_q"]
                for c in range(KT // 2 + 1):
                    if c < KT // 2:
                        b = at["mix_b"] + c
                        for jj in range(2):
                            if c + jj > 0:
                                block_split(q)
                                open_group(g)
                                product(g, q, ctx, range(KT))
                            if c == 0 and jj == 0:
                                pe.wait_ge(pv_used, unit_base[l + 1])
                            if jj == 0:
                                pe.wait_ge(b_landed[b % 2], 16 * (b // 2 + 1))
                            project_branch(g + 1, b, jj, range(4), 0, ctx)
                            g, q = g + 2, q + 1
                    if c > 0:
                        down(l, g, q, (c - 1) % 2, ctx, g_count(l, "mix", 2 * c),
                             norm=4 * l + 1 if c == KT // 2 else None)
                        g, q = g + 8, q + 2
                for kt in range(KT):
                    norm_tile(4 * l + 2, kt)
                g, q, up_n = at["ffn_g"], at["ffn_q"], UP_COUNT[l == 0]
                pg, pq, unit = 2 * (up_n + KT), FFN_BODY_Q, UNITS if l == 0 else None
                ups(l, g, q, ctx, h=2 * l + 1, unit=unit)
                g, q = g + up_n, q + 4
                with pe.Fori(0, FFN_LOOPS) as i:
                    ups(l, g, q, ctx, i, pg, pq, unit=unit and unit + 1)
                    down(l, g + up_n, q + 4, 0, ctx, g_count(l, "ffn", 2), i, pg, pq, 4)
                    ups(l, g + up_n + KT, q + 6, ctx, i, pg, pq, unit=unit and unit + 2)
                    down(l, g + 2 * up_n + KT, q + 10, 1, ctx, g_count(l, "ffn", 4), i, pg, pq, 4)
                if l == 0:
                    quad(4 * UNITS - 2)
                    quad(4 * UNITS - 1)
                    turn(2 * UNITS - 1)
                down(l, at["down_g"], q + pq * FFN_LOOPS, 0, ctx, g_count(l, "ffn", NFF), norm=4 * l + 3)
                if l + 1 < DEPTH:
                    for kt in range(KT):
                        norm_tile(4 * l + 4, kt)

        @block.scalar
        def _(act):
            link = Chain(act, act_link)

            def split(q, i=0, per_q=0, per_g=0):
                if q >= PLAN.blocks:
                    return
                act.wait_ge(w_landed[q % RAW], 16 * (q // RAW + 1) + 16 * (per_q // RAW) * i)
                if q >= SPL:
                    act.wait_ge(mm_done, PLAN.group_end[q - SPL] + per_g * i)
                act.activation(whi[:, q % SPL, :], raw[:, q % RAW, :], ACT.Copy).then_inc(w_hi, 1)

            def squares(k):
                w = T if norm_ctx(k) else NX
                for kt in range(KT):
                    n = KT * k + kt
                    if kt == KT - 2:
                        act.activation(warm[:, 0:1], eps[:, 0:1], ACT.Ln)
                    norm_source_ready(act, k, kt)
                    if n >= 2:
                        act.wait_ge(sq_used, n - 1 if k else max(n - 2, 1))
                    source = x if k % 2 == 0 else y
                    act.activation(sq[n % 2][:, 0:w], source[:, kt, 0:w], ACT.Square).then_inc(sq_ready, 1)

            def inverse_root(k):
                w = T if norm_ctx(k) else NX
                act.wait_ge(sq_used, KT * (k + 1))
                link(act.activation(rstd[:, 0:w], auxw[:, 0, 0:w], ACT.Ln, bias=eps[:, 0:1], scale=1.0 / D))
                act.activation(rstd[:, 0:w], rstd[:, 0:w], ACT.Exp, scale=-0.5).then_inc(rstd_ready, 1)

            def heads(l, n, scale, shift, ctx):
                w = T if ctx else NX
                for kt in range(KT):
                    act.wait_ge(t_ready[kt % 2], KT // 2 * n + kt // 2 + 1)
                    if kt % 2 == 0:
                        for t0, t1, s in segments(ctx):
                            ins = act.activation(hhi[:, kt, t0:t1], mod[kt % 4][:, t0:t1], ACT.Identity,
                                                 bias=ada[:, l, shift + kt, s:s + 1])
                    else:
                        for t0, t1, s in segments(ctx):
                            ins = act.activation(mod[kt % 4][:, t0:t1], mod[kt % 4][:, t0:t1], ACT.Identity,
                                                 bias=ada[:, l, shift + kt, s:s + 1], scale=ada[:, l, scale + kt, s:s + 1])
                        link(ins)
                        ins = act.activation(hhi[:, kt, 0:w], mod[kt % 4][:, 0:w], ACT.Copy)
                    ins.then_inc(h_hi, 1)

            def read_projection(l, tile, g):
                w = T if l < DEPTH - 1 or tile in WITH_CTX else NX
                act.wait_ge(mm_done, g + 1)
                act.activation(proj[:, tile, 0:w], accs[slot(g)][:, 0:w], ACT.Copy,
                               scale=DK ** -0.5 if tile == TGQ else 1.0).then_inc(acc_free[slot(g)], 1)

            def pair_exp(l, n):
                w = T if l < DEPTH - 1 else NX
                act.wait_ge(e_args, len(LEVELS) * l + n)
                act.activation(pair[n % 2][:, :, 0:w], pair[n % 2][:, :, 0:w], ACT.Exp,
                               scale=1.0 / TAU).then_inc(e_exp, 1)

            def gla_step(l, n):
                w = T if l < DEPTH - 1 else NX
                if n == STEP_Z:
                    act.wait_ge(z_full, l + 1)
                    for d in range(2):
                        ins = act.activation(pair[0][:, d, :], auxw[:, d, 0:T], ACT.Abs,
                                             bias=par[:, l, C_BA + d:C_BA + d + 1])
                    ins.then_inc(z_used, 1)
                    act.wait_ge(z_used, 2 * l + 1)
                    link(act.activation(pair[0], pair[0], ACT.Exp, scale=-1.0))
                    act.activation(pair[0], pair[0], ACT.Ln, bias=1.0).then_inc(z_log, 1)
                elif n == STEP_V:
                    act.wait_ge(v_full, l + 1)
                    act.activation(vtok.rearrange("p b n -> p (b n)"), aux_flat[:, 0:1536], ACT.Copy).then_inc(v_ready, 1)
                    act.wait_ge(cum_ready, l + 1)
                    act.activation(qdec[:, 0, 0:w], cumf[:, 0:w], ACT.Exp, scale=1.0 / TAU)
                    act.activation(qdec[:, 1, 0:w], cumb[:, 0:w], ACT.Exp, scale=1.0 / TAU)
                    act.activation(dec[:, 0, :], cumf[:, CH - 1::CH], ACT.Exp, scale=1.0 / TAU)
                    act.activation(dec[:, 1, :], cumb[:, 0::CH], ACT.Exp, scale=1.0 / TAU)
                elif n == STEP_KD:
                    act.wait_ge(kd_args, l + 1)
                    act.activation(pair[1], pair[1], ACT.Exp, scale=1.0 / TAU).then_inc(kd_exp, 1)
                elif n == STEP_KEYS:
                    act.wait_ge(kt_full, l + 1)
                    act.activation(ktok.rearrange("p d b n -> p (d b n)"), aux_flat[:, 0:1536],
                                   ACT.Copy).then_inc(kt_ready, 1)
                if STEP_STATE <= n < STEP_STATE + len(LEVELS):
                    pair_exp(l, n - STEP_STATE + 1)

            def gla_finish(l):
                w = T if l < DEPTH - 1 else NX
                act.wait_ge(o_full, l + 1)
                if l == 0:
                    act.wait_ge(mm_done, PLAN.turn[FIRST_UNITS + 7] + 1)
                for t in range(2):
                    o = aux[:, 2 * t:2 * t + 2, 0:w // 2].rearrange("p s (c i) -> p s c i", i=CH)
                    for func, dst in ((ACT.Copy, bt[:, 6 + t, 0:w]), (ACT.Square, pair[0][:, t, 0:w])):
                        ins = act.activation(dst.rearrange("p (c s i) -> p s c i", s=2, i=CH), o, func)
                ins.then_inc(o_copied, 1)
                act.wait_ge(o_sum, l + 1)
                link(act.activation(pair[1][:, :, 0:w], auxw[:, :, 0:w], ACT.Ln, bias=eps[:, 0:1], scale=1.0 / DV))
                act.activation(pair[1][:, :, 0:w], pair[1][:, :, 0:w], ACT.Exp, scale=-0.5).then_inc(o_rstd, 1)

            def gla_gate(l):
                w = T if l < DEPTH - 1 else NX
                act.activation(proj[:, TGR:TGR + 2, 0:w], proj[:, TGR:TGR + 2, 0:w], ACT.Silu).then_inc(r_silu, 1)

            def unit_scores(l, u, r):
                n, nl = head_base[l] + 4 * u + r, P * (len(key_blocks(l, u)) - 2)
                act.wait_ge(s_full, n + 1)
                if r == 0:
                    if u == 0:
                        act.wait_ge(gla_out, l + 1)
                    elif u > 1:
                        act.wait_ge(pt_full, block_index(l, u - 1, 0))
                act.activation(sco[u % 2][:, r, nl:nl + NC], aux[:, 1, 0:NC], ACT.Copy, scale=HD ** -0.5).then_inc(s_ctx, 1)

            def unit_exp(l, u, half):
                b, nk = u % 2, P * len(key_blocks(l, u))
                if half == 0:
                    act.wait_ge(m_ready, unit_base[l] + u + 1)
                for r in (2 * half, 2 * half + 1):
                    act.activation(sco[b][:, r, 0:nk], sco[b][:, r, 0:nk], ACT.Exp, bias=small[:, b, 4 + r:5 + r],
                                   accum_out=small[:, b, 16 + r:17 + r])
                if half == 1:
                    act.activation(small[:, b, 12:16], small[:, b, 8:12], ACT.Exp).then_inc(p_exp, 1)

            def read_gate(g, dst, before):
                act.wait_ge(mm_done, g + 1)
                if before is not None:
                    wait_evac(act, before)
                act.activation(dst, accs[slot(g)][:, 0:dst.shape[-1]], ACT.Tanh, scale=0.5).then_inc(acc_free[slot(g)], 1)

            def chunk_head(n, par_, jj, w, src, scale, per=0, i=0):
                act.wait_ge(g_val, n + per * i)
                act.activation(gact[:, par_, jj, 0, 0:w], src[:, 0:w], ACT.Copy, scale=scale).then_inc(g_hi, 1)

            def read_quad(a, i=0, per_g=0):
                g = PLAN.quad[a]
                act.wait_ge(mm_done, g + 1 + per_g * i)
                act.activation(row, accs[slot(g)][:, 0:512], ACT.Copy).then_inc(acc_free[slot(g)], 1)

            def ups(l, c, g, q, par_, w, i=0, per_g=0, per_q=0, per_t=0, unit=None):
                for n in range(4):
                    kk, dst = n // 2, (conv_a, conv_g)[n % 2][n // 2]
                    f = (2 * c + kk) + NFF * (n % 2)
                    gg = g + UP_GROUPS[unit is not None][n]
                    act.wait_ge(mm_done, gg + 1 + per_g * i)
                    if not (c == 0 and per_t == 0):
                        act.wait_ge(g_ready, g_count(l, "ffn", 2 * c - 1 + kk) + per_t * i)
                    source = accs[slot(gg)]
                    if n == 3:
                        act.activation(late_u[:, 0:w], source[:, 0:w], ACT.Copy).then_inc(acc_free[slot(gg)], 1)
                        wait_evac(act, gg, i, per_g)
                        source = late_u
                    act.activation(dst[:, 0:w], source[:, 0:w], ACT.Identity,
                                   bias=par[:, l, bass.ds(C_CB + f + per_t * i, 1)],
                                   scale=par[:, l, bass.ds(C_CW + 2 * NFF + f + per_t * i, 1)]).then_inc(conv_mid, 1)
                    split(q + n + SPL, i, per_q, per_g)
                    if unit is not None and n == 0:
                        read_quad(2 * unit, i, per_g)
                    if n % 2:
                        if n == 1:
                            wait_evac(act, gg, i, per_g)
                        else:
                            act.wait_ge(taps_added, NFF // 2 * l + c + 1 + per_t // 2 * i)
                        act.activation(conv_g[kk][:, 0:w], conv_g[kk][:, 0:w], ACT.Silu).then_inc(silu_ready, 1)
                        if n == 1:
                            chunk_head(g_count(l, "ffn", 2 * c + 1), par_, 0, w, conv_a[0], 1.0, per_t, i)

            def read_gate_piece(l, j, f, w):
                if f == 1:
                    read_gate(gate_group(l, j, 0), gates[0][:, 0:w], gate_group(l, j - 1, 1) if j else None)
                    split(PLAN.layers[l]["gate_q"] + 2 * j + SPL)
                if f == 3:
                    read_gate(gate_group(l, j, 2), gates[1][:, 0:w], gate_group(l, j - 1, 3) if j else None)
                    split(PLAN.layers[l]["gate_q"] + 2 * j + 1 + SPL)

            act.wait_ge(consts_in, 16 * 4)
            act.activation(cvec[:, :, :], cvec[:, :, :], ACT.Silu).then_inc(cvec_ready, 1)
            act.wait_ge(eps_set, 1)
            for m in range(FIRST_UNITS):
                if m == 1:
                    squares(0)
                read_quad(2 * m)
            inverse_root(0)
            for l, at in enumerate(PLAN.layers):
                ctx = l < DEPTH - 1
                w = T if ctx else NX
                if l == 0:
                    split(0)
                    split(1)
                heads(l, 2 * l, SC1, SH1, True)
                if l > 0:
                    act.wait_ge(x_spilled, 16 * l)
                for n in range(len(ORDER) + 1):
                    if l == 0 and n % 2 == 0:
                        read_quad(LATE_QUAD + n)
                    gla_step(l, n)
                    if n < len(ORDER):
                        read_projection(l, ORDER[n], at["proj_g"][n])
                        split(at["q"] + n + SPL)
                act.wait_ge(pool_d, 2 * (l + 1))
                for t in range(2):
                    g = at["gate_g"] + t
                    act.wait_ge(mm_done, g + 1)
                    act.activation(bt[:, 4 + t, 0:w], accs[slot(g)][:, 0:w], ACT.Copy,
                                   scale=par[:, l, C_PSC + t:C_PSC + t + 1]).then_inc(acc_free[slot(g)], 1)
                gla_finish(l)
                gla_gate(l)
                read_gate_piece(l, 0, 1, w)
                act.wait_ge(va_full, l + 1)
                act.activation(vat.rearrange("p b n -> p (b n)"), aux_flat[:, 512:1280], ACT.Copy).then_inc(va_ready, 1)
                read_gate_piece(l, 0, 3, w)
                us = units(l)
                for u in range(len(us) + 1):
                    for i in range(STEPS):
                        if u < len(us) and i < 4:
                            unit_scores(l, u, i)
                        if u > 0 and 0 < i <= len(key_blocks(l, u - 1)):
                            n = block_index(l, u - 1, i - 1)
                            if u == 1 and i <= 2:
                                act.wait_ge(rope_done, 5 * (l + 1))
                            act.wait_ge(pt_full, n + 1)
                            act.activation(ptb[n % 2], aux[:, 2, :], ACT.Copy).then_inc(pt_ready, 1)
                        if u < len(us):
                            if i in (4, 5):
                                unit_exp(l, u, i - 4)
                            for j, f in pieces(len(us), u, i):
                                read_gate_piece(l, j, f, w)
                g, q = at["mix_g"], at["mix_q"]
                for c in range(KT // 2 + 1):
                    if c < KT // 2:
                        for jj in range(2):
                            before = (g + 1 - 4 - (8 if c > 1 else 0)) if c else None
                            read_gate(g, mgate[jj][:, 0:w], before)
                            split(q + SPL)
                            chunk_head(g_count(l, "mix", 2 * c + jj + 1), c % 2, jj, w, part[:, 2 * c + jj, :], 0.5)
                            g, q = g + 2, q + 1
                    if c == KT // 2:
                        squares(4 * l + 1)
                        inverse_root(4 * l + 1)
                    if c > 0:
                        split(q + SPL)
                        split(q + 1 + SPL)
                        g, q = g + 8, q + 2
                squares(4 * l + 2)
                inverse_root(4 * l + 2)
                heads(l, 2 * l + 1, SC2, SH2, ctx)
                g, q, up_n = at["ffn_g"], at["ffn_q"], UP_COUNT[l == 0]
                pg, pq, unit = 2 * (up_n + KT), FFN_BODY_Q, UNITS if l == 0 else None
                ups(l, 0, g, q, 0, w, unit=unit)
                chunk_head(g_count(l, "ffn", 2), 0, 1, w, conv_a[1], 1.0)
                g, q = g + up_n, q + 4
                with act.Fori(0, FFN_LOOPS) as i:
                    ups(l, 1, g, q, 1, w, i, pg, pq, 4, unit=unit and unit + 1)
                    split(q + 4 + SPL, i, pq, pg)
                    chunk_head(g_count(l, "ffn", 4), 1, 1, w, conv_a[1], 1.0, 4, i)
                    split(q + 5 + SPL, i, pq, pg)
                    ups(l, 2, g + up_n + KT, q + 6, 0, w, i, pg, pq, 4, unit=unit and unit + 2)
                    split(q + 10 + SPL, i, pq, pg)
                    chunk_head(g_count(l, "ffn", 6), 0, 1, w, conv_a[1], 1.0, 4, i)
                    split(q + 11 + SPL, i, pq, pg)
                q += FFN_BODY_Q * FFN_LOOPS
                if l == 0:
                    read_quad(4 * UNITS - 2)
                squares(4 * l + 3)
                inverse_root(4 * l + 3)
                split(q + SPL)
                split(q + 1 + SPL)
                if l + 1 < DEPTH:
                    squares(4 * l + 4)
                    inverse_root(4 * l + 4)

        @block.vector
        def _(v):
            link = Chain(v, dve_link)

            def rest(q, i=0, per_q=0):
                if q >= PLAN.blocks:
                    return
                v.wait_ge(w_hi, q + 1 + per_q * i)
                v.tensor_tensor(wlo[:, q % SPL, :], raw[:, q % RAW, :], whi[:, q % SPL, :].bitcast(F32),
                                ALU.subtract).then_inc(w_split, 1)

            def modulate(l, n, k, post, scale, shift, ctx):
                v.wait_ge(rstd_ready, k + 1)
                w = T if ctx else NX
                for kt in range(KT + 1):
                    if kt < KT and kt % 2 == 0:
                        x_valid(v, l, post, kt)
                        if kt >= 4:
                            v.wait_ge(h_ready, KT * n + kt - 3)
                        for t0, t1, s in segments(ctx):
                            ins = v.scalar_tensor_tensor(mod[kt % 4][:, t0:t1], x[:, kt, t0:t1],
                                                         ada[:, l, scale + kt, s:s + 1], rstd[:, t0:t1], ALU.mult, ALU.mult)
                        ins.then_inc(t_ready[0], 1)
                    j = kt - 1
                    if j >= 0:
                        v.wait_ge(h_hi, KT * n + j + 1)
                    if j >= 0 and j % 2 == 0:
                        for t0, t1, s in segments(ctx):
                            ins = v.scalar_tensor_tensor(hlo[:, j, t0:t1], mod[j % 4][:, t0:t1],
                                                         ada[:, l, shift + j, s:s + 1], hhi[:, j, t0:t1].bitcast(F32),
                                                         ALU.add, ALU.subtract)
                        ins.then_inc(h_ready, 1)
                    elif j >= 0:
                        v.tensor_tensor(hlo[:, j, 0:w], mod[j % 4][:, 0:w], hhi[:, j, 0:w].bitcast(F32),
                                        ALU.subtract).then_inc(h_ready, 1)

            def residual(l, k, gate, ctx):
                v.wait_ge(rstd_ready, k + 1)
                w, n = T if ctx else NX, k // 2
                if k % 4 == 1:
                    v.wait_ge(x_in, 16 * (l + 2))
                for kt in range(KT + 1):
                    if kt < KT:
                        if kt >= 2:
                            x_valid(v, l, n + 1, kt - 2)
                        for t0, t1, s in segments(ctx):
                            ins = v.scalar_tensor_tensor(tmp[kt % 2][:, t0:t1], y[:, kt, t0:t1],
                                                         ada[:, l, gate + kt, s:s + 1], rstd[:, t0:t1], ALU.mult, ALU.mult)
                        ins.then_inc(y_scaled, 1)
                    j = kt - 1
                    if j >= 0 and j % 2 == 0:
                        v.wait_ge(y_scaled, KT * n + j + 1)
                        v.tensor_tensor(x[:, j, 0:w], x[:, j, 0:w], tmp[0][:, 0:w], ALU.add).then_inc(x_ready[0], 1)

            def halves(ap, width, half, w):
                a = ap[:, 0:w].rearrange("p (n s i) -> p n s i", s=2, i=half)
                return a[:, :, 0, :], a[:, :, 1, :]

            def pair_args(l, n):
                half, w = LEVELS[n - 1], T if l < DEPTH - 1 else NX
                fl, fr = halves(cumf, T, half, w)
                bl, br = halves(cumb, T, half, w)
                al, ar = halves(pair[n % 2][:, 0, :], T, half, w)
                ql, qr = halves(pair[n % 2][:, 1, :], T, half, w)
                shape = list(fl.shape)
                edge_f = fl[:, :, half - 1:half].broadcast_to(shape)
                edge_b = br[:, :, 0:1].broadcast_to(shape)
                v.tensor_tensor(al, edge_f, fl, ALU.subtract)
                v.tensor_tensor(ar, edge_b, br, ALU.subtract)
                v.tensor_tensor(qr, fr, edge_f, ALU.subtract)
                v.tensor_tensor(ql, bl, edge_b, ALU.subtract).then_inc(e_args, 1)

            def pair_scale(l, n):
                w = T if l < DEPTH - 1 else NX
                v.wait_ge(e_exp, len(LEVELS) * l + n)
                v.tensor_tensor(pair[n % 2][:, 0, 0:w], pair[n % 2][:, 0, 0:w], proj[:, TGK, 0:w], ALU.mult)
                v.tensor_tensor(pair[n % 2][:, 1, 0:w], pair[n % 2][:, 1, 0:w], proj[:, TGQ, 0:w],
                                ALU.mult).then_inc(ab_ready, 1)

            def take_level(l, n):
                cc = NCH // 2 if l < DEPTH - 1 else NX // CH // 2
                v.wait_ge(gram_full, NGRAM * l + n + 1)
                if n:
                    v.wait_ge(gram_used, NGRAM * l + n)
                mask = gmask[:, n, :].rearrange("p (a b i) -> p a b i", a=1, b=1).broadcast_to([P, GLA_H, cc, CH])
                v.copy_predicated(attg[:, :, 0:cc, :], mask,
                                  aux[:, :, 0:cc * CH].rearrange("p h (c i) -> p h c i", i=CH)).then_inc(gram_used, 1)

            def gla_step(l, n):
                w = T if l < DEPTH - 1 else NX
                if n == STEP_Z:
                    v.wait_ge(z_used, 2 * l + 1)
                    for d in range(2):
                        ins = v.tensor_scalar(pair[1][:, d, :], auxw[:, d, 0:T], par[:, l, C_BA + d:C_BA + d + 1], 0.0,
                                              ALU.add, ALU.min)
                    ins.then_inc(z_used, 1)
                    v.wait_ge(z_used, 2 * (l + 1))
                    v.wait_ge(z_log, l + 1)
                    link(v.tensor_tensor(pair[0], pair[1], pair[0], ALU.subtract))
                    v.wait_ge(scanm_in, 16 * (l + 1))
                    v.tensor_tensor_scan(cumf, scanm, pair[0][:, 0, :], 0.0, ALU.mult, ALU.add)
                    v.tensor_tensor_scan(cumb[:, ::-1], scanm, pair[0][:, 1, ::-1], 0.0, ALU.mult,
                                         ALU.add).then_inc(cum_ready, 1)
                    v.wait_ge(cum_ready, l + 1)
                    cf, cb = (a.rearrange("p (c i) -> p c i", i=CH) for a in (cumf, cumb))
                    kf, kb = (pair[1][:, d, :].rearrange("p (c i) -> p c i", i=CH) for d in range(2))
                    v.tensor_tensor(kf, cf[:, :, CH - 1:CH].broadcast_to([P, NCH, CH]), cf, ALU.subtract)
                    v.tensor_tensor(kb, cb[:, :, 0:1].broadcast_to([P, NCH, CH]), cb, ALU.subtract).then_inc(kd_args, 1)
                elif n == STEP_KD:
                    wait_evac(v, proj_group(l, TGK))
                    v.wait_ge(kd_exp, l + 1)
                    v.tensor_tensor(pair[1][:, 0, :], pair[1][:, 0, :], proj[:, TGK, :], ALU.mult)
                    v.tensor_tensor(pair[1][:, 1, :], pair[1][:, 1, :], proj[:, TGK, :], ALU.mult).then_inc(kd_ready, 1)
                elif n == STEP_KEYS:
                    wait_evac(v, proj_group(l, TGQ))
                    v.tensor_scalar(pair[0][:, 1, 0:w], proj[:, TGQ, 0:w], 2.0, None, ALU.mult).then_inc(ab_ready, 1)
                    for d in range(2):
                        v.tensor_tensor(qdec[:, d, 0:w], qdec[:, d, 0:w], proj[:, TGQ, 0:w], ALU.mult)
                elif n == STEP_STATE:
                    v.wait_ge(kt_full, l + 1)
                    pair_args(l, 1)
                    orders = ([8, 9, 10, 11] + list(range(8)), [11, 10, 9, 8] + list(range(7, -1, -1)))
                    for order, d in zip(orders, range(2)):
                        ins = v.memset(state[:, d, order[0], :], 0.0)
                    link(ins)
                    v.wait_ge(u_full, l + 1)
                    for m in range(NCH - 1):
                        for d in range(2):
                            a, b = orders[d][m], orders[d][m + 1]
                            ins = v.scalar_tensor_tensor(state[:, d, b, :], state[:, d, a, :], dec[:, d, a:a + 1],
                                                         aux[:, 2 * d + a % 2, (a // 2) * DV:(a // 2) * DV + DV],
                                                         ALU.mult, ALU.add)
                        if m < NCH - 2:
                            link(ins)
                    ins.then_inc(states_ready, 1)
                    pair_scale(l, 1)
                elif STEP_GRAM <= n < STEP_GRAM + NGRAM:
                    m = n - STEP_GRAM
                    take_level(l, m)
                    if m + 2 < NGRAM:
                        pair_args(l, m + 2)
                        pair_scale(l, m + 2)

            def gla_finish(l):
                w = T if l < DEPTH - 1 else NX
                v.wait_ge(o_rstd, l + 1)
                link(v.tensor_tensor(bt[:, 6:8, 0:w], bt[:, 6:8, 0:w], pair[1][:, :, 0:w], ALU.mult))
                v.wait_ge(r_silu, l + 1)
                for t in range(2):
                    ins = v.scalar_tensor_tensor(bt[:, 6 + t, 0:w], bt[:, 6 + t, 0:w], par[:, l, C_GN + t:C_GN + t + 1],
                                                 proj[:, TGR + t, 0:w], ALU.mult, ALU.mult)
                ins.then_inc(gla_out, 1)

            def rope(l):
                v.wait_ge(tables_in, 32 * (l + 1))
                for n, tile in enumerate((TK, 0, 1, 2, 3)):
                    v.wait_ge(rot_full, 5 * l + n + 1)
                    if n > 0:
                        v.wait_ge(rope_done, 5 * l + n)
                    v.tensor_tensor(gtmp[:, 0:NX], aux[:, min(n, 3), :], ropes, ALU.mult).then_inc(rot_used, 1)
                    link(v.tensor_tensor(proj[:, tile, 0:NX], proj[:, tile, 0:NX], ropec, ALU.mult))
                    v.wait_ge(rot_used, 5 * l + n + 1)
                    v.tensor_tensor(proj[:, tile, 0:NX], proj[:, tile, 0:NX], gtmp[:, 0:NX], ALU.add).then_inc(rope_done, 1)

            def unit_scores(l, u, r):
                qb, _ = units(l)[u]
                nl = P * len(local_blocks(qb))
                if nl:
                    n = head_base[l] + 4 * u + r
                    v.wait_ge(s_full, n + 1)
                    if r == 0 and u > 1:
                        v.wait_ge(pt_full, block_index(l, u - 1, 0))
                    m0 = 0 if qb > 0 else P
                    v.scalar_tensor_tensor(sco[u % 2][:, r, 0:nl], aux[:, 0, 0:nl], HD ** -0.5, amask[:, m0:m0 + nl],
                                           ALU.mult, ALU.add).then_inc(s_local, 1)

            def head_max(l, u, r):
                b, nk, qb = u % 2, P * len(key_blocks(l, u)), units(l)[u][0]
                v.wait_ge(s_ctx, head_base[l] + 4 * u + r + 1)
                if qb < 4:
                    v.wait_ge(s_local, lhead_base[l] + 4 * u + r + 1)
                return v.tensor_reduce(small[:, b, r:r + 1], sco[b][:, r, 0:nk], AX_X, ALU.max)

            def unit_max(l, u):
                b, g = u % 2, units(l)[u][1]
                sink = par[:, l, C_SINK + 4 * g:C_SINK + 4 * g + 4]
                link(head_max(l, u, 3))
                link(v.tensor_tensor(small[:, b, 0:4], small[:, b, 0:4], sink, ALU.max))
                v.tensor_scalar(small[:, b, 4:8], small[:, b, 0:4], -1.0, None, ALU.mult)
                v.tensor_tensor(small[:, b, 8:12], sink, small[:, b, 0:4], ALU.subtract).then_inc(m_ready, 1)

            def unit_normalise(l, u):
                b, nk = u % 2, P * len(key_blocks(l, u))
                v.wait_ge(p_exp, unit_base[l] + u + 1)
                link(v.tensor_tensor(small[:, b, 16:20], small[:, b, 16:20], small[:, b, 12:16], ALU.add))
                link(v.reciprocal(small[:, b, 20:24], small[:, b, 16:20]))
                for r in range(4):
                    ins = v.tensor_scalar(sco[b][:, r, 0:nk], sco[b][:, r, 0:nk], small[:, b, 20 + r:21 + r], None,
                                          ALU.mult)
                ins.then_inc(p_ready, 1)

            def unit_output(l, u):
                qb, g = units(l)[u]
                rows = slice(g * HD, g * HD + HD)
                v.wait_ge(pv_full, unit_base[l] + u + 1)
                v.tensor_copy(bt[rows, 0:NQT, qb * P:qb * P + P],
                              aux[rows, 3, :].rearrange("p (r q) -> p r q", r=4)).then_inc(pv_used, 1)

            def gated(g, gate_g, gate, dst, w):
                v.wait_ge(mm_done, g + 1)
                wait_evac(v, gate_g)
                v.scalar_tensor_tensor(dst[:, 0:w], gate[:, 0:w], 1.0, accs[slot(g)][:, 0:w], ALU.add,
                                       ALU.mult).then_inc(acc_free[slot(g)], 1)
                wait_evac(v, g)

            def chunk_rest(n, par_, jj, w, src, scale, per=0, i=0):
                v.wait_ge(g_hi, n + per * i)
                v.scalar_tensor_tensor(gact[:, par_, jj, 1, 0:w], src[:, 0:w], scale,
                                       gact[:, par_, jj, 0, 0:w].bitcast(F32), ALU.mult, ALU.subtract).then_inc(g_ready, 1)

            def gate_step(l, j, f, w):
                q = PLAN.layers[l]["gate_q"] + 2 * j
                if f == 1:
                    rest(q + SPL)
                elif f == 2:
                    gated(gate_group(l, j, 1), gate_group(l, j, 0), gates[0], part[:, j, :], w)
                elif f == 3:
                    rest(q + 1 + SPL)
                elif f == 4:
                    gated(gate_group(l, j, 3), gate_group(l, j, 2), gates[1], gtmp, w)
                    link(v.tensor_tensor(part[:, j, 0:w], part[:, j, 0:w], gtmp[:, 0:w], ALU.add))

            def add_quad(a, i=0, per_g=0):
                g = PLAN.quad[a]
                wait_evac(v, PLAN.quad[a - 1], i, per_g)
                v.wait_ge(mm_done, g + 1 + per_g * i)
                v.tensor_tensor(row, row, accs[slot(g)][:, 0:512], ALU.add).then_inc(acc_free[slot(g)], 1)

            def take_turn(m, i=0, per_g=0):
                g, (l, u) = PLAN.turn[m], divmod(m, UNITS)
                row = 4 * u + (8 * i if per_g else 0)
                v.wait_ge(mm_done, g + 1 + per_g * i)
                v.tensor_tensor(ada[:, l, bass.ds(row, 4), :], accs[slot(g)][:, 0:8].rearrange("p (n s) -> p n s", s=2),
                                par[:, l, bass.ds(C_BADA + row, 4)].unsqueeze(2).broadcast_to([P, 4, 2]),
                                ALU.add).then_inc(acc_free[slot(g)], 1)

            def fold(l, rows, count):
                for row, gain, bias in rows:
                    a = ada[:, l, row:row + KT, :]
                    ins = v.scalar_tensor_tensor(a, a, bias, par[:, l, gain:gain + KT].unsqueeze(2).broadcast_to([P, KT, 2]),
                                                 ALU.add, ALU.mult)
                ins.then_inc(cond_ready, 1)
                v.wait_ge(cond_ready, count)

            def add_down(g, q, w, i=0, per_g=0, per_q=0, tile=None, last=False):
                for m in range(KT):
                    gg = g + m
                    v.wait_ge(mm_done, gg + 1 + per_g * i)
                    v.tensor_tensor(y[:, m, 0:w], y[:, m, 0:w], accs[slot(gg)][:, 0:w], ALU.add).then_inc(acc_free[slot(gg)], 1)
                    if m == 1 and tile is not None:
                        rest(q - 1 + SPL, i, per_q)
                        tile_product(*tile)
                    if m % 4 == 3 and not last:
                        rest(q + m // 4 + SPL, i, per_q)
                    if m == 4 and tile is not None:
                        tile_rest(*tile)

            def tile_product(l, c, kk, par_, w, i=0, per_t=0):
                v.wait_ge(silu_ready, NFF * l + 2 * c + kk + 1 + per_t * i)
                v.tensor_tensor(conv_a[kk][:, 0:w], conv_a[kk][:, 0:w], conv_g[kk][:, 0:w], ALU.mult).then_inc(g_val, 1)

            def tile_rest(l, c, kk, par_, w, i=0, per_t=0):
                t = g_count(l, "ffn", 2 * c + kk + 1)
                v.wait_ge(g_val, t + per_t * i)
                chunk_rest(t, par_, kk, w, conv_a[kk], 1.0, per_t, i)

            def ups(l, c, g, q, par_, w, i=0, per_g=0, per_q=0, per_t=0, unit=None):
                ctx = w == T
                for n in range(4):
                    kk, dst = n // 2, (conv_a, conv_g)[n % 2][n // 2]
                    f = (2 * c + kk) + NFF * (n % 2)
                    b = slot(g + UP_GROUPS[unit is not None][n])
                    source = late_u if n == 3 else accs[b]
                    v.wait_ge(conv_mid, 2 * NFF * l + 4 * c + n + 1 + 2 * per_t * i)
                    for tap, d0, d1, s0, s1 in ((0, 1, 0, 0, 1), (2, 0, 1, 1, 0)):
                        wt = par[:, l, bass.ds(C_CW + 2 * NFF * tap + f + per_t * i, 1)]
                        for t0, t1, _ in segments(ctx):
                            ins = v.scalar_tensor_tensor(dst[:, t0 + d0:t1 - d1], source[:, t0 + s0:t1 - s1], wt,
                                                         dst[:, t0 + d0:t1 - d1], ALU.mult, ALU.add)
                        if tap == 0:
                            link(ins)
                    ins.then_inc(taps_added if n == 3 else acc_free[b], 1)
                    if n < 3:
                        rest(q + n + SPL, i, per_q)
                    if unit is not None and n == 2:
                        add_quad(2 * unit + 1, i, per_g)
                    if n == 1:
                        tile_product(l, c, 0, par_, w, i, per_t)
                        tile_rest(l, c, 0, par_, w, i, per_t)
                if unit is not None:
                    take_turn(unit, i, per_g)

            v.memset(eps[:, :], EPS).then_inc(eps_set, 1)
            v.wait_ge(consts_in, 16 * 4)
            for m in range(FIRST_UNITS):
                if m == 1:
                    for n in range(1, KT):
                        v.wait_ge(sq_ready, n + 1)
                        if n > 1:
                            v.wait_ge(sq_used, n - 1)
                        v.tensor_tensor(sq_sum, sq[0] if n == 1 else sq_sum, sq[n % 2], ALU.add).then_inc(sq_used, 1)
                add_quad(2 * m + 1)
                take_turn(m)
            wait_evac(v, PLAN.turn[FIRST_UNITS - 1])
            scale1 = ((SC1, C_GPRE, 1.0),)
            others = ((G1, C_GPOST, 0.0), (SC2, C_GPRE2, 1.0), (G2, C_GPOST2, 0.0))
            fold(0, scale1, 1)
            for l, at in enumerate(PLAN.layers):
                ctx = l < DEPTH - 1
                w = T if ctx else NX
                if l == 0:
                    rest(0)
                    rest(1)
                modulate(l, 2 * l, 4 * l, 2 * l, SC1, SH1, True)
                for n in range(len(ORDER) + 1):
                    if l == 0 and late_turns(n) is not None:
                        take_turn(late_turns(n))
                    if l == 0 and n % 2:
                        add_quad(LATE_QUAD + n)
                    if n > 0:
                        rest(at["q"] + n - 1 + SPL)
                    gla_step(l, n)
                if l == 0:
                    take_turn(FIRST_UNITS + 7)
                    wait_evac(v, PLAN.turn[FIRST_UNITS + 7])
                    fold(0, others, 2)
                gla_finish(l)
                gate_step(l, 0, 1, w)
                rope(l)
                gate_step(l, 0, 2, w)
                gate_step(l, 0, 3, w)
                us = units(l)
                for u in range(len(us) + 1):
                    for i in range(STEPS):
                        if u < len(us) and i < 4:
                            unit_scores(l, u, i)
                            if i > 0:
                                head_max(l, u, i - 1)
                        if u < len(us) and i == 3:
                            unit_max(l, u)
                        if u > 0 and i == 0:
                            unit_normalise(l, u - 1)
                        before = divmod(STEPS * u + i - 1, STEPS)
                        if 0 <= before[0] < len(us):
                            for j, f in pieces(len(us), *before):
                                gate_step(l, j, f, w)
                        if u > 1 and i == 1:
                            unit_output(l, u - 2)
                unit_output(l, len(us) - 1)
                g, q = at["mix_g"], at["mix_q"]
                for c in range(KT // 2 + 1):
                    if c < KT // 2:
                        for jj in range(2):
                            rest(q + SPL)
                            gated(g + 1, g, mgate[jj], mtmp, w)
                            j, t = 2 * c + jj, g_count(l, "mix", 2 * c + jj + 1)
                            v.tensor_tensor(part[:, j, 0:w], part[:, j, 0:w], mtmp[:, 0:w], ALU.add).then_inc(g_val, 1)
                            v.wait_ge(g_val, t)
                            chunk_rest(t, c % 2, jj, w, part[:, j, :], 0.5)
                            g, q = g + 2, q + 1
                    if c > 0:
                        v.wait_ge(y_zero, 2 * l + 1)
                        if c > 1:
                            wait_evac(v, g - 4 - 1 if c < KT // 2 else g - 1)
                        add_down(g, q, w, last=c == KT // 2)
                        g, q = g + 8, q + 2
                residual(l, 4 * l + 1, G1, ctx)
                rest(at["ffn_q"])
                rest(at["ffn_q"] + 1)
                modulate(l, 2 * l + 1, 4 * l + 2, 2 * l + 1, SC2, SH2, ctx)
                v.wait_ge(y_zero, 2 * l + 2)
                g, q = at["ffn_g"], at["ffn_q"]
                up_n = UP_COUNT[l == 0]
                pg, pq, unit = 2 * (up_n + KT), FFN_BODY_Q, UNITS if l == 0 else None
                ups(l, 0, g, q, 0, w, unit=unit)
                rest(q + 3 + SPL)
                tile_product(l, 0, 1, 0, w)
                tile_rest(l, 0, 1, 0, w)
                g, q = g + up_n, q + 4
                with v.Fori(0, FFN_LOOPS) as i:
                    link.enter(i, 8)
                    ups(l, 1, g, q, 1, w, i, pg, pq, 4, unit=unit and unit + 1)
                    add_down(g + up_n, q + 4, w, i, pg, pq, tile=(l, 1, 1, 1, w, i, 4))
                    ups(l, 2, g + up_n + KT, q + 6, 0, w, i, pg, pq, 4, unit=unit and unit + 2)
                    add_down(g + 2 * up_n + KT, q + 10, w, i, pg, pq, tile=(l, 2, 1, 0, w, i, 4))
                    link.leave(FFN_LOOPS)
                q += pq * FFN_LOOPS
                if l == 0:
                    add_quad(4 * UNITS - 1)
                    take_turn(2 * UNITS - 1)
                add_down(at["down_g"], q, w, last=True)
                residual(l, 4 * l + 3, G2, ctx)
                rest(q + SPL)
                rest(q + 1 + SPL)
                if l == 0:
                    wait_evac(v, PLAN.turn[2 * UNITS - 1])
                    fold(1, scale1 + others, 3)

        @block.gpsimd
        def _(pool):
            link = Chain(pool, pool_link)

            def pooling(l):
                ctx = l < DEPTH - 1
                segs = [(8, 0, NX)] + ([(NX + 24, NX, NC)] if ctx else [])
                n = segs[-1][0] + segs[-1][2] + 8
                pool.wait_ge(consts_in, 16 * 4)
                for t in range(2):
                    u = proj[:, TPOOL + t, :]
                    wait_evac(pool, proj_group(l, TPOOL + t))
                    link(pool.memset(up[:, 0:n], 0.0))
                    for p0, t0, m in segs:
                        ins = pool.tensor_scalar(up[:, p0:p0 + m], u[:, t0:t0 + m], 1.0, None, ALU.mult)
                    link(ins)
                    link(pool.tensor_tensor(pa[:, 1:n], up[:, 0:n - 1], up[:, 1:n], ALU.add))
                    upper, lower = POOL_WINDOWS[t]
                    if t == 0:
                        pool.tensor_tensor(pb[64:128, 2:n - 1], pa[64:128, 1:n - 2], pa[64:128, 3:n], ALU.add)
                        link(pool.tensor_scalar(pb[0:64, 8:n - 8], pa[0:64, 8:n - 8], 1.0 / upper, None, ALU.mult))
                    else:
                        link(pool.tensor_tensor(pb[:, 2:n - 1], pa[:, 1:n - 2], pa[:, 3:n], ALU.add))
                        link(pool.tensor_tensor(pa[:, 4:n - 4], pb[:, 2:n - 6], pb[:, 6:n - 2], ALU.add))
                        pool.tensor_scalar(pb[0:64, 8:n - 8], pa[0:64, 8:n - 8], 1.0 / upper, None, ALU.mult)
                        link(pool.tensor_tensor(pb[64:128, 8:n - 8], pa[64:128, 4:n - 12], pa[64:128, 12:n - 4], ALU.add))
                    link(pool.tensor_scalar(pb[64:128, 8:n - 8], pb[64:128, 8:n - 8], 1.0 / lower, None, ALU.mult))
                    for p0, _, m in segs:
                        for side, c0 in enumerate((p0, p0 + m - EDGE)):
                            k0 = K_EDGE + (2 * t + side) * EDGE
                            ins = pool.tensor_tensor(pb[:, c0:c0 + EDGE], pb[:, c0:c0 + EDGE], con[:, k0:k0 + EDGE], ALU.mult)
                    link(ins)
                    for p0, t0, m in segs:
                        ins = pool.tensor_tensor(u[:, t0:t0 + m], pb[:, p0:p0 + m], u[:, t0:t0 + m], ALU.subtract)
                    ins.then_inc(pool_d, 1)
                    pool.wait_ge(pool_d, 2 * l + t + 1)

            def modulate(l, n, k, post, ctx):
                w = T if ctx else NX
                pool.wait_ge(rstd_ready, k + 1)
                for kt in range(1, KT, 2):
                    x_valid(pool, l, post, kt)
                    if kt >= 4:
                        pool.wait_ge(h_ready, KT * n + kt - 3)
                    pool.tensor_tensor(mod[kt % 4][:, 0:w], x[:, kt, 0:w], rstd[:, 0:w], ALU.mult).then_inc(t_ready[1], 1)

            def residual(l, k, ctx):
                w, n = T if ctx else NX, k // 2
                for kt in range(1, KT, 2):
                    pool.wait_ge(y_scaled, KT * n + kt + 1)
                    pool.tensor_tensor(x[:, kt, 0:w], x[:, kt, 0:w], tmp[1][:, 0:w], ALU.add).then_inc(x_ready[1], 1)

            for l in range(DEPTH):
                ctx = l < DEPTH - 1
                modulate(l, 2 * l, 4 * l, 2 * l, True)
                pooling(l)
                pool.wait_ge(pv_used, unit_base[l + 1])
                pool.memset(y[:, :, :], 0.0).then_inc(y_zero, 1)
                residual(l, 4 * l + 1, ctx)
                modulate(l, 2 * l + 1, 4 * l + 2, 2 * l + 1, ctx)
                pool.memset(y[:, :, :], 0.0).then_inc(y_zero, 1)
                residual(l, 4 * l + 3, ctx)


def _tiles(a):
    return np.ascontiguousarray(a.reshape(-1, P, a.shape[-1]).transpose(1, 0, 2))


def _rows(a):
    return a.reshape(-1, P).T


def _block(w, cols):
    return w[:, cols].reshape(KT, P, P).transpose(1, 0, 2).reshape(P, BLK)


def _chunk(w, c, half):
    return w[2 * c * P:2 * (c + 1) * P, half * 512:half * 512 + 512].reshape(2, P, 512).transpose(1, 0, 2).reshape(P, BLK)


def _weight_stream(w_in, w_o, w_up, w_down):
    at = dict(q=0, k=512, v=640, pool=768, gq=1024, gk=1152, gv=1280, gr=1536, lr=1792, mg=1824)
    run = lambda o: np.arange(o, o + P)
    heads = lambda t: np.concatenate([np.arange(t * HD, t * HD + HD), np.arange((t + 4) * HD, (t + 5) * HD)])
    cols = {TK: run(at["k"]), TV: run(at["v"]), TGQ: run(at["gq"]), TGK: run(at["gk"])}
    cols.update({t: heads(t) for t in range(NQT)})
    for t in range(2):
        cols[TPOOL + t], cols[TGV + t], cols[TGR + t] = run(at["pool"] + t * P), run(at["gv"] + t * P), run(at["gr"] + t * P)
    out = []
    for l in range(DEPTH):
        lr = np.concatenate([w_in[l][:, at["lr"]:at["mg"]], np.zeros((D, P - 32), w_in.dtype)], axis=1)
        for tile in ORDER:
            out.append(_block(lr, run(0)) if tile == TLR else _block(w_in[l], cols[tile]))
        gate = lambda b, j: _block(w_in[l], run(at["mg"] + b * D + j * P))
        for j in range(KT):
            out += [gate(1, j), gate(2, j)]
        for c in range(KT // 2 + 1):
            if c < KT // 2:
                out += [gate(0, 2 * c), gate(0, 2 * c + 1)]
            if c > 0:
                out += [_chunk(w_o[l], c - 1, 0), _chunk(w_o[l], c - 1, 1)]
        for c in range(NFF // 2 + 1):
            if c < NFF // 2:
                for j in (2 * c, 2 * c + 1):
                    out += [_block(w_up[l], run(j * P)), _block(w_up[l], run((NFF + j) * P))]
            if c > 0:
                out += [_chunk(w_down[l], c - 1, 0), _chunk(w_down[l], c - 1, 1)]
    return np.stack(out)


def _branch_stream(w_att, w_pool, w_gla):
    out = []
    for l in range(DEPTH):
        both = np.concatenate([w_pool[l], w_gla[l]], axis=0)
        order = np.concatenate([np.arange(h * HD, h * HD + HD) for t in range(NQT) for h in (t, t + 4)])
        for w in (both, w_att[l][order]):
            w = w.reshape(4, P, KT, P)
            for b in range(KT // 2):
                out.append(w[:, :, 2 * b:2 * b + 2, :].transpose(1, 2, 0, 3))
    return np.ascontiguousarray(np.stack(out))


def _parameters(i):
    f = i["b_ada"].dtype
    par = np.zeros((P, DEPTH, NPAR), f)
    for l in range(DEPTH):
        for c, v in ((C_BADA, i["b_ada"][l]), (C_GPRE, i["g_pre_mix"][l]), (C_GPOST, i["g_post_mix"][l]),
                     (C_GPRE2, i["g_pre_ffn"][l]), (C_GPOST2, i["g_post_ffn"][l]), (C_PSC, i["pool_scale"][l]),
                     (C_BA, i["gla_ba"][l].reshape(-1)), (C_GN, i["gla_norm"][l].reshape(-1)),
                     (C_CW, i["conv_w"][l].reshape(-1)), (C_CB, i["conv_b"][l])):
            r = _rows(v)
            par[:, l, c:c + r.shape[1]] = r
        par[:, l, C_SINK:C_SINK + 8] = i["att_sink"][l][None, :]
    return par


def _small_weights(gla_wa2, pool_w):
    wa2 = np.zeros((DEPTH, 32, 256), gla_wa2.dtype)
    poolw = np.zeros((DEPTH, P, 256), pool_w.dtype)
    for l in range(DEPTH):
        for d in range(2):
            wa2[l, 16 * d:16 * d + 16, P * d:P * d + P] = gla_wa2[l, d]
        for g in range(4):
            r = 64 * (g % 2)
            poolw[l, r:r + 64, (g // 2) * P + r:(g // 2) * P + r + 64] = pool_w[l, g]
    return wa2, poolw


def _constants():
    con = np.zeros((P, NCON), np.float32)
    p = np.arange(P)
    con[:, K_ONES:K_ONES + P] = 1.0
    con[:, K_BONES:K_BONES + P] = p[:, None] // 64 == p[None, :] // 64
    half = HD // 2
    for m in range(P):
        if m % HD < half:
            con[m + half, K_ROT + m] = -1.0
        else:
            con[m - half, K_ROT + m] = 1.0
    con[:, K_ID:K_ID + P] = np.eye(P)
    for v in range(2):
        con[v::32, K_SEL + v] = 1.0
    scanm = np.broadcast_to((np.arange(T) % CH != 0).astype(np.float32), (P, T)).copy()
    gm = np.zeros((P, NGRAM, CH), np.int32)
    a, b = (p % CH)[:, None], np.arange(CH)[None, :]
    for n, half_ in enumerate(LEVELS):
        gm[:, n + 1, :] = (a // (2 * half_) == b // (2 * half_)) & (a // half_ != b // half_)
    gm[:, 0, :] = a == b
    am = np.zeros((P, 3 * P), np.float32)
    am[:, 0:P] = np.where(p[None, :] >= p[:, None], 0.0, NEG)
    am[:, 2 * P:] = np.where(p[None, :] <= p[:, None], 0.0, NEG)
    n = HD // 4
    base = (10000.0 ** (-np.arange(n) / n)).astype(np.float32)
    tok = np.arange(NX)
    ang = np.concatenate([(tok // GRID_W).astype(np.float32)[:, None] * base,
                          (tok % GRID_W).astype(np.float32)[:, None] * base], axis=-1).T
    rope = np.concatenate([np.tile(np.cos(ang), (4, 1)), np.tile(np.sin(ang), (4, 1))], axis=1).astype(np.float32)
    for t, windows in enumerate(POOL_WINDOWS):
        for half_, w in enumerate(windows):
            for side in range(2):
                tok = np.arange(EDGE) + side * (NC - EDGE)
                cnt = np.clip(tok + w - w // 2, 0, NC) - np.clip(tok - w // 2, 0, NC)
                c = K_EDGE + (2 * t + side) * EDGE
                con[64 * half_:64 * half_ + 64, c:c + EDGE] = (w / cnt).astype(np.float32)
    return con, scanm, gm, am, rope


def _conditioning(w_ada):
    w = w_ada.reshape(DEPTH, 2, 4, P, UNITS, 512)
    return np.ascontiguousarray(w.transpose(0, 4, 1, 3, 2, 5)).reshape(DEPTH * UNITS * 2, P, 2048)


def kernel(**inputs):
    import concourse.bacc as bacc
    from concourse.bass_utils import run_bass_kernel_spmd

    i = {k: np.asarray(v) for k, v in inputs.items()}
    x_t = _tiles(np.concatenate([i["x"][0].T, i["ctx"][0].T], axis=1))
    c_t = np.zeros((P, KT, 32), i["c"].dtype)
    c_t[:, :, 0], c_t[:, :, 1] = _rows(i["c"][0]), _rows(i["c_ctx"])
    wa2, poolw = _small_weights(i["gla_wa2"], i["pool_w"])
    con, scanm, gm, am, rope = _constants()
    arrays = {
        "x_t": x_t, "c_t": c_t, "par_d": _parameters(i), "con_d": con, "ada_d": _conditioning(i["w_ada"]),
        "wst_d": _weight_stream(i["w_in"], i["w_o"], i["w_up"], i["w_down"]),
        "brw_d": _branch_stream(i["w_br_att"], i["w_br_pool"], i["w_br_gla"]),
        "wa2_d": wa2, "poolw_d": poolw, "scanm_d": scanm, "gmask_d": gm, "amask_d": am, "rope_d": rope,
    }
    nc = bacc.Bacc("TRN2", target_bir_lowering=False, num_devices=1)
    aps = {n: nc.dram_tensor(n, a.shape, mybir.dt.from_np(a.dtype), kind="ExternalInput").ap() for n, a in arrays.items()}
    out = nc.dram_tensor("out", (P, KT, NX), F32, kind="ExternalOutput").ap()
    build(nc, out=out, **aps)
    r = run_bass_kernel_spmd(nc, [arrays], core_ids=[0])
    return np.ascontiguousarray(r.results[0]["out"].transpose(1, 0, 2).reshape(D, NX).T)[None]
```
